# Optimizing a Trainium2 kernel written in Bass

```python
import jax, jax.numpy as jnp
from jax import lax
import numpy as np

D_MODEL = 1024
BATCH = 1
SEQ = 512
DEPTH = 1

PLE_DIM = 256
M_HEADS = 4
M_HEAD_DIM = 128
M_WIDTH = M_HEADS * M_HEAD_DIM
M_CHUNK = 64
A_HEADS = 8
A_KV_GROUPS = 2
A_HEAD_DIM = 64
A_WIDTH = A_HEADS * A_HEAD_DIM
KV_WIDTH = A_KV_GROUPS * A_HEAD_DIM
CMP_BLOCK = 32
CMP_STRIDE = 16
CMP_HIDDEN = 128
SEL_BLOCK = 64
N_SELECT = 16
WINDOW = 512
A_Q_BLOCK = 32
ALIBI_MAX = 8.0
MIX_WIDTH = M_WIDTH + A_WIDTH
IN_WIDTH = 4 * M_WIDTH + 2 * M_HEADS + A_WIDTH + 6 * KV_WIDTH + 3 * A_HEADS
D_FF = 2048
CONV_WIDTH = 3
EPS = 1e-6
NEG = -1e30
BIG = 1e30


def rms_norm(x, g):
    xf = x.astype(jnp.float32)
    y = xf * lax.rsqrt(jnp.mean(xf * xf, axis=-1, keepdims=True) + EPS)
    return (y * g.astype(jnp.float32)).astype(x.dtype)

def alibi_slopes(n):
    return jnp.exp2(-ALIBI_MAX * jnp.arange(1, n + 1, dtype=jnp.float32) / n)

def mlstm(q, k, v, i_pre, f_pre):
    B, S, H, dh = q.shape
    L = M_CHUNK
    NC = S // L
    f32 = jnp.float32

    def chunks(t):
        t = t.astype(f32).reshape((B, NC, L, H) + t.shape[3:])
        return jnp.moveaxis(t, 3, 1)

    qc = chunks(q) * (dh ** -0.5)
    kc = chunks(k)
    vc = chunks(v)
    ig = chunks(i_pre)
    b = jnp.cumsum(jax.nn.log_sigmoid(chunks(f_pre)), axis=-1)
    bL = b[..., -1]
    a = bL[..., None] - b + ig

    def step(carry, inp):
        C, n, m = carry
        k_, v_, a_, bL_ = inp
        m_new = jnp.maximum(bL_ + m, jnp.max(a_, axis=-1))
        decay = jnp.exp(bL_ + m - m_new)
        w = jnp.exp(a_ - m_new[..., None])
        C_new = decay[..., None, None] * C + jnp.einsum('bhl,bhlk,bhlv->bhkv', w, k_, v_)
        n_new = decay[..., None] * n + jnp.einsum('bhl,bhlk->bhk', w, k_)
        return (C_new, n_new, m_new), (C, n, m)

    init = (jnp.zeros((B, H, dh, dh), f32), jnp.zeros((B, H, dh), f32), jnp.zeros((B, H), f32))
    xs = (jnp.moveaxis(kc, 2, 0), jnp.moveaxis(vc, 2, 0), jnp.moveaxis(a, 2, 0), jnp.moveaxis(bL, 2, 0))
    _, (Cs, ns, ms) = lax.scan(step, init, xs)
    Cs = jnp.moveaxis(Cs, 0, 2)
    ns = jnp.moveaxis(ns, 0, 2)
    ms = jnp.moveaxis(ms, 0, 2)

    bq = b + ms[..., None]
    causal = jnp.tril(jnp.ones((L, L), dtype=bool))
    Dm = jnp.where(causal, b[..., :, None] - b[..., None, :] + ig[..., None, :], -jnp.inf)
    m = jnp.maximum(bq, jnp.max(Dm, axis=-1))
    inter = jnp.exp(bq - m)
    Wt = jnp.exp(Dm - m[..., None]) * jnp.einsum('bhcld,bhcsd->bhcls', qc, kc)
    num = inter[..., None] * jnp.einsum('bhcld,bhcdv->bhclv', qc, Cs) + jnp.einsum('bhcls,bhcsv->bhclv', Wt, vc)
    den = inter * jnp.einsum('bhcld,bhcd->bhcl', qc, ns) + jnp.sum(Wt, axis=-1)
    h = num / jnp.maximum(jnp.abs(den), jnp.exp(-m))[..., None]
    return jnp.moveaxis(h, 1, 3).reshape(B, S, H, dh)

def nsa(q, kc_raw, vc_raw, ks_raw, vs_raw, kw_raw, vw_raw, g_pre, pe_k, pe_v, ck_w1, ck_w2, cv_w1, cv_w2):
    f32 = jnp.float32
    B, S, H, dh = q.shape
    G = A_KV_GROUPS
    R = H // G
    qg = q.astype(f32).reshape(B, S, G, R, dh).transpose(0, 2, 3, 1, 4) * (dh ** -0.5)
    gates = jax.nn.sigmoid(g_pre.astype(f32).reshape(B, S, G, R, 3)).transpose(0, 2, 3, 1, 4)
    to_g = lambda t: t.astype(f32).transpose(0, 2, 1, 3)

    Nc = (S - CMP_BLOCK) // CMP_STRIDE + 1
    cidx = jnp.arange(Nc)[:, None] * CMP_STRIDE + jnp.arange(CMP_BLOCK)[None, :]

    def compress(t, pe, w1, w2):
        blk = to_g(t)[:, :, cidx] + pe.astype(f32)
        flat = blk.reshape(B, G, Nc, CMP_BLOCK * dh)
        return jax.nn.gelu(flat @ w1.astype(f32)) @ w2.astype(f32)

    Kc = compress(kc_raw, pe_k, ck_w1, ck_w2)
    Vc = compress(vc_raw, pe_v, cv_w1, cv_w2)
    cmp_start = jnp.arange(Nc) * CMP_STRIDE
    cmp_end = cmp_start + CMP_BLOCK - 1

    Ns = S // SEL_BLOCK
    n_sel = min(N_SELECT, Ns)
    Ks = to_g(ks_raw).reshape(B, G, Ns, SEL_BLOCK, dh)
    Vs = to_g(vs_raw).reshape(B, G, Ns, SEL_BLOCK, dh)
    sel_start = jnp.arange(Ns) * SEL_BLOCK
    overlap = ((cmp_start[:, None] <= sel_start[None, :] + SEL_BLOCK - 1)
               & (cmp_end[:, None] >= sel_start[None, :])).astype(f32)

    pad = ((0, 0), (0, 0), (WINDOW, 0), (0, 0))
    Kw = jnp.pad(to_g(kw_raw), pad)
    Vw = jnp.pad(to_g(vw_raw), pad)

    slope = alibi_slopes(H).reshape(1, G, R, 1, 1)
    bi = jnp.arange(B)[:, None, None, None]
    gi = jnp.arange(G)[None, :, None, None]
    T = A_Q_BLOCK

    def block(qb):
        t0 = qb * T
        t = t0 + jnp.arange(T)
        qblk = lax.dynamic_slice_in_dim(qg, t0, T, axis=3)
        gblk = lax.dynamic_slice_in_dim(gates, t0, T, axis=3)

        valid_c = cmp_end[None, :] <= t[:, None]
        dist_c = (t[:, None] - cmp_end[None, :]).astype(f32)
        s_c = jnp.einsum('bgrtd,bgnd->bgrtn', qblk, Kc) - slope * dist_c
        p_c = jnp.where(valid_c, jax.nn.softmax(jnp.where(valid_c, s_c, NEG), axis=-1), 0.0)
        o_c = jnp.einsum('bgrtn,bgnd->bgrtd', p_c, Vc)

        imp = jnp.einsum('bgrtn,nj->bgtj', p_c, overlap)
        j = jnp.arange(Ns)[None, :]
        cur = (t // SEL_BLOCK)[:, None]
        forced = (j == 0) | (j == cur) | (j == cur - 1)
        causal_b = sel_start[None, :] <= t[:, None]
        score = jnp.where(causal_b, jnp.where(forced, BIG, imp), NEG)
        sel_idx = lax.top_k(score, n_sel)[1]
        Ksel = Ks[bi, gi, sel_idx]
        Vsel = Vs[bi, gi, sel_idx]
        pos_s = sel_idx[..., None] * SEL_BLOCK + jnp.arange(SEL_BLOCK)
        dist_s = (t[None, None, :, None, None] - pos_s)
        valid_s = (dist_s >= 0)[:, :, None]
        s_s = jnp.einsum('bgrtd,bgtnld->bgrtnl', qblk, Ksel) - slope[..., None] * dist_s[:, :, None].astype(f32)
        s_s = jnp.where(valid_s, s_s, NEG).reshape(B, G, R, T, n_sel * SEL_BLOCK)
        p_s = jax.nn.softmax(s_s, axis=-1).reshape(B, G, R, T, n_sel, SEL_BLOCK)
        o_s = jnp.einsum('bgrtnl,bgtnld->bgrtd', p_s, Vsel)

        kwin = lax.dynamic_slice_in_dim(Kw, t0, WINDOW + T, axis=2)
        vwin = lax.dynamic_slice_in_dim(Vw, t0, WINDOW + T, axis=2)
        pos_w = t0 - WINDOW + jnp.arange(WINDOW + T)
        dist_w = t[:, None] - pos_w[None, :]
        valid_w = (pos_w[None, :] >= 0) & (dist_w >= 0) & (dist_w < WINDOW)
        s_w = jnp.einsum('bgrtd,bgsd->bgrts', qblk, kwin) - slope * dist_w.astype(f32)
        p_w = jax.nn.softmax(jnp.where(valid_w, s_w, NEG), axis=-1)
        o_w = jnp.einsum('bgrts,bgsd->bgrtd', p_w, vwin)

        return gblk[..., 0:1] * o_c + gblk[..., 1:2] * o_s + gblk[..., 2:3] * o_w

    outs = lax.map(block, jnp.arange(S // T))
    return outs.transpose(1, 0, 4, 2, 3, 5).reshape(B, S, H * dh)

def conv_ffn(h, w_up, conv_w, conv_b, w_down):
    u = h @ w_up
    gate, val = jnp.split(u, 2, axis=-1)
    gate = lax.conv_general_dilated(gate, conv_w[:, None, :].astype(gate.dtype), window_strides=(1,),
                                    padding=[(CONV_WIDTH - 1, 0)],
                                    dimension_numbers=('NWC', 'WIO', 'NWC'),
                                    feature_group_count=D_FF) + conv_b
    return (jax.nn.silu(gate) * val) @ w_down

def first_inputs(seed: int = 0) -> dict:
    key = jax.random.key(seed)
    ks = jax.random.split(key, 24)
    f32 = jnp.float32
    nrm = lambda k, shape, scale: jax.random.normal(k, shape, f32) * scale
    gain = lambda k, shape: 1.0 + 0.05 * jax.random.normal(k, shape, f32)
    i_bias = nrm(ks[4], (DEPTH, M_HEADS), 0.1)
    f_bias = jnp.linspace(3.0, 6.0, M_HEADS, dtype=f32)[None, :] + nrm(ks[5], (DEPTH, M_HEADS), 0.1)
    return {
        "x": nrm(ks[0], (BATCH, SEQ, D_MODEL), 1.0),
        "p": nrm(ks[1], (DEPTH, BATCH, SEQ, PLE_DIM), 1.0),
        "ln1_g": gain(ks[2], (DEPTH, D_MODEL)),
        "w_in": nrm(ks[3], (DEPTH, D_MODEL, IN_WIDTH), D_MODEL ** -0.5),
        "mlstm_gate_bias": jnp.concatenate([i_bias, f_bias], axis=-1),
        "mlstm_norm_g": gain(ks[6], (DEPTH, M_WIDTH)),
        "cmp_pos_k": nrm(ks[7], (DEPTH, CMP_BLOCK, A_HEAD_DIM), 0.02),
        "cmp_pos_v": nrm(ks[8], (DEPTH, CMP_BLOCK, A_HEAD_DIM), 0.02),
        "cmp_k_w1": nrm(ks[9], (DEPTH, CMP_BLOCK * A_HEAD_DIM, CMP_HIDDEN), (CMP_BLOCK * A_HEAD_DIM) ** -0.5),
        "cmp_k_w2": nrm(ks[10], (DEPTH, CMP_HIDDEN, A_HEAD_DIM), CMP_HIDDEN ** -0.5),
        "cmp_v_w1": nrm(ks[11], (DEPTH, CMP_BLOCK * A_HEAD_DIM, CMP_HIDDEN), (CMP_BLOCK * A_HEAD_DIM) ** -0.5),
        "cmp_v_w2": nrm(ks[12], (DEPTH, CMP_HIDDEN, A_HEAD_DIM), CMP_HIDDEN ** -0.5),
        "w_out": nrm(ks[13], (DEPTH, MIX_WIDTH, D_MODEL), MIX_WIDTH ** -0.5),
        "ln2_g": gain(ks[14], (DEPTH, D_MODEL)),
        "w_up": nrm(ks[15], (DEPTH, D_MODEL, 2 * D_FF), D_MODEL ** -0.5),
        "conv_w": nrm(ks[16], (DEPTH, CONV_WIDTH, D_FF), CONV_WIDTH ** -0.5),
        "conv_b": nrm(ks[17], (DEPTH, D_FF), 0.02),
        "w_down": nrm(ks[18], (DEPTH, D_FF, D_MODEL), D_FF ** -0.5),
        "ple_norm_g": gain(ks[19], (DEPTH, D_MODEL)),
        "w_ple_gate": nrm(ks[20], (DEPTH, D_MODEL, D_MODEL), D_MODEL ** -0.5),
        "w_ple_proj": nrm(ks[21], (DEPTH, PLE_DIM, D_MODEL), PLE_DIM ** -0.5),
        "final_g": gain(ks[22], (D_MODEL,)),
    }

def first_block(x, p, ln1_g, w_in, mlstm_gate_bias, mlstm_norm_g, cmp_pos_k, cmp_pos_v, cmp_k_w1, cmp_k_w2,
              cmp_v_w1, cmp_v_w2, w_out, ln2_g, w_up, conv_w, conv_b, w_down, ple_norm_g, w_ple_gate,
              w_ple_proj, final_g):
    B, S, _ = x.shape
    sizes = [M_WIDTH] * 4 + [M_HEADS, M_HEADS, A_WIDTH] + [KV_WIDTH] * 6 + [3 * A_HEADS]
    offs = np.cumsum(sizes)[:-1].tolist()
    for i in range(DEPTH):
        h = rms_norm(x, ln1_g[i])
        z = h @ w_in[i]
        mq, mk, mv, mo, mi, mf, aq, akc, avc, aks, avs, akw, avw, ag = jnp.split(z, offs, axis=-1)
        mshape = (B, S, M_HEADS, M_HEAD_DIM)
        hm = mlstm(mq.reshape(mshape), mk.reshape(mshape), mv.reshape(mshape),
                   mi + mlstm_gate_bias[i, :M_HEADS], mf + mlstm_gate_bias[i, M_HEADS:])
        hm = rms_norm(hm, mlstm_norm_g[i].reshape(M_HEADS, M_HEAD_DIM)).reshape(B, S, M_WIDTH)
        m_out = (hm * jax.nn.sigmoid(mo.astype(jnp.float32))).astype(x.dtype)
        kvshape = (B, S, A_KV_GROUPS, A_HEAD_DIM)
        a_out = nsa(aq.reshape(B, S, A_HEADS, A_HEAD_DIM), akc.reshape(kvshape), avc.reshape(kvshape),
                    aks.reshape(kvshape), avs.reshape(kvshape), akw.reshape(kvshape), avw.reshape(kvshape),
                    ag, cmp_pos_k[i], cmp_pos_v[i], cmp_k_w1[i], cmp_k_w2[i], cmp_v_w1[i], cmp_v_w2[i]).astype(x.dtype)
        x = x + jnp.concatenate([m_out, a_out], axis=-1) @ w_out[i]
        x = x + conv_ffn(rms_norm(x, ln2_g[i]), w_up[i], conv_w[i], conv_b[i], w_down[i])
        gate = jax.nn.sigmoid(rms_norm(x, ple_norm_g[i]) @ w_ple_gate[i])
        x = x + gate * (p[i].astype(x.dtype) @ w_ple_proj[i])
    return rms_norm(x, final_g)


DEPTH_2 = 2

GRID_W = 64
N_META = 16
HEAD_DIM = 64
ATTN_HEADS = 8
ATTN_KV_HEADS = 2
ATTN_GROUP = ATTN_HEADS // ATTN_KV_HEADS
ATTN_WIDTH = ATTN_HEADS * HEAD_DIM
ATTN_KV_WIDTH = ATTN_KV_HEADS * HEAD_DIM
NA_HEADS = 8
NA_WIDTH = NA_HEADS * HEAD_DIM
NA_KH_MAX = 8
NA_KW = 16
Q_BLOCK = 128
ROPE_THETA = 10000.0
IN_SPLITS = (ATTN_WIDTH, ATTN_KV_WIDTH, ATTN_KV_WIDTH, ATTN_WIDTH,
             NA_WIDTH, NA_WIDTH, NA_WIDTH, NA_WIDTH, D_MODEL, D_MODEL)
IN_COLS = ATTN_WIDTH * 2 + ATTN_KV_WIDTH * 2 + NA_WIDTH * 4 + D_MODEL * 2


def rms_norm_2(x, g):
    xf = x.astype(jnp.float32)
    y = xf * lax.rsqrt(jnp.mean(xf * xf, axis=-1, keepdims=True) + EPS)
    return (y * g.astype(jnp.float32)).astype(x.dtype)

def split_cols(p):
    outs, off = [], 0
    for w in IN_SPLITS:
        outs.append(p[..., off:off + w])
        off += w
    return outs

def axial_rope_tables(n_real):
    t = jnp.arange(n_real, dtype=jnp.int32)
    zeros = jnp.zeros((N_META,), jnp.int32)
    row = jnp.concatenate([zeros, t // GRID_W]).astype(jnp.float32)
    col = jnp.concatenate([zeros, t % GRID_W]).astype(jnp.float32)
    axis_dim = HEAD_DIM // 2
    inv = ROPE_THETA ** (-jnp.arange(0, axis_dim, 2, dtype=jnp.float32) / axis_dim)
    ang_r = row[:, None] * inv[None]
    ang_c = col[:, None] * inv[None]
    ang = jnp.concatenate([ang_r, ang_r, ang_c, ang_c], axis=-1)
    return jnp.cos(ang), jnp.sin(ang)

def apply_axial_rope(x, cos, sin):
    axis_dim = HEAD_DIM // 2
    q4 = axis_dim // 2
    xf = x.astype(jnp.float32)
    xr, xc = xf[..., :axis_dim], xf[..., axis_dim:]
    rot = jnp.concatenate([-xr[..., q4:], xr[..., :q4], -xc[..., q4:], xc[..., :q4]], axis=-1)
    return (xf * cos[None, :, None, :] + rot * sin[None, :, None, :]).astype(x.dtype)

def gqa_attention(q, k, v):
    b, l = q.shape[:2]
    n = l - N_META
    scale = HEAD_DIM ** -0.5

    def attend(qb):
        s = jnp.einsum('bqkgd,bskd->bkgqs', qb, k).astype(jnp.float32) * scale
        p = jax.nn.softmax(s, axis=-1).astype(v.dtype)
        return jnp.einsum('bkgqs,bskd->bqkgd', p, v)

    qg = q.reshape(b, l, ATTN_KV_HEADS, ATTN_GROUP, HEAD_DIM)
    o_meta = attend(qg[:, :N_META])
    q_blocks = qg[:, N_META:].reshape(b, n // Q_BLOCK, Q_BLOCK, ATTN_KV_HEADS, ATTN_GROUP, HEAD_DIM)
    q_blocks = q_blocks.transpose(1, 0, 2, 3, 4, 5)
    o_real = lax.map(attend, q_blocks).transpose(1, 0, 2, 3, 4, 5)
    o_real = o_real.reshape(b, n, ATTN_KV_HEADS, ATTN_GROUP, HEAD_DIM)
    return jnp.concatenate([o_meta, o_real], axis=1).reshape(b, l, ATTN_WIDTH)

def neighbourhood_attention(q, k, v, rpb):
    b, l = q.shape[:2]
    n = l - N_META
    rows = n // GRID_W
    kh = min(NA_KH_MAX, rows)
    scale = HEAD_DIM ** -0.5
    qm, km, vm = q[:, :N_META], k[:, :N_META], v[:, :N_META]

    s_mm = jnp.einsum('bqhd,bmhd->bhqm', qm, km).astype(jnp.float32) * scale
    o_meta = jnp.einsum('bhqm,bmhd->bqhd', jax.nn.softmax(s_mm, axis=-1).astype(v.dtype), vm)

    qg = q[:, N_META:].reshape(b, rows, GRID_W, NA_HEADS, HEAD_DIM)
    kg = k[:, N_META:].reshape(b, rows, GRID_W, NA_HEADS, HEAD_DIM)
    vg = v[:, N_META:].reshape(b, rows, GRID_W, NA_HEADS, HEAD_DIM)

    r = jnp.arange(rows)
    row_start = jnp.clip(r - kh // 2, 0, rows - kh)
    row_bias_idx = row_start[:, None] + jnp.arange(kh)[None] - r[:, None] + NA_KH_MAX - 1
    c = jnp.arange(GRID_W)
    col_start = jnp.clip(c - NA_KW // 2, 0, GRID_W - NA_KW)
    col_idx = col_start[:, None] + jnp.arange(NA_KW)[None]
    col_bias_idx = col_idx - c[:, None] + NA_KW - 1
    rpb_cols = rpb[:, :, col_bias_idx]

    def row_step(args):
        q_row, rs, rbi = args
        k_band = lax.dynamic_slice_in_dim(kg, rs, kh, axis=1)
        v_band = lax.dynamic_slice_in_dim(vg, rs, kh, axis=1)
        k_win = k_band[:, :, col_idx]
        v_win = v_band[:, :, col_idx]
        s_win = jnp.einsum('bchd,bicjhd->bhcij', q_row, k_win).astype(jnp.float32) * scale
        bias = rpb_cols[:, rbi].transpose(0, 2, 1, 3)
        s_win = s_win + bias[None].astype(jnp.float32)
        s_meta = jnp.einsum('bchd,bmhd->bhcm', q_row, km).astype(jnp.float32) * scale
        s = jnp.concatenate([s_win.reshape(b, NA_HEADS, GRID_W, kh * NA_KW), s_meta], axis=-1)
        p = jax.nn.softmax(s, axis=-1).astype(v.dtype)
        p_win = p[..., :kh * NA_KW].reshape(b, NA_HEADS, GRID_W, kh, NA_KW)
        p_meta = p[..., kh * NA_KW:]
        return (jnp.einsum('bhcij,bicjhd->bchd', p_win, v_win)
                + jnp.einsum('bhcm,bmhd->bchd', p_meta, vm))

    o_rows = lax.map(row_step, (qg.transpose(1, 0, 2, 3, 4), row_start, row_bias_idx))
    o_real = o_rows.transpose(1, 0, 2, 3, 4).reshape(b, n, NA_WIDTH)
    return jnp.concatenate([o_meta.reshape(b, N_META, NA_WIDTH), o_real], axis=1)

def hybrid_layer(x, norm_g, w_in, q_norm_g, k_norm_g, rpb, w_o_attn, w_o_na, w_out, cos, sin):
    b, l, _ = x.shape
    h = rms_norm_2(x, norm_g)
    proj = jnp.einsum('bld,de->ble', h, w_in)
    qa, ka, va, za, qb, kb, vb, zb, ga, gb = split_cols(proj)

    qa = apply_axial_rope(rms_norm_2(qa.reshape(b, l, ATTN_HEADS, HEAD_DIM), q_norm_g), cos, sin)
    ka = apply_axial_rope(rms_norm_2(ka.reshape(b, l, ATTN_KV_HEADS, HEAD_DIM), k_norm_g), cos, sin)
    va = va.reshape(b, l, ATTN_KV_HEADS, HEAD_DIM)
    oa = gqa_attention(qa, ka, va) * jax.nn.silu(za)

    qb = qb.reshape(b, l, NA_HEADS, HEAD_DIM)
    kb = kb.reshape(b, l, NA_HEADS, HEAD_DIM)
    vb = vb.reshape(b, l, NA_HEADS, HEAD_DIM)
    ob = neighbourhood_attention(qb, kb, vb, rpb) * jax.nn.silu(zb)

    ya = jnp.einsum('ble,ed->bld', oa, w_o_attn)
    yb = jnp.einsum('ble,ed->bld', ob, w_o_na)
    mixed = jax.nn.sigmoid(ga) * ya + jax.nn.sigmoid(gb) * yb
    return x + jnp.einsum('bld,de->ble', mixed, w_out)

def second_inputs(seed: int = 0) -> dict:
    key = jax.random.key(seed)
    ks = jax.random.split(key, 12)
    f32 = jnp.float32
    x = jax.random.normal(ks[0], (BATCH, SEQ, D_MODEL), f32)
    meta_tokens = jax.random.normal(ks[1], (N_META, D_MODEL), f32)
    norm_g = 1.0 + 0.05 * jax.random.normal(ks[2], (DEPTH_2, D_MODEL), f32)
    w_in = jax.random.normal(ks[3], (DEPTH_2, D_MODEL, IN_COLS), f32) * D_MODEL ** -0.5
    q_norm_g = 1.0 + 0.05 * jax.random.normal(ks[4], (DEPTH_2, HEAD_DIM), f32)
    k_norm_g = 1.0 + 0.05 * jax.random.normal(ks[5], (DEPTH_2, HEAD_DIM), f32)
    na_rpb = 0.1 * jax.random.normal(ks[6], (DEPTH_2, NA_HEADS, 2 * NA_KH_MAX - 1, 2 * NA_KW - 1), f32)
    w_o_attn = jax.random.normal(ks[7], (DEPTH_2, ATTN_WIDTH, D_MODEL), f32) * ATTN_WIDTH ** -0.5
    w_o_na = jax.random.normal(ks[8], (DEPTH_2, NA_WIDTH, D_MODEL), f32) * NA_WIDTH ** -0.5
    w_out = jax.random.normal(ks[9], (DEPTH_2, D_MODEL, D_MODEL), f32) * D_MODEL ** -0.5
    final_norm_g = 1.0 + 0.05 * jax.random.normal(ks[10], (D_MODEL,), f32)
    return {"x": x, "meta_tokens": meta_tokens, "norm_g": norm_g, "w_in": w_in,
            "q_norm_g": q_norm_g, "k_norm_g": k_norm_g, "na_rpb": na_rpb,
            "w_o_attn": w_o_attn, "w_o_na": w_o_na, "w_out": w_out,
            "final_norm_g": final_norm_g}

def second_block(x, meta_tokens, norm_g, w_in, q_norm_g, k_norm_g, na_rpb, w_o_attn, w_o_na, w_out, final_norm_g):
    b, s, _ = x.shape
    meta = jnp.broadcast_to(meta_tokens[None].astype(x.dtype), (b, N_META, D_MODEL))
    h = jnp.concatenate([meta, x], axis=1)
    cos, sin = axial_rope_tables(s)
    for i in range(DEPTH_2):
        h = hybrid_layer(h, norm_g[i], w_in[i], q_norm_g[i], k_norm_g[i], na_rpb[i],
                         w_o_attn[i], w_o_na[i], w_out[i], cos, sin)
    h = rms_norm_2(h, final_norm_g)
    return h[:, N_META:]


def setup_inputs(seed=0):
    out = dict(first_inputs(seed))
    for name, value in second_inputs(seed + 1).items():
        if name != "x":
            out[name + "_2"] = value
    return out


def reference(
    x, p, ln1_g, w_in, mlstm_gate_bias, mlstm_norm_g, cmp_pos_k, cmp_pos_v, cmp_k_w1, cmp_k_w2,
    cmp_v_w1, cmp_v_w2, w_out, ln2_g, w_up, conv_w, conv_b, w_down, ple_norm_g, w_ple_gate,
    w_ple_proj, final_g, meta_tokens_2, norm_g_2, w_in_2, q_norm_g_2, k_norm_g_2, na_rpb_2,
    w_o_attn_2, w_o_na_2, w_out_2, final_norm_g_2,
):
    x = first_block(
        x, p, ln1_g, w_in, mlstm_gate_bias, mlstm_norm_g, cmp_pos_k, cmp_pos_v, cmp_k_w1,
        cmp_k_w2, cmp_v_w1, cmp_v_w2, w_out, ln2_g, w_up, conv_w, conv_b, w_down, ple_norm_g,
        w_ple_gate, w_ple_proj, final_g,
    )
    return second_block(
        x, meta_tokens_2, norm_g_2, w_in_2, q_norm_g_2, k_norm_g_2, na_rpb_2, w_o_attn_2,
        w_o_na_2, w_out_2, final_norm_g_2,
    )


_drawn_inputs = setup_inputs


def setup_inputs(seed=0):
    import zlib

    import numpy as np

    out = dict(_drawn_inputs(seed))
    spreads = {}
    factors = {'mlstm_norm_g': 3.014,
     'cmp_pos_k': 8.0,
     'cmp_pos_v': 8.0,
     'conv_b': 6.287,
     'ple_norm_g': 7.346,
     'norm_g_2': 6.982,
     'q_norm_g_2': 8.0,
     'k_norm_g_2': 8.0,
     'na_rpb_2': 8.0}
    for name, (base, spread) in spreads.items():
        noise = np.random.default_rng([zlib.crc32(name.encode()), seed]).standard_normal(out[name].shape)
        drawn = base * np.exp(spread * noise) if base else spread * noise
        out[name] = __import__('jax').numpy.asarray(drawn.astype(out[name].dtype))
    for name, factor in factors.items():
        out[name] = (out[name] * factor).astype(out[name].dtype)
    return out
```

```python
import math
from contextlib import ExitStack

import concourse.bass as bass
import numpy as np
from concourse import mybir

F32, F32R, BF16 = mybir.dt.float32, mybir.dt.float32r, mybir.dt.bfloat16
ALU, ACT, AX = mybir.AluOpType, mybir.ActivationFunctionType, mybir.AxisListType

P = 128
S, D = 512, 1024
KT, TT = D // P, S // P
EPS, NEG = 1e-6, -1e30
PLE, FF = 256, 2048
MH, MD = 4, 128
AH, AG, AD = 8, 2, 64
CB, CS, CH = 32, 16, 128
NC = (S - CB) // CS + 1
MW, AW, KW = MH * MD, AH * AD, AG * AD
Z_MQ, Z_MK, Z_MV, Z_MO = 0, MW, 2 * MW, 3 * MW
Z_MI = 4 * MW
Z_AQ = Z_MI + 2 * MH
Z_KC = Z_AQ + AW
Z_VC, Z_KS, Z_VS, Z_KX, Z_VX = (Z_KC + i * KW for i in range(1, 6))
Z_AG = Z_KC + 6 * KW
META = 16
T2 = S + META
HALF = T2 // 2
GW, ROWS = 64, S // 64
NAW = 16
QB = P // ROWS
C_QA, C_KA, C_VA, C_ZA = 0, 512, 640, 768
C_QB, C_KB, C_VB, C_ZB, C_GA, C_GB = 1280, 1792, 2304, 2816, 3328, 4352
DCP = 2 * NAW - 1 + 16


def constants():
    q = np.arange(P)
    out = {"ident": np.eye(P)}
    dist = (S - P) + q[:, None] - np.arange(S)[None, :]
    out["dist"] = np.where(dist >= 0, dist, 1e30)
    out["later"] = np.where(q[None, :] >= q[:, None], 0.0, NEG)
    t = (np.arange(TT)[None, :] * P + q[:, None])[:, :, None, None]
    end = np.arange(32)[None, None, None, :] * CS + CB - 1
    slope = (2.0 ** -(np.arange(AH) + 1.0))[None, None, :, None]
    ok = (end <= t) & (np.arange(32) < NC)
    out["cbias"] = np.where(ok, -slope * (t - end), NEG) + 0 * slope
    out["cvalid"] = (ok + 0 * end)[:, :, 0, :]
    out["same"] = (q[:, None] // AD == q[None, :] // AD)
    rot = np.zeros((P, P))
    for h in range(2):
        for a in range(2):
            for i in range(16):
                lo, hi = h * 64 + a * 32 + i, h * 64 + a * 32 + 16 + i
                rot[hi, lo] = -1.0
                rot[lo, hi] = 1.0
    out["rot"] = rot
    inv = (np.float32(10000.0) ** (-np.arange(0, 32, 2, dtype=np.float32) / np.float32(32))).astype(np.float32)
    n = np.arange(S)
    row = np.concatenate([n % ROWS, np.zeros(META, int)]).astype(np.float32)
    col = np.concatenate([n // ROWS, np.zeros(META, int)]).astype(np.float32)
    ang = np.concatenate([row[None] * inv[:, None]] * 2 + [col[None] * inv[:, None]] * 2)
    out["cos"] = np.tile(np.cos(ang), (2, 1))
    out["sin"] = np.tile(np.sin(ang), (2, 1))
    cc, jj = (q // ROWS)[:, None], (np.arange(2 * P) // ROWS)[None, :]
    for name, b in (("na_first", 0), ("na_inner", 1), ("na_last", GW // QB - 1)):
        c, j = QB * b + cc, QB * b - 8 + jj
        start = np.clip(c - NAW // 2, 0, GW - NAW)
        out[name] = np.where((j >= start) & (j < start + NAW), 0.0, NEG)
    sel = np.zeros((P, MH, P))
    for h in range(MH):
        sel[h, h] = 1.0
    out["pick"] = sel
    return {k: np.asarray(v, np.float32).reshape(P, -1) for k, v in out.items()}


PARAMS = [("ln1", 8), ("ln2", 8), ("ple", 8), ("fin1", 8), ("conv_w", 48), ("conv_b", 16), ("mnorm", 4),
          ("pe_k", 32), ("pe_v", 32), ("gate_b", 2), ("norm_a", 8), ("norm_b", 8), ("fin2", 8),
          ("qg_a", 1), ("qg_b", 1), ("kg_a", 1), ("kg_b", 1)]


def offsets(pairs):
    at, out = 0, {}
    for name, n in pairs:
        out[name] = (at, n)
        at += n
    return out, at


class Lane:

    def __init__(self, new_sem, engine, name):
        self.new_sem, self.engine, self.name = new_sem, engine, name
        self.seen = {}
        self.last = None
        self.stage("start")

    def stage(self, stage):
        self.sem, self.count = self.new_sem(f"{self.name}_{stage}"), 0

    def did(self, instruction):
        instruction.then_inc(self.sem, 1)
        self.count += 1
        self.last = (self.sem, self.count)
        return self.last

    def wait(self, *marks):
        for mark in marks:
            if mark is not None and self.seen.get(mark[0].name, 0) < mark[1]:
                self.engine.wait_ge(*mark)
                self.seen[mark[0].name] = mark[1]


class Slots:

    def __init__(self, buffers):
        self.buffers, self.free_at, self.n = buffers, [() for _ in buffers], 0

    def take(self, *lanes):
        i = self.n % len(self.buffers)
        self.n += 1
        for lane in lanes:
            lane.wait(*self.free_at[i])
        self.i = i
        return self.buffers[i], i

    def free(self, i, *marks):
        self.free_at[i] = marks


def program(nc, A):
    ctx = ExitStack()
    sems = {}

    def new_sem(name):
        sems[name] = ctx.enter_context(nc.semaphore(name))
        return sems[name]

    with ctx:
        PE, AC, DV, PO, SP = (Lane(new_sem, e, n) for e, n in (
            (nc.tensor, "pe"), (nc.scalar, "act"), (nc.vector, "dve"), (nc.gpsimd, "pool"), (nc.sync, "sp")))
        compute = (PE, AC, DV, PO)

        def stage(name):
            for lane in compute:
                lane.stage(name)

        def fence():
            lasts = [lane.last for lane in compute]
            for lane in (*compute, SP):
                lane.wait(*lasts)

        cursor = [nc.sbuf_base + (-nc.sbuf_base) % 64]

        def region(size):
            at = cursor[0]
            cursor[0] += size + (-size) % 64
            assert cursor[0] <= nc.sbuf_usable_end, (cursor[0], nc.sbuf_usable_end)
            return at

        def place(name, shape, dt, at):
            t = nc.alloc_sbuf_tensor_at(name, shape, dt, offset=at)
            n = 2 if dt == BF16 else 4
            return t, at + n * math.prod(shape[1:]) + (-n * math.prod(shape[1:])) % 64

        def fixed(name, shape, dt=F32):
            at = region((2 if dt == BF16 else 4) * math.prod(shape[1:]))
            return place(name, shape, dt, at)[0]

        X = fixed("x_feature_major", [P, KT, T2])
        H_hi, H_lo = fixed("h_hi", [P, KT, T2], F32R), fixed("h_lo", [P, KT, T2], F32R)
        g_at = region(2 * 4 * KT * T2)
        G_hi, g_mid = place("g_hi", [P, KT, T2], F32R, g_at)
        G_lo, _ = place("g_lo", [P, KT, T2], F32R, g_mid)
        UNIT = 2048
        raw = [fixed(f"w_raw{i}", [P, UNIT]) for i in range(3)]
        whi = [fixed(f"w_hi{i}", [P, UNIT], F32R) for i in range(2)]
        wlo = [fixed(f"w_lo{i}", [P, UNIT], F32R) for i in range(2)]
        prm_at, prm_n = offsets(PARAMS)
        prm = fixed("params", [P, prm_n])
        ident = fixed("identity", [P, P])
        ones = fixed("ones", [P, P])
        sq = [fixed(f"squares{i}", [P, T2]) for i in range(2)]
        rstd = fixed("rstd", [P, T2])
        tmp = fixed("h_rounded_from", [P, T2])
        eps = fixed("eps", [P, 1])
        pad_at = cursor[0]
        R = cursor[0]
        R_END = nc.sbuf_usable_end

        bank = ctx.enter_context(nc.psum_tensor("bank", [P, 8, 512], F32))

        load = new_sem("load_small")
        loads = [0]

        def small(dst, src):
            nc.sync.dma_start(dst, src).then_inc(load, 16)
            loads[0] += 16
            return (load, loads[0])

        cst = A["consts"]
        widths = A["const_at"]

        def table(name, dst):
            at, n = widths[name]
            return small(dst, cst[:, at:at + n])

        small(prm[:, :], A["params"][:, :])
        table("ident", ident[:, :])

        x_rows, _ = place("x_rows", [P, TT, D], F32, g_at)
        loaded = small(x_rows[:, :, :], A["x"].rearrange("(t p) d -> p t d", p=P))
        m_ones = PO.did(nc.gpsimd.memset(ones[:, :], 1.0))
        m_eps = PO.did(nc.gpsimd.memset(eps[:, :], EPS))

        def param(name, i=0, n=1, parts=slice(0, P)):
            at = prm_at[name][0] + i
            return prm[parts, at:at + n]

        units = []

        def plan(w, k0, kts, cols, split=True):
            src = w.rearrange("(k p) n -> p k n", p=P)
            n = sum(b - a for a, b in cols)
            pieces, at = [], 0
            for a, b in cols:
                pieces.append((at, b - a, src[:, k0:k0 + kts, a:b]))
                at += b - a
            assert kts * n <= UNIT
            units.append((pieces, kts, n, split))

        def plan_cols(w, c0, c1, k0=0, kts=KT, step=256):
            for c in range(c0, c1, step):
                plan(w, k0, kts, [(c, min(c + step, c1))])

        def head_pairs(c, a):
            return [(c + AD * h, c + AD * h + AD) for j in range(2) for h in (2 * a + j, 4 + 2 * a + j)]

        w_in = A["w_in"]
        plan(w_in, 0, KT, [(Z_MI, Z_MI + 2 * MH), (Z_AG, Z_AG + 3 * AH)])
        plan_cols(w_in, Z_MQ, Z_MI)
        for a in range(2):
            plan(w_in, 0, KT, head_pairs(Z_AQ, a))
        plan_cols(w_in, Z_KC, Z_AG)
        for w1 in ("cmp_k_w1", "cmp_v_w1"):
            for half in range(2):
                src = A[w1].rearrange("(j d) n -> d j n", d=AD)[:, 16 * half:16 * half + 16, :]
                units.append(([(None, None, src)], 16, CH, False))
        plan_cols(A["w_out"], 0, D)
        for half in range(2):
            for c in range(half * FF // 2, (half + 1) * FF // 2, 128):
                plan(A["w_up"], 0, KT, [(c, c + 128), (FF + c, FF + c + 128)])
            plan_cols(A["w_down"], 0, D, k0=KT * half)
        for c in range(0, D, 256):
            plan(A["w_ple_gate"], 0, KT, [(c, c + 256)])
            plan(A["w_ple_proj"], 0, 2, [(c, c + 256)])
        for layer in range(2):
            w = A["w_in_2"][layer, :, :]
            for a in range(2):
                plan(w, 0, KT, head_pairs(C_QA, a))
            plan_cols(w, C_KA, C_ZA)
            plan_cols(w, C_ZA, C_QB)
            plan_cols(w, C_QB, C_ZB)
            plan_cols(w, C_ZB, C_GA)
            for c in range(0, D, 256):
                plan(w, 0, KT, [(C_GA + c, C_GA + c + 256)])
                plan(A["w_o_attn_2"][layer, :, :], 0, 4, [(c, c + 256)])
                plan(w, 0, KT, [(C_GB + c, C_GB + c + 256)])
                plan(A["w_o_na_2"][layer, :, :], 0, 4, [(c, c + 256)])
            plan_cols(A["w_out_2"][layer, :, :], 0, D)

        raw_sem = [new_sem(f"w_arrived{i}") for i in range(3)]
        raw_n = [0, 0, 0]
        arrived, split_done, used = {}, {}, {}
        state = {"dma": 0, "split": 0, "use": 0}

        def released(u):
            return split_done.get(u) if units[u][3] else used.get(u)

        def fetch():
            while state["dma"] < len(units):
                u = state["dma"]
                i = u % 3
                if u >= 3:
                    marks = released(u - 3)
                    if marks is None:
                        return
                    SP.wait(*marks)
                pieces, kts, n, _ = units[u]
                dst = raw[i][:, 0:kts * n].rearrange("p (k n) -> p k n", k=kts)
                for at, width, src in pieces:
                    if at is None:
                        for half in range(2):
                            nc.sync.dma_start(dst[64 * half:64 * half + 64, :, :], src).then_inc(raw_sem[i], 16)
                            raw_n[i] += 16
                    else:
                        nc.sync.dma_start(dst[:, :, at:at + width], src).then_inc(raw_sem[i], 16)
                        raw_n[i] += 16
                arrived[u] = (raw_sem[i], raw_n[i])
                state["dma"] += 1

        def split(u):
            if u >= len(units) or u in split_done or not units[u][3]:
                return
            _, kts, n, _ = units[u]
            i = u % 2
            prior = used.get(u - 2, ())
            AC.wait(arrived[u], *prior)
            hi = AC.did(nc.scalar.activation(whi[i][:, 0:kts * n], raw[u % 3][:, 0:kts * n], ACT.Copy))
            DV.wait(arrived[u], *prior, hi)
            lo = DV.did(nc.vector.tensor_tensor(wlo[i][:, 0:kts * n], raw[u % 3][:, 0:kts * n],
                                                whi[i][:, 0:kts * n].bitcast(F32), ALU.subtract))
            split_done[u] = (hi, lo)

        def weights():
            u = state["use"]
            state["use"] += 1
            fetch()
            split(u)
            fetch()
            _, kts, n, do_split = units[u]
            if not do_split:
                PE.wait(arrived[u])
                split(u + 1)
                return raw[u % 3][:, 0:kts * n].rearrange("p (k n) -> p k n", k=kts), None, u
            PE.wait(*split_done[u])
            views = [t[u % 2][:, 0:kts * n].rearrange("p (k n) -> p k n", k=kts) for t in (whi, wlo)]
            return views[0], views[1], u

        def weights_done(u, mark):
            used[u] = (mark,)
            fetch()
            if u + 1 < len(units):
                split(u + 1)
                fetch()

        def prefetch_split(u):
            split(u)

        def product(outs, stationary, moving, k, first, last):
            ins = None
            terms = ((0, 0), (0, 1), (1, 0))
            for n, (a, b) in enumerate(terms):
                for i, out in enumerate(outs):
                    ins = nc.tensor.matmul(out, stationary[a](k), moving[b](k)[i],
                                           start=first and n == 0, stop=last and n == 2)
            return ins

        def chunks(n):
            return [(0, n)] if n <= 512 else [(0, HALF), (HALF, n)]

        def to_features(act, kts, wviews, cols, n, out_banks, k0=0, first=True, last=True):
            hi, lo = wviews
            ch = chunks(n)
            outs = [bank[:, out_banks + i, 0:b - a] for i, (a, b) in enumerate(ch)]
            mv = [lambda k, t=t: [t[:, k + k0, a:b] for a, b in ch] for t in act]
            st = [lambda k, t=t: cols(t, k) for t in (hi, lo)]
            for k in range(kts):
                ins = product(outs, st, mv, k, first and k == 0, last and k == kts - 1)
            return PE.did(ins)

        def columns(c):
            return lambda t, k: t[:, k, c:c + P]

        def feature_view(b, n):
            if n <= 512:
                return bank[:, b, 0:n]
            return bank[:, b:b + 2, 0:HALF]

        def dest(ap, n):
            return ap if n <= 512 else ap.rearrange("p (c t) -> p c t", c=2)

        def to_tokens(act, t0, tn, wviews, c0, cn, out):
            st = [lambda k, t=t: t[:, k, t0:t0 + tn] for t in act]
            mv = [lambda k, t=t: [t[:, k, c0:c0 + cn]] for t in wviews]
            for k in range(KT):
                ins = product([out], st, mv, k, k == 0, k == KT - 1)
            return PE.did(ins)

        def split_into(hi, lo, src, *marks, shape=lambda x: x):
            AC.wait(*marks)
            a = AC.did(nc.scalar.activation(shape(hi), src, ACT.Copy))
            DV.wait(*marks, a)
            b = DV.did(nc.vector.tensor_tensor(shape(lo), src, shape(hi.bitcast(F32)), ALU.subtract))
            return a, b

        dense = Slots([0, 2])

        def mean_square(x_tile, n, kts, b, *ready):
            freed = [(), ()]
            for k in range(kts):
                AC.wait(*ready, *freed[k % 2])
                m = AC.did(nc.scalar.activation(sq[k % 2][:, 0:n], x_tile(k), ACT.Square))
                PE.wait(m, m_ones)
                for i, (a, z) in enumerate(chunks(n)):
                    ins = nc.tensor.matmul(bank[:, b + i, 0:z - a], ones[:, :], sq[k % 2][:, a:z],
                                           start=k == 0, stop=k == kts - 1)
                m = PE.did(ins)
                freed[k % 2] = (m,)
            return m

        def root_reciprocal(out, src, scale, *marks):
            AC.wait(*marks, m_eps)
            m = AC.did(nc.scalar.activation(out, src, ACT.Sqrt, bias=eps[0:out.shape[0], :], scale=scale))
            DV.wait(m)
            return DV.did(nc.vector.reciprocal(out, out))

        def rms_norm_split(gain, n, *ready):
            m = mean_square(lambda k: X[:, k, 0:n], n, KT, 4, *ready)
            DV.wait(*ready)
            r = root_reciprocal(dest(rstd[:, 0:n], n), feature_view(4, n), 1.0 / D, m)
            marks = []
            bufs = (tmp, sq[0], sq[1])
            freed = {}
            for k in range(KT):
                t = bufs[k % 3]
                DV.wait(r, *freed.get(k % 3, ()))
                c = DV.did(nc.vector.scalar_tensor_tensor(t[:, 0:n], X[:, k, 0:n], param(gain, k), rstd[:, 0:n],
                                                          ALU.mult, ALU.mult))
                a, b = split_into(H_hi[:, k, 0:n], H_lo[:, k, 0:n], t[:, 0:n], c)
                freed[k % 3] = (a, b)
                marks += [a, b]
            PE.wait(*marks)
            return marks

        stage("x_in")
        fetch()
        small_loaded = (load, loads[0])
        for lane in compute:
            lane.wait(small_loaded)
        split(0)
        x_done = []
        turn = Slots([0, 1, 2, 3, 4, 5, 6, 7])
        for k in range(KT):
            b, i = turn.take(PE)
            for t in range(TT):
                ins = nc.tensor.transpose(bank[:, b, t * P:(t + 1) * P], x_rows[:, t, k * P:(k + 1) * P], ident[:, :])
            m = PE.did(ins)
            AC.wait(m)
            x_done.append(AC.did(nc.scalar.activation(X[:, k, 0:S], bank[:, b, :], ACT.Copy)))
        stage("norm1")
        rms_norm_split("ln1", S, *x_done)

        c = R
        mqT, c = place("mq", [P, MH, S], F32, c)
        mkT, c = place("mk", [P, MH, S], F32, c)
        mv, c = place("mv", [P, TT, MH, MD + 1], F32, c)
        mo, c = place("mo_gate", [P, TT, MW], F32, c)
        g4, c = place("gate_rows", [MH, 5, S], F32, c)
        gate_row = {n: g4[:, i, :] for i, n in enumerate(("f", "a", "b", "i", "m"))}
        assert c <= R_END, c
        c2 = g_at
        aqT, c2 = place("aq", [P, 4, S], F32, c2)
        kvT, c2 = place("kv", [P, 4, S], F32, c2)
        vs, c2 = place("vs", [P, 2, TT, KW], F32, c2)
        ag, c2 = place("ag", [P, TT, 3 * AH], F32, c2)
        col4, c2 = place("gate_columns", [P, 3, TT, MH], F32, c2)
        msq, c2 = place("m_square", [P, 2, TT, MH], F32, c2)
        late, c2 = place("later", [P, P], F32, c2)
        pick, c2 = place("pick", [P, MH, P], F32, c2)
        den, c2 = place("mlstm_den", [P, 4], F32, c2)
        diag = [None, None]
        diag[0], c2 = place("diag0", [P, P], F32, c2)
        assert c2 <= g_at + 2 * 4 * KT * T2, c2 - g_at

        stage("project1")
        fence()
        table("later", late[:, :])
        tab1 = table("pick", pick[:, :, :].rearrange("p h q -> p (h q)"))

        Hs = (H_hi, H_lo)
        hi, lo, u = weights()
        b, i = dense.take(PE)
        for n in range(2):
            for k in range(KT):
                ins = product([bank[0:MH, b + n, 0:S]],
                              [lambda k, t=t: t[:, k, MH * n:MH * n + MH] for t in (hi, lo)],
                              [lambda k, t=t: [t[:, k, 0:S]] for t in Hs], k, k == 0, k == KT - 1)
        m = PE.did(ins)
        AC.wait(m)
        mi = AC.did(nc.scalar.activation(gate_row["i"], bank[0:MH, b, 0:S], ACT.Identity, bias=param("gate_b", 0, 1, slice(0, MH))))
        mf = AC.did(nc.scalar.activation(gate_row["f"], bank[0:MH, b + 1, 0:S], ACT.Identity, bias=param("gate_b", 1, 1, slice(0, MH))))
        dense.free(i, mf)
        b, i = dense.take(PE)
        for t in range(TT):
            m = to_tokens(Hs, t * P, P, (hi, lo), 2 * MH, 3 * AH, bank[:, b, t * 3 * AH:(t + 1) * 3 * AH])
        weights_done(u, m)
        AC.wait(m)
        m = AC.did(nc.scalar.activation(ag[:, :, :].rearrange("p t g -> p (t g)"), bank[:, b, 0:TT * 3 * AH], ACT.Tanh, scale=0.5))
        dense.free(i, m)
        DV.wait(m)
        ag_done = DV.did(nc.vector.tensor_scalar(ag[:, :, :], ag[:, :, :], 0.5, 0.5, ALU.mult, ALU.add))

        def evacuate(dst, src, mark, scale=None, lane=None):
            if lane is DV:
                DV.wait(mark)
                if scale is None:
                    return DV.did(nc.vector.tensor_copy(dst, src))
                return DV.did(nc.vector.tensor_scalar(dst, src, scale, None, ALU.mult))
            AC.wait(mark)
            if scale is None:
                return AC.did(nc.scalar.activation(dst, src, ACT.Copy))
            return AC.did(nc.scalar.activation(dst, src, ACT.Copy, scale=scale))

        def project_features(dsts, n, act=Hs, scale=None, cols=None, kts=KT):
            hi, lo, u = weights()
            out = []
            for j, dst in enumerate(dsts):
                b, i = dense.take(PE)
                m = to_features(act, kts, (hi, lo), (cols or columns)(j if cols else j * P), n, b)
                if j == len(dsts) - 1:
                    weights_done(u, m)
                e = evacuate(dest(dst, n), feature_view(b, n), m, scale, DV if j % 2 else AC)
                dense.free(i, e)
                out.append(e)
            return out

        def project_tokens(dst_of, tiles, act=Hs, ranges=((0, 256),), func=None):
            hi, lo, u = weights()
            out = []
            jobs = [(r, t) for r in range(len(ranges)) for t in range(len(tiles))]
            for n, (r, t) in enumerate(jobs):
                c0, cn = ranges[r]
                t0, tn = tiles[t]
                b, i = dense.take(PE)
                m = to_tokens(act, t0, tn, (hi, lo), c0, cn, bank[0:tn, b, 0:cn])
                if n == len(jobs) - 1:
                    weights_done(u, m)
                dst, shape = dst_of(r, t)
                src = shape(bank[0:tn, b, 0:cn])
                if func is None:
                    e = evacuate(dst, src, m, None, DV if n % 2 else AC)
                else:
                    AC.wait(m)
                    e = AC.did(nc.scalar.activation(dst, src, func, scale=0.5))
                dense.free(i, e)
                out.append(e)
            return out

        tiles1 = [(t * P, P) for t in range(TT)]
        mlstm_in = []
        for a in range(2):
            mlstm_in += project_features([mqT[:, 2 * a + j, :] for j in range(2)], S, scale=MD ** -0.5)
        for a in range(2):
            mlstm_in += project_features([mkT[:, 2 * a + j, :] for j in range(2)], S)
        for a in range(2):
            mlstm_in += project_tokens(lambda r, t: (mv[:, t, 2 * a:2 * a + 2, 0:MD],
                                                     lambda x: x.rearrange("p (h d) -> p h d", h=2)), tiles1)
        mlstm_in.append(PO.did(nc.gpsimd.memset(mv[:, :, :, MD:MD + 1], 1.0)))
        for a in range(2):
            mlstm_in += project_tokens(lambda r, t: (mo[:, t, 256 * a:256 * a + 256], lambda x: x), tiles1, func=ACT.Tanh)

        stage("gates")
        gr = gate_row
        DV.wait(mf, mi)
        m = DV.did(nc.vector.scalar_tensor_tensor(gr["a"], gr["f"], -1.0, gr["f"], ALU.mult, ALU.min))
        AC.wait(m)
        m = AC.did(nc.scalar.activation(gr["a"], gr["a"], ACT.Exp))
        AC.wait(m, m_ones)
        m = AC.did(nc.scalar.activation(gr["a"], gr["a"], ACT.Ln, bias=ones[0:MH, 0:1]))
        DV.wait(m)
        m = DV.did(nc.vector.scalar_tensor_tensor(gr["f"], gr["f"], 0.0, gr["a"], ALU.min, ALU.subtract))
        DV.wait(m)
        m = DV.did(nc.vector.memset(gr["m"], 1.0))
        DV.wait(m)
        m = DV.did(nc.vector.tensor_tensor_scan(gr["b"], gr["m"], gr["f"], 0.0, ALU.mult, ALU.add))
        DV.wait(m)
        m = DV.did(nc.vector.tensor_tensor(gr["i"], gr["i"], gr["b"], ALU.subtract))
        DV.wait(m)
        m = DV.did(nc.vector.tensor_tensor_scan(gr["a"], gr["i"], gr["i"], 0.0, ALU.max, ALU.max))
        DV.wait(m)
        m = DV.did(nc.vector.tensor_tensor(gr["m"], gr["b"], gr["a"], ALU.add))
        DV.wait(m)
        m = DV.did(nc.vector.tensor_scalar(gr["f"], gr["a"], -1.0, None, ALU.mult))
        PE.wait(m, tab1)
        b, i = dense.take(PE)
        for n, name in enumerate(("i", "m")):
            for t in range(TT):
                ins = nc.tensor.transpose(bank[:, b, (n * TT + t) * MH:(n * TT + t + 1) * MH],
                                          gr[name][:, t * P:(t + 1) * P], ident[0:MH, 0:MH])
        m = PE.did(ins)
        DV.wait(m)
        m = DV.did(nc.vector.tensor_copy(col4[:, 0:2, :, :].rearrange("p a t h -> p (a t h)"), bank[:, b, 0:2 * TT * MH]))
        dense.free(i, m)
        AC.wait(m)
        em_done = AC.did(nc.scalar.activation(col4[:, 2, :, :], col4[:, 1, :, :], ACT.Exp, scale=-1.0))

        stage("mlstm")
        c3 = c
        negM, c3 = place("neg_M", [P, S], F32, c3)
        decay, c3 = place("decay", [P, S], F32, c3)
        WT, c3 = place("mlstm_weights", [P, TT, S], F32, c3)
        assert c3 <= R_END, c3
        scores = Slots([4, 5])
        outs_ = Slots([6, 7])
        hm = {}
        wt_free = ()
        neg_free = ()
        PE.wait(*mlstm_in)
        marks_last = []
        for h in range(MH):
            b, i = dense.take(PE)
            m = PE.did(nc.tensor.matmul(bank[:, b, 0:S], pick[0:MH, h, :], gr["f"], start=True, stop=True))
            AC.wait(*neg_free)
            mneg = evacuate(negM[:, :], bank[:, b, 0:S], m)
            dense.free(i, mneg)
            wmarks = []
            for s in range(TT):
                n = S - s * P
                b, i = scores.take(PE)
                mqk = PE.did(nc.tensor.matmul(bank[:, b, 0:n], mkT[:, h, s * P:(s + 1) * P], mqT[:, h, s * P:S],
                                              start=True, stop=True))
                DV.wait(mneg, *wt_free)
                md = DV.did(nc.vector.tensor_tensor(diag[0][:, :], negM[:, s * P:(s + 1) * P], late[:, :], ALU.add))
                AC.wait(md, em_done, *wmarks[-1:])
                me = AC.did(nc.scalar.activation(decay[:, 0:P], diag[0][:, :], ACT.Exp, bias=col4[:, 0, s, h:h + 1]))
                if n > P:
                    me = AC.did(nc.scalar.activation(decay[:, P:n], negM[:, (s + 1) * P:S], ACT.Exp,
                                                     bias=col4[:, 0, s, h:h + 1]))
                DV.wait(me, mqk)
                mw = DV.did(nc.vector.tensor_tensor(WT[:, s, s * P:S], bank[:, b, 0:n], decay[:, 0:n], ALU.mult))
                scores.free(i, mw)
                wmarks.append(mw)
            neg_free = (me,)
            PE.wait(*wmarks)
            for l in range(TT):
                b, i = outs_.take(PE)
                for s in range(l + 1):
                    ins = nc.tensor.matmul(bank[:, b, 0:MD + 1], WT[:, s, l * P:(l + 1) * P], mv[:, s, h, :],
                                           start=s == 0, stop=s == l)
                m = PE.did(ins)
                DV.wait(m, em_done)
                d1 = DV.did(nc.vector.scalar_tensor_tensor(den[:, 0:1], bank[:, b, MD:MD + 1], -1.0, col4[:, 2, l, h:h + 1],
                                                           ALU.mult, ALU.max))
                DV.wait(d1)
                d1 = DV.did(nc.vector.tensor_tensor(den[:, 1:2], bank[:, b, MD:MD + 1], den[:, 0:1], ALU.max))
                DV.wait(d1)
                d1 = DV.did(nc.vector.reciprocal(den[:, 2:3], den[:, 1:2]))
                DV.wait(d1)
                hmv = mqT[:, h, l * P:(l + 1) * P]
                d1 = DV.did(nc.vector.tensor_scalar(hmv, bank[:, b, 0:MD], den[:, 2:3], None, ALU.mult))
                outs_.free(i, d1)
                AC.wait(d1, *([wt_sq] if (h or l) else []))
                wt_sq = AC.did(nc.scalar.activation(decay[:, 0:P], hmv, ACT.Square, accum_out=msq[:, 0, l, h:h + 1]))
            wt_free = (m,)
        AC.wait(wt_sq)
        r = root_reciprocal(msq[:, 1, :, :], msq[:, 0, :, :], 1.0 / MD, wt_sq)
        DV.wait(r)
        r = DV.did(nc.vector.tensor_scalar(msq[:, 1, :, :], msq[:, 1, :, :], 0.5, None, ALU.mult))
        DV.wait(r)
        hm_v = mqT[:, :, :].rearrange("p h (t d) -> p t h d", t=TT)
        mrow = mo
        marks = []
        for t in range(TT):
            g = mo[:, t, :].rearrange("p (h d) -> p h d", h=MH)
            m = DV.did(nc.vector.scalar_tensor_tensor(g, g, 1.0, hm_v[:, t, :, :], ALU.add, ALU.mult))
            DV.wait(m)
            marks.append(DV.did(nc.vector.tensor_tensor(g, g, msq[:, 1, t, :].unsqueeze(2).broadcast_to([P, MH, MD]), ALU.mult)))
        m_out_done = marks

        stage("project_a")
        nsa_in = []
        for a in range(2):
            nsa_in += project_features([aqT[:, 2 * a + j, :] for j in range(2)], S, scale=AD ** -0.5)
        cmp_in = project_features([kvT[:, j, :] for j in range(2)], S)
        for n in range(2):
            hi, lo, u = weights()
            b, i = dense.take(PE)
            m = to_features(Hs, KT, (hi, lo), columns(0), S, b)
            e = evacuate(kvT[:, 2 + n, :], bank[:, b, 0:S], m)
            dense.free(i, e)
            nsa_in.append(e)
            b, i = dense.take(PE)
            for t in range(TT):
                m = to_tokens(Hs, t * P, P, (hi, lo), P, KW, bank[:, b, t * KW:(t + 1) * KW])
            weights_done(u, m)
            e = evacuate(vs[:, n, :, :].rearrange("p t c -> p (t c)"), bank[:, b, :], m, None, DV)
            dense.free(i, e)
            nsa_in.append(e)

        stage("compress")
        fence()
        c = R
        mqkeep, c = place("_a", [P, 16], F32, c)
        block, c = place("cmp_blocks", [P, CB, NC], F32, c)
        hid, c = place("cmp_hidden", [P, 4, 32], F32, c)
        cw2, c = place("cmp_w2", [P, 2, 2 * AD], F32, c)
        kcT, c = place("kc", [P, 32], F32, c)
        vcn, c = place("vc", [32, KW], F32, c)
        assert c <= R + 8192 + 8192, c - R
        m = None
        AC.wait(PO.did(nc.gpsimd.memset(kcT[:, :], 0.0)))
        for n, w2 in enumerate(("cmp_k_w2", "cmp_v_w2")):
            for half in range(2):
                w2_in = small(cw2[:, n, half * AD:half * AD + AD], A[w2][:, :])
        for n in range(2):
            src = kvT[:, n, :]
            DV.wait(*cmp_in)
            if m is not None:
                DV.wait(m)
            win = bass_windows(src)
            pe = param("pe_k" if n == 0 else "pe_v", 0, CB)
            mb = DV.did(nc.vector.tensor_tensor(block[:, :, :], win, pe.unsqueeze(2).broadcast_to([P, CB, NC]), ALU.add))
            PE.wait(mb)
            b, i = dense.take(PE)
            for half in range(2):
                w1, _, u = weights()
                for g in range(AG):
                    rows = slice(g * AD, (g + 1) * AD)
                    for j in range(16):
                        jj = 16 * half + j
                        ins = nc.tensor.matmul(bank[:, b + g, 0:NC], w1[rows, j, :], block[rows, jj, :],
                                               start=jj == 0, stop=jj == CB - 1)
                m = PE.did(ins)
                weights_done(u, m)
            xg = bank[:, b:b + 2, 0:NC]
            hx, h3 = hid[:, 0:2, 0:NC], hid[:, 2:4, 0:NC]
            AC.wait(m)
            e = AC.did(nc.scalar.activation(hx, xg, ACT.Copy))
            AC.wait(e)
            e = AC.did(nc.scalar.activation(h3, hx, ACT.Square))
            DV.wait(e)
            e = DV.did(nc.vector.tensor_scalar(h3, h3, 0.044715, 1.0, ALU.mult, ALU.add))
            DV.wait(e)
            e = DV.did(nc.vector.tensor_tensor(h3, h3, hx, ALU.mult))
            AC.wait(e)
            e = AC.did(nc.scalar.activation(h3, h3, ACT.Tanh, scale=math.sqrt(2 / math.pi)))
            DV.wait(e)
            e = DV.did(nc.vector.scalar_tensor_tensor(h3, h3, 1.0, hx, ALU.add, ALU.mult))
            DV.wait(e)
            e = DV.did(nc.vector.tensor_scalar(hx, h3, 0.5, None, ALU.mult))
            dense.free(i, e)
            PE.wait(e, w2_in)
            b, i = dense.take(PE)
            for g in range(AG):
                if n == 0:
                    ins = nc.tensor.matmul(bank[:, b + g, 0:NC], cw2[:, 0, :], hid[:, g, 0:NC], start=True, stop=True)
                else:
                    ins = nc.tensor.matmul(bank[0:NC, b, g * AD:(g + 1) * AD], hid[:, g, 0:NC], cw2[:, 1, 0:AD],
                                           start=True, stop=True)
            m = PE.did(ins)
            if n == 0:
                for g in range(AG):
                    rows = slice(g * AD, (g + 1) * AD)
                    e = evacuate(kcT[rows, 0:NC], bank[rows, b + g, 0:NC], m)
            else:
                e = evacuate(vcn[0:NC, :], bank[0:NC, b, 0:KW], m)
            dense.free(i, e)
            cmp_done = e
        DV.wait(cmp_done)
        AC.wait(e)

        stage("nsa")
        fence()
        dist, c = place("distance", [P, S], F32, c)
        cb, c = place("cmp_bias", [P, TT, AH * 32], F32, c)
        cv, c = place("cmp_valid", [P, TT, 32], F32, c)
        assert c <= R + 16384, c - R
        c = R + 8192 + 8192
        a_rows, c = place("a_rows", [P, TT, AW], F32, c)
        assert c <= R + 16384 + 8256 + 63
        _, c = place("_mo_again", [P, TT, MW], F32, R + 16384 + 4 * TT * MH * (MD + 1))
        sc_s = [None, None]
        pr_s = [None, None]
        pt_s = [None, None]
        for n in range(2):
            sc_s[n], c = place(f"scores{n}", [P, S], F32, c)
            pr_s[n], c = place(f"probs{n}", [P, S], F32, c)
            pt_s[n], c = place(f"probsT{n}", [P, TT, P], F32, c)
        stat, c = place("softmax_stats", [P, 8, AH], F32, c)
        mixed, c = place("branch_part", [P, 512], F32, c)
        assert c <= R_END, c
        table("dist", dist[:, :])
        table("cbias", cb[:, :, :].rearrange("p t x -> p (t x)"))
        tabs = table("cvalid", cv[:, :, :].rearrange("p t x -> p (t x)"))
        DV.wait(tabs, ag_done)
        PE.wait(*nsa_in, tabs)
        scores, turned, outb = Slots([4, 5]), Slots([6]), Slots([7, 0])
        sc, pr, pt = Slots(sc_s), Slots(pr_s), Slots(pt_s)
        a_done = []

        def qk_rows(h):
            return slice(AD * (h // 4), AD * (h // 4) + AD)

        for t in range(TT):
            b, i = scores.take(PE)
            b2, i2 = scores.take(PE)
            for h in range(AH):
                ins = nc.tensor.matmul(bank[:, b + h // 4, h % 4 * 32:h % 4 * 32 + NC + 1], aqT[qk_rows(h), h % 4, t * P:(t + 1) * P],
                                       kcT[qk_rows(h), 0:NC + 1], start=True, stop=True)
            m = PE.did(ins)
            s_, si = sc.take(DV)
            DV.wait(m)
            e = DV.did(nc.vector.tensor_tensor(s_[:, 0:256].rearrange("p (g x) -> p g x", g=2), bank[:, b:b + 2, 0:128],
                                               cb[:, t, :].rearrange("p (g x) -> p g x", g=2), ALU.add))
            scores.free(i, e)
            scores.free(i2, e)
            DV.wait(e)
            s3 = s_[:, 0:256].rearrange("p (h n) -> p h n", h=AH)
            e = DV.did(nc.vector.reduce_max(stat[:, 0, :], s3, AX.X))
            DV.wait(e)
            e = DV.did(nc.vector.tensor_tensor(s3, s3, stat[:, 0, :].unsqueeze(2).broadcast_to([P, AH, 32]), ALU.subtract))
            AC.wait(e)
            e = AC.did(nc.scalar.activation(s_[:, 0:256], s_[:, 0:256], ACT.Exp))
            DV.wait(e)
            e = DV.did(nc.vector.reduce_sum(stat[:, 1, :], s3, AX.X))
            p_, pi = pr.take(DV)
            p3 = p_[:, 0:256].rearrange("p (h n) -> p h n", h=AH)
            e2 = DV.did(nc.vector.tensor_tensor(p3, s3, cv[:, t, :].unsqueeze(1).broadcast_to([P, AH, 32]), ALU.mult))
            sc.free(si, e2)
            gates = ag[:, t, :].rearrange("p (h b) -> p b h", b=3)
            DV.wait(e)
            e = DV.did(nc.vector.reciprocal(stat[:, 1, :], stat[:, 1, :]))
            DV.wait(e)
            e = DV.did(nc.vector.tensor_tensor(stat[:, 1, :], stat[:, 1, :], gates[:, 0, :], ALU.mult))
            b, i = turned.take(PE)
            PE.wait(e2)
            q_, qi = pt.take(AC)
            ob, oi = outb.take(PE)
            for g in range(2):
                for h in range(4):
                    ins = nc.tensor.transpose(bank[0:32, b, h * P:(h + 1) * P], p_[:, (4 * g + h) * 32:(4 * g + h + 1) * 32], ident[:, :])
                m = PE.did(ins)
                AC.wait(*( [mo_] if g else []))
                m = evacuate(q_[0:NC, :, :].rearrange("p t q -> p (t q)"), bank[0:NC, b, :], m)
                PE.wait(m)
                for h in range(4):
                    ins = nc.tensor.matmul(bank[:, ob, (4 * g + h) * AD:(4 * g + h + 1) * AD], q_[0:NC, h, :],
                                           vcn[0:NC, g * AD:(g + 1) * AD], start=True, stop=True)
                mo_ = PE.did(ins)
            turned.free(i, m)
            pr.free(pi, mo_)
            pt.free(qi, mo_)
            DV.wait(mo_, e)
            ar = a_rows[:, t, :].rearrange("p (h d) -> p h d", h=AH)
            e = DV.did(nc.vector.tensor_tensor(ar, bank[:, ob, :].rearrange("p (h d) -> p h d", h=AH),
                                               stat[:, 1, :].unsqueeze(2).broadcast_to([P, AH, AD]), ALU.mult))
            outb.free(oi, e)
            n = (t + 1) * P
            acc = e
            for br in range(2):
                ob, oi = outb.take(PE)
                stat_ready = acc

                def score(h):
                    b, i = scores.take(PE)
                    m = PE.did(nc.tensor.matmul(bank[:, b, 0:n], aqT[qk_rows(h), h % 4, t * P:(t + 1) * P],
                                                kvT[qk_rows(h), 2 + br, 0:n], start=True, stop=True))
                    s_, si = sc.take(DV)
                    DV.wait(m)
                    e = DV.did(nc.vector.scalar_tensor_tensor(s_[:, 0:n], dist[:, S - n:S], -2.0 ** -(h + 1), bank[:, b, 0:n],
                                                              ALU.mult, ALU.add))
                    scores.free(i, e)
                    DV.wait(e)
                    e = DV.did(nc.vector.reduce_max(stat[:, 2, h:h + 1], s_[:, 0:n], AX.X, negate=True))
                    p_, pi = pr.take(AC)
                    AC.wait(e, stat_ready)
                    e = AC.did(nc.scalar.activation(p_[:, 0:n], s_[:, 0:n], ACT.Exp, bias=stat[:, 2, h:h + 1],
                                                    accum_out=stat[:, 3, h:h + 1]))
                    sc.free(si, e)
                    return p_, pi, e

                def value(h, p_, pi, ready):
                    b, i = turned.take(PE)
                    PE.wait(ready)
                    for k in range(t + 1):
                        ins = nc.tensor.transpose(bank[:, b, k * P:(k + 1) * P], p_[:, k * P:(k + 1) * P], ident[:, :])
                    m = PE.did(ins)
                    pr.free(pi, m)
                    lane = DV if h % 3 == 2 else AC
                    q_, qi = pt.take(lane)
                    m = evacuate(q_[:, 0:t + 1, :].rearrange("p t q -> p (t q)"), bank[:, b, 0:n], m, None, lane)
                    turned.free(i, m)
                    PE.wait(m)
                    for k in range(t + 1):
                        ins = nc.tensor.matmul(bank[:, ob, h * AD:(h + 1) * AD], q_[:, k, :],
                                               vs[:, br, k, (h // 4) * AD:(h // 4 + 1) * AD], start=k == 0, stop=k == t)
                    m = PE.did(ins)
                    pt.free(qi, m)
                    return m

                order = [0, 4, 1, 5, 2, 6, 3, 7]
                ahead = score(order[0])
                for n_, h in enumerate(order):
                    now = ahead
                    if n_ + 1 < AH:
                        ahead = score(order[n_ + 1])
                    m = value(h, *now)
                DV.wait(now[2])
                e = DV.did(nc.vector.reciprocal(stat[:, 4, :], stat[:, 3, :]))
                DV.wait(e)
                e = DV.did(nc.vector.tensor_tensor(stat[:, 4, :], stat[:, 4, :], gates[:, 1 + br, :], ALU.mult))
                DV.wait(e, m)
                mx = mixed[:, :].rearrange("p (h d) -> p h d", h=AH)
                e = DV.did(nc.vector.tensor_tensor(mx, bank[:, ob, :].rearrange("p (h d) -> p h d", h=AH),
                                                   stat[:, 4, :].unsqueeze(2).broadcast_to([P, AH, AD]), ALU.mult))
                outb.free(oi, e)
                DV.wait(e)
                acc = DV.did(nc.vector.tensor_tensor(a_rows[:, t, :], a_rows[:, t, :], mixed[:, :], ALU.add))
            a_done.append(acc)

        stage("mix_out")
        fence()
        for k in range(KT):
            rows = mo if k < 4 else a_rows
            b, i = dense.take(PE)
            for t in range(TT):
                ins = nc.tensor.transpose(bank[:, b, t * P:(t + 1) * P], rows[:, t, (k % 4) * P:(k % 4 + 1) * P], ident[:, :])
            m = PE.did(ins)
            if k < 4:
                s_, si = sc.take(AC)
                AC.wait(m)
                m = AC.did(nc.scalar.activation(s_[:, :], bank[:, b, :], ACT.Copy, scale=param("mnorm", k)))
                dense.free(i, m)
                AC.wait(m)
                a, z = split_into(H_hi[:, k, 0:S], H_lo[:, k, 0:S], s_[:, :], m)
                sc.free(si, a, z)
            else:
                a, z = split_into(H_hi[:, k, 0:S], H_lo[:, k, 0:S], bank[:, b, :], m)
                dense.free(i, a, z)
            PE.wait(a, z)

        def add_residual(act, kts, n, units_n, act_k0=0, x_ready=()):
            out = []
            for uu in range(units_n):
                hi, lo, u = weights()
                for j in range(2):
                    k = 2 * uu + j
                    b, i = dense.take(PE)
                    m = to_features(act, kts, (hi, lo), columns(j * P), n, b)
                    if j:
                        weights_done(u, m)
                    DV.wait(m, *x_ready)
                    e = DV.did(nc.vector.tensor_tensor(dest(X[:, k, 0:n], n), feature_view(b, n), dest(X[:, k, 0:n], n), ALU.add))
                    dense.free(i, e)
                    out.append(e)
            return out

        x_done = add_residual(Hs, KT, S, 4)

        stage("ffn")
        rms_norm_split("ln2", S, *x_done)
        fence()
        Gs = (G_hi, G_lo)
        c = R
        conv = [None, None]
        acc_ = [None, None]
        th = [None, None]
        for n in range(2):
            conv[n], c = place(f"conv_in{n}", [P, S + 2], F32, c)
            acc_[n], c = place(f"conv_out{n}", [P, S], F32, c)
            th[n], c = place(f"conv_tanh{n}", [P, S], F32, c)
        zero = [PO.did(nc.gpsimd.memset(conv[n][:, 0:2], 0.0)) for n in range(2)]
        DV.wait(*zero)
        cv_s = Slots([0, 1])
        for half in range(2):
            g_ready = []
            for jj in range(KT):
                j = half * KT + jj
                hi, lo, u = weights()
                bg, ig = dense.take(PE)
                mg = to_features(Hs, KT, (hi, lo), columns(0), S, bg)
                mvv = to_features(Hs, KT, (hi, lo), columns(P), S, bg + 1)
                weights_done(u, mvv)
                n, ni = cv_s.take(AC)
                AC.wait(mg)
                e1 = AC.did(nc.scalar.activation(conv[n][:, 2:S + 2], bank[:, bg, :], ACT.Copy))
                e2 = AC.did(nc.scalar.activation(acc_[n][:, :], bank[:, bg, :], ACT.Identity, scale=param("conv_w", 32 + j),
                                                 bias=param("conv_b", j)))
                DV.wait(e1, e2)
                e = DV.did(nc.vector.scalar_tensor_tensor(acc_[n][:, :], conv[n][:, 1:S + 1], param("conv_w", 16 + j), acc_[n][:, :],
                                                          ALU.mult, ALU.add))
                DV.wait(e)
                e = DV.did(nc.vector.scalar_tensor_tensor(acc_[n][:, :], conv[n][:, 0:S], param("conv_w", j), acc_[n][:, :],
                                                          ALU.mult, ALU.add))
                AC.wait(e)
                e = AC.did(nc.scalar.activation(th[n][:, :], acc_[n][:, :], ACT.Tanh, scale=0.5))
                DV.wait(e)
                e = DV.did(nc.vector.scalar_tensor_tensor(th[n][:, :], th[n][:, :], 1.0, acc_[n][:, :], ALU.add, ALU.mult))
                DV.wait(e, mvv)
                e = DV.did(nc.vector.scalar_tensor_tensor(th[n][:, :], th[n][:, :], 0.5, bank[:, bg + 1, :], ALU.mult, ALU.mult))
                dense.free(ig, e)
                a, z = split_into(G_hi[:, jj, 0:S], G_lo[:, jj, 0:S], th[n][:, :], e, *(x_done if jj == 0 and half else ()))
                cv_s.free(ni, a, z)
                g_ready += [a, z]
            PE.wait(*g_ready)
            x_done = add_residual(Gs, KT, S, 4)
            AC.wait(PE.last)
            DV.wait(PE.last)

        stage("ple")
        fence()
        c = R
        p_rows, c = place("p_rows", [P, TT, PLE], F32, c)
        gate, c = place("ple_gate", [P, 2, S], F32, c)
        p_in = small(p_rows[:, :, :], A["p"].rearrange("(t q) d -> q t d", q=P))
        rms_norm_split("ple", S, *x_done)
        PE.wait(p_in)
        for k in range(2):
            b, i = dense.take(PE)
            for t in range(TT):
                ins = nc.tensor.transpose(bank[:, b, t * P:(t + 1) * P], p_rows[:, t, k * P:(k + 1) * P], ident[:, :])
            m = PE.did(ins)
            a, z = split_into(G_hi[:, k, 0:S], G_lo[:, k, 0:S], bank[:, b, :], m)
            dense.free(i, a, z)
            PE.wait(a, z)
        gfree = [(), ()]
        for q in range(4):
            hi, lo, u = weights()
            gm = []
            for j in range(2):
                b, i = dense.take(PE)
                m = to_features(Hs, KT, (hi, lo), columns(j * P), S, b)
                if j:
                    weights_done(u, m)
                AC.wait(m, *gfree[j])
                e = AC.did(nc.scalar.activation(gate[:, j, :], bank[:, b, :], ACT.Tanh, scale=0.5))
                dense.free(i, e)
                gm.append(e)
            hi, lo, u = weights()
            for j in range(2):
                k = 2 * q + j
                b, i = dense.take(PE)
                m = to_features(Gs, 2, (hi, lo), columns(j * P), S, b)
                if j:
                    weights_done(u, m)
                DV.wait(gm[j], m)
                e = DV.did(nc.vector.scalar_tensor_tensor(gate[:, j, :], gate[:, j, :], 1.0, bank[:, b, :], ALU.add, ALU.mult))
                dense.free(i, e)
                DV.wait(e)
                e = DV.did(nc.vector.scalar_tensor_tensor(X[:, k, 0:S], gate[:, j, :], 0.5, X[:, k, 0:S], ALU.mult, ALU.add))
                gfree[j] = (e,)
        x_done = [e]

        stage("between")
        fence()
        c = R
        Y, c = place("y_rows", [P, 2, S], F32, c)
        meta, c = place("meta_rows", [META, D], F32, c)
        meta_in = small(meta[:, :], A["meta"][:, :])
        m = mean_square(lambda k: X[:, k, 0:S], S, KT, 4, *x_done)
        r = root_reciprocal(rstd[:, 0:S], bank[:, 4, :], 1.0 / D, m)
        yfree = [(), ()]
        marks = []
        for k in range(KT):
            DV.wait(r, *yfree[k % 2])
            e = DV.did(nc.vector.scalar_tensor_tensor(Y[:, k % 2, :], X[:, k, 0:S], param("fin1", k), rstd[:, 0:S], ALU.mult, ALU.mult))
            AC.wait(e)
            e = AC.did(nc.scalar.activation(X[:, k, 0:S].rearrange("p (c r) -> p r c", r=ROWS),
                                            Y[:, k % 2, :].rearrange("p (r c) -> p r c", r=ROWS), ACT.Copy))
            yfree[k % 2] = (e,)
            marks.append(e)
        PE.wait(meta_in)
        b, i = dense.take(PE)
        for k in range(KT):
            ins = nc.tensor.transpose(bank[:, b, k * META:(k + 1) * META], meta[:, k * P:(k + 1) * P], ident[0:META, 0:META])
        m = PE.did(ins)
        AC.wait(m)
        e = AC.did(nc.scalar.activation(X[:, :, S:T2], bank[:, b, 0:KT * META].rearrange("p (k m) -> p k m", k=KT), ACT.Copy))
        dense.free(i, e)
        marks.append(e)
        x_done = marks

        Os = None
        for layer in range(2):
            L = "ab"[layer]
            last = layer == 1
            nq = TT if last else TT + 1
            n_out = S if last else T2
            stage(f"qkv_{L}")
            fence()
            c = R
            ob_hi, g_c = place(f"ob_hi_{L}", [P, 4, T2], F32R, g_at)
            ob_lo, g_c = place(f"ob_lo_{L}", [P, 4, T2], F32R, g_c)
            oa_hi, g_c = place(f"oa_hi_{L}", [P, 4, T2], F32R, g_c)
            oa_lo, g_c = place(f"oa_lo_{L}", [P, 4, T2], F32R, g_c)
            qT, c = place(f"q_{L}", [P, 4, T2], F32, c)
            kT, c = place(f"k_{L}", [P, 4, T2], F32, c)
            vr, c = place(f"v_{L}", [P, 5, 512], F32, c)
            orow, c = place(f"o_rows_{L}", [P, 5, 512], F32, c)
            tail = c
            cos, c = place(f"cos_{L}", [P, T2], F32, c)
            sin, c = place(f"sin_{L}", [P, T2], F32, c)
            rot, c = place(f"rot_{L}", [P, P], F32, c)
            same, c = place(f"same_{L}", [P, P], F32, c)
            assert c <= R_END, (c, R_END)
            table("cos", cos[:, :])
            table("sin", sin[:, :])
            table("rot", rot[:, :])
            rope_in = table("same", same[:, :])
            rms_norm_split(f"norm_{L}", T2, *x_done)

            def rope(dst, cols, scale, gain, wv):
                b, i = dense.take(PE)
                m = to_features(Hs, KT, wv, cols, T2, b)
                fv = feature_view(b, T2)
                AC.wait(m, *rope_free[0])
                e1 = AC.did(nc.scalar.activation(dest(sq[0][:, :], T2), fv, ACT.Square))
                e2 = AC.did(nc.scalar.activation(dest(tmp[:, :], T2), fv, ACT.Copy, scale=param(gain)))
                dense.free(i, e2)
                PE.wait(e1, e2, rope_in)
                for n, (a, z) in enumerate(chunks(T2)):
                    nc.tensor.matmul(bank[:, 4 + n, 0:HALF], same[:, :], sq[0][:, a:z], start=True, stop=True)
                for n, (a, z) in enumerate(chunks(T2)):
                    ins = nc.tensor.matmul(bank[:, 6 + n, 0:HALF], rot[:, :], tmp[:, a:z], start=True, stop=True)
                m2 = PE.did(ins)
                r = root_reciprocal(dest(rstd[:, :], T2), bank[:, 4:6, 0:HALF], 1.0 / AD, m2)
                DV.wait(e2, rope_in)
                t1 = DV.did(nc.vector.tensor_tensor(dst, tmp[:, :], cos[:, :], ALU.mult))
                DV.wait(m2)
                t2 = DV.did(nc.vector.tensor_tensor(dest(sq[1][:, :], T2), bank[:, 6:8, 0:HALF], dest(sin[:, :], T2), ALU.mult))
                DV.wait(t2, t1)
                t1 = DV.did(nc.vector.tensor_tensor(dst, dst, sq[1][:, :], ALU.add))
                DV.wait(t1, r)
                t1 = DV.did(nc.vector.scalar_tensor_tensor(dst, dst, scale, rstd[:, :], ALU.mult, ALU.mult))
                rope_free[0] = (t1,)
                PE.wait(t1)
                return m

            rope_free = [()]
            for a in range(2):
                hi, lo, u = weights()
                for j in range(2):
                    m = rope(qT[:, 2 * a + j, :], columns(j * P), AD ** -0.5, f"qg_{L}", (hi, lo))
                weights_done(u, m)
            hi, lo, u = weights()
            rope(kT[:, 0, :], columns(0), 1.0, f"kg_{L}", (hi, lo))
            tiles2 = [(t * P, P) for t in range(TT)] + [(S, META)]
            for t, (t0, tn) in enumerate(tiles2):
                b, i = dense.take(PE)
                m = to_tokens(Hs, t0, tn, (hi, lo), P, P, bank[0:tn, b, 0:P])
                if t == TT:
                    weights_done(u, m)
                e = evacuate(vr[0:tn, t, 0:P], bank[0:tn, b, 0:P], m, None, DV if t % 2 else AC)
                dense.free(i, e)
                PE.wait(e)

            stage(f"gqa_{L}")
            fence()
            c = tail
            pr_s, pt_s = [None, None], [None, None]
            for n in range(2):
                pr_s[n], c = place(f"gqa_probs{n}_{L}", [P, T2], F32, c)
                pt_s[n], c = place(f"gqa_probsT{n}_{L}", [P, 5, P], F32, c)
            stat, c = place(f"gqa_stats_{L}", [P, 4, AH], F32, c)
            assert c <= R_END, (c, R_END)
            pr, pt = Slots(pr_s), Slots(pt_s)
            scores, turned, outb = Slots([2, 4]), Slots([6]), Slots([7, 0])
            order = [0, 4, 1, 5, 2, 6, 3, 7]
            ov = ()
            for t in range(nq):
                q0, qn = tiles2[t]
                ob, oi = outb.take(PE)
                prev_o = ov

                def score(h):
                    b, i = scores.take(PE)
                    for n, (a, z) in enumerate(chunks(T2)):
                        ins = nc.tensor.matmul(bank[0:qn, b + n, 0:HALF], qT[qk_rows(h), h % 4, q0:q0 + qn],
                                               kT[qk_rows(h), 0, a:z], start=True, stop=True)
                    m = PE.did(ins)
                    DV.wait(m, *prev_o)
                    e = DV.did(nc.vector.tensor_reduce(stat[0:qn, 0, h:h + 1], bank[0:qn, b:b + 2, 0:HALF], AX.XY, ALU.max, negate=True))
                    p_, pi = pr.take(AC)
                    AC.wait(e, m)
                    e = AC.did(nc.scalar.activation(dest(p_[0:qn, :], T2), bank[0:qn, b:b + 2, 0:HALF], ACT.Exp,
                                                    bias=stat[0:qn, 0, h:h + 1], accum_out=stat[0:qn, 1, h:h + 1]))
                    scores.free(i, e)
                    return p_, pi, e

                def value(h, p_, pi, ready):
                    b, i = turned.take(PE)
                    PE.wait(ready)
                    for k in range(TT):
                        ins = nc.tensor.transpose(bank[:, b, k * P:k * P + qn], p_[0:qn, k * P:(k + 1) * P], ident[0:qn, 0:qn])
                    m = PE.did(ins)
                    q_, qi = pt.take(DV, AC)
                    m1 = evacuate(q_[:, 0:TT, 0:qn], bank[:, b, :].rearrange("p (k q) -> p k q", k=TT)[:, :, 0:qn], m, None, DV)
                    PE.wait(m1)
                    m = PE.did(nc.tensor.transpose(bank[0:META, b, 0:qn], p_[0:qn, S:T2], ident[0:qn, 0:qn]))
                    pr.free(pi, m)
                    m2 = evacuate(q_[0:META, TT, 0:qn], bank[0:META, b, 0:qn], m)
                    turned.free(i, m2)
                    for k in range(TT + 1):
                        if k == TT:
                            PE.wait(m2)
                        kn = tiles2[k][1]
                        ins = nc.tensor.matmul(bank[0:qn, ob, h * AD:(h + 1) * AD], q_[0:kn, k, 0:qn],
                                               vr[0:kn, k, (h // 4) * AD:(h // 4 + 1) * AD], start=k == 0, stop=k == TT)
                    m = PE.did(ins)
                    pt.free(qi, m)
                    return m

                ahead = score(order[0])
                for n_, h in enumerate(order):
                    now = ahead
                    if n_ + 1 < AH:
                        ahead = score(order[n_ + 1])
                    m = value(h, *now)
                DV.wait(now[2])
                e = DV.did(nc.vector.reciprocal(stat[0:qn, 2, :], stat[0:qn, 1, :]))
                DV.wait(e, m)
                e = DV.did(nc.vector.tensor_tensor(orow[0:qn, t, :].rearrange("p (h d) -> p h d", h=AH),
                                                   bank[0:qn, ob, :].rearrange("p (h d) -> p h d", h=AH),
                                                   stat[0:qn, 2, :].unsqueeze(2).broadcast_to([qn, AH, AD]), ALU.mult))
                outb.free(oi, e)
                ov = (e,)
                AC.wait(e)

            def gated_features(hi_dst, lo_dst, zname):
                stage(f"{zname}_{L}")
                fence()
                c = tail
                zt, c = place(f"{zname}_t_{L}", [P, 2, T2], F32, c)
                assert c <= R_END, (c, R_END)
                zfree = [(), ()]
                for uu in range(2):
                    hi, lo, u = weights()
                    for j in range(2):
                        k = 2 * uu + j
                        b, i = dense.take(PE)
                        mz = to_features(Hs, KT, (hi, lo), columns(j * P), n_out, b)
                        if j:
                            weights_done(u, mz)
                        zs = dest(zt[:, k % 2, 0:n_out], n_out)
                        AC.wait(mz, *zfree[k % 2])
                        e = AC.did(nc.scalar.activation(zs, feature_view(b, n_out), ACT.Tanh, scale=0.5))
                        DV.wait(e, mz)
                        e = DV.did(nc.vector.scalar_tensor_tensor(zs, zs, 1.0, feature_view(b, n_out), ALU.add, ALU.mult))
                        dense.free(i, e)
                        b2 = 4 + 2 * (k % 2)
                        PE.wait(*zfree[k % 2])
                        for t in range(nq):
                            t0, tn = tiles2[t]
                            for a, z in ((0, HALF), (HALF, T2)) if n_out > 512 else ((0, 512),):
                                lo_t, hi_t = max(t0, a), min(t0 + tn, z)
                                if lo_t < hi_t:
                                    r0, r1 = lo_t - t0, hi_t - t0
                                    bk = b2 + (1 if a else 0)
                                    ins = nc.tensor.matmul(bank[:, bk, lo_t - a:hi_t - a], orow[0:tn, t, k * P:(k + 1) * P],
                                                           ident[0:tn, r0:r1], start=True, stop=True, is_transpose=True) if r1 - r0 == tn else \
                                        nc.tensor.matmul(bank[:, bk, lo_t - a:hi_t - a], orow[0:tn, t, k * P:(k + 1) * P],
                                                         ident[0:tn, r0:r1], start=True, stop=True)
                        m = PE.did(ins)
                        DV.wait(e, m)
                        e = DV.did(nc.vector.scalar_tensor_tensor(zs, zs, 0.5, feature_view(b2, n_out), ALU.mult, ALU.mult))
                        a_, z_ = split_into(hi_dst[:, k, 0:n_out], lo_dst[:, k, 0:n_out], zt[:, k % 2, 0:n_out], e)
                        zfree[k % 2] = (e, a_, z_)
                        PE.wait(a_, z_)

            gated_features(oa_hi, oa_lo, "za")

            stage(f"na_in_{L}")
            fence()
            marks = []
            for a in range(2):
                marks += project_features([qT[:, 2 * a + j, :] for j in range(2)], T2, scale=AD ** -0.5)
            for a in range(2):
                marks += project_features([kT[:, 2 * a + j, :] for j in range(2)], T2)
            shifted = [(0, 64)] + [(64 + P * t, P) for t in range(3)] + [(S - 64, 64 + META)]
            for a in range(2):
                marks += project_tokens(lambda r, t: (vr[0:shifted[t][1], t, 256 * a:256 * a + 256], lambda x: x), shifted)
            PE.wait(*marks)
            DV.wait(*marks)
            stage(f"na_{L}")
            fence()
            c = tail
            bias, c = place(f"na_bias_{L}", [P, 2, 2 * P], F32, c)
            mask, c = place(f"na_mask_{L}", [P, 2 * P], F32, c)
            maskb, c = place(f"na_mask16_{L}", [P, 3, 2 * P], BF16, c)
            idb, c = place(f"ident16_{L}", [P, P], BF16, c)
            KN = 2 * P + META
            pr_s, sc_s, pt_s = [None] * 2, [None] * 2, [None] * 2
            for n in range(2):
                sc_s[n], c = place(f"na_scores{n}_{L}", [P, KN], F32, c)
                pr_s[n], c = place(f"na_probs{n}_{L}", [P, KN], F32, c)
                pt_s[n], c = place(f"na_probsT{n}_{L}", [P, 3, P], F32, c)
            nstat, c = place(f"na_stats_{L}", [P, 5, 3, AH], F32, c)
            assert c <= R_END, (c, R_END)
            mcopy = AC.did(nc.scalar.activation(idb[:, :], ident[:, :], ACT.Copy))
            for n, name in enumerate(("na_first", "na_inner", "na_last")):
                SP.wait(mcopy)
                m = table(name, mask[:, :])
                AC.wait(m)
                mcopy = AC.did(nc.scalar.activation(maskb[:, n, :], mask[:, :], ACT.Copy))
            PE.wait(mcopy)
            pr, pt, sc = Slots(pr_s), Slots(pt_s), Slots(sc_s)
            scores, turned = Slots([4, 5]), Slots([6, 7])
            outb = Slots([0, 1, 2, 3])
            brel = A["na_rel"]
            bias_sem = [new_sem(f"na_bias_in{n}_{L}") for n in range(2)]
            bias_n = [0, 0]
            bias_free = [(), ()]
            for h in range(AH):
                hb = h % 2
                SP.wait(*bias_free[hb])
                for cc in range(QB):
                    off = (NAW - 1 - cc) * ROWS
                    nc.sync.dma_start(bias[cc * ROWS:(cc + 1) * ROWS, hb, :],
                                      brel[layer, h, :, off:off + 2 * P]).then_inc(bias_sem[hb], 16)
                    bias_n[hb] += 16
                b_in = (bias_sem[hb], bias_n[hb])
                rows = slice(AD * (h % 2), AD * (h % 2) + AD)
                qh, kh = qT[rows, h // 2, :], kT[rows, h // 2, :]

                def na_score(t):
                    q0, qn = tiles2[t]
                    b, i = scores.take(PE)
                    if t < TT:
                        k0, kn = max(0, P * t - 64), min(S, P * t + 192) - max(0, P * t - 64)
                        m0 = 64 if t == 0 else 0
                        which = 0 if t == 0 else 2 if t == TT - 1 else 1
                        nc.tensor.matmul(bank[:, b, 0:kn], idb[:, :], maskb[:, which, m0:m0 + kn], start=True, stop=False,
                                         skip_group_check=True)
                        nc.tensor.matmul(bank[:, b, 0:kn], qh[:, q0:q0 + qn], kh[:, k0:k0 + kn], start=False, stop=True,
                                         skip_group_check=True)
                    else:
                        kn, m0 = 0, 0
                    m = PE.did(nc.tensor.matmul(bank[0:qn, b, kn:kn + META], qh[:, q0:q0 + qn], kh[:, S:T2], start=t == TT,
                                                stop=True, skip_group_check=True))
                    n = kn + META
                    s_, si = sc.take(DV)
                    DV.wait(m)
                    if kn:
                        DV.wait(b_in)
                        eb = DV.did(nc.vector.tensor_tensor(s_[:, 0:kn], bank[:, b, 0:kn], bias[:, hb, m0:m0 + kn], ALU.add))
                        bias_free[hb] = (eb,)
                    e = DV.did(nc.vector.tensor_copy(s_[0:qn, kn:n], bank[0:qn, b, kn:n]))
                    scores.free(i, e)
                    DV.wait(e)
                    e = DV.did(nc.vector.reduce_max(nstat[0:qn, t, 0, h:h + 1], s_[0:qn, 0:n], AX.X, negate=True))
                    p_, pi = pr.take(AC)
                    AC.wait(e)
                    e = AC.did(nc.scalar.activation(p_[0:qn, 0:n], s_[0:qn, 0:n], ACT.Exp, bias=nstat[0:qn, t, 0, h:h + 1],
                                                    accum_out=nstat[0:qn, t, 1, h:h + 1]))
                    sc.free(si, e)
                    return p_, pi, e, kn

                def na_value(t, p_, pi, ready, kn):
                    q0, qn = tiles2[t]
                    parts = {0: [(0, 64, 0, 0), (64, P, 1, 0), None],
                             1: [(0, P, 1, 0), (P, P, 2, 0), None],
                             2: [(0, P, 2, 0), (P, P, 3, 0), None],
                             3: [(0, P, 3, 0), (P, 64 + META, 4, 0)],
                             4: [None]}[t]
                    b, i = turned.take(PE)
                    PE.wait(ready)
                    jobs = []
                    for n, part in enumerate(parts):
                        if part is None:
                            if t == 4:
                                ins = nc.tensor.transpose(bank[0:META, b, n * P:n * P + qn], p_[0:qn, 0:META], ident[0:qn, 0:qn])
                                jobs.append((n, 0, META, 4, True))
                            else:
                                ins = nc.tensor.transpose(bank[0:64 + META, b, n * P:(n + 1) * P], p_[:, kn - 64:kn + META], ident[:, :])
                                jobs.append((n, 64, META, 4, False))
                        else:
                            p0, pn, vt, _ = part
                            ins = nc.tensor.transpose(bank[0:pn, b, n * P:(n + 1) * P], p_[:, p0:p0 + pn], ident[:, :])
                            jobs.append((n, 0, pn, vt, False))
                    m = PE.did(ins)
                    pr.free(pi, m)
                    q_, qi = pt.take(AC, DV)
                    for n, r0, rn, _, _ in jobs:
                        m2 = evacuate(q_[r0:r0 + rn, n, 0:qn], bank[r0:r0 + rn, b, n * P:n * P + qn], m, None, AC)
                    turned.free(i, m2)
                    PE.wait(m2)
                    ob, oi = outb.take(PE)
                    for j, (n, r0, rn, vt, own) in enumerate(jobs):
                        v = vm[0:META, h * AD:(h + 1) * AD] if own else vr[r0:r0 + rn, vt, h * AD:(h + 1) * AD]
                        ins = nc.tensor.matmul(bank[0:qn, ob, 0:AD], q_[r0:r0 + rn, n, 0:qn], v, start=j == 0, stop=j == len(jobs) - 1)
                    m = PE.did(ins)
                    pt.free(qi, m)
                    DV.wait(m, ready)
                    e = DV.did(nc.vector.reciprocal(nstat[0:qn, t, 2, h:h + 1], nstat[0:qn, t, 1, h:h + 1]))
                    DV.wait(e)
                    e = DV.did(nc.vector.tensor_scalar(orow[0:qn, t, h * AD:(h + 1) * AD], bank[0:qn, ob, 0:AD],
                                                       nstat[0:qn, t, 2, h:h + 1], None, ALU.mult))
                    outb.free(oi, e)
                    return e

                if h == 0 and not last:
                    vm, c = place(f"v_meta_{L}", [META, 512], F32, c)
                    assert c <= R_END
                    vm_in = new_sem(f"v_meta_in_{L}")
                    SP.wait(*marks)
                    nc.sync.dma_start(vm[:, :], vr[64:64 + META, 4, :]).then_inc(vm_in, 16)
                    PE.wait((vm_in, 16))
                elif last:
                    vm = None
                ahead = na_score(0)
                for t in range(nq):
                    now = ahead
                    if t + 1 < nq:
                        ahead = na_score(t + 1)
                    na_value(t, *now)
            gated_features(ob_hi, ob_lo, "zb")

            stage(f"mixed_{L}")
            fence()
            c = R
            mixt, c = place(f"mixed_{L}", [P, KT, T2], F32, c)
            sg, c = place(f"gates_{L}", [P, 4, T2], F32, c)
            assert c <= R_END
            sfree = [()] * 4
            part_mark = [None, None]
            for q in range(4):
                for which, act in ((0, (oa_hi, oa_lo)), (1, (ob_hi, ob_lo))):
                    hi, lo, u = weights()
                    gm = []
                    for j in range(2):
                        b, i = dense.take(PE)
                        m = to_features(Hs, KT, (hi, lo), columns(j * P), n_out, b)
                        if j:
                            weights_done(u, m)
                        sl = 2 * which + j
                        AC.wait(m, *sfree[sl])
                        e = AC.did(nc.scalar.activation(dest(sg[:, sl, 0:n_out], n_out), feature_view(b, n_out), ACT.Tanh, scale=0.5))
                        dense.free(i, e)
                        gm.append(e)
                    hi, lo, u = weights()
                    for j in range(2):
                        k = 2 * q + j
                        sl = 2 * which + j
                        b, i = dense.take(PE)
                        m = to_features(act, 4, (hi, lo), columns(j * P), n_out, b)
                        if j:
                            weights_done(u, m)
                        gs = dest(sg[:, sl, 0:n_out], n_out)
                        DV.wait(gm[j], m)
                        e = DV.did(nc.vector.scalar_tensor_tensor(gs, gs, 1.0, feature_view(b, n_out), ALU.add, ALU.mult))
                        dense.free(i, e)
                        DV.wait(e)
                        if which == 0:
                            part_mark[j] = DV.did(nc.vector.tensor_scalar(mixt[:, k, 0:n_out], sg[:, sl, 0:n_out], 0.5, None, ALU.mult))
                            sfree[sl] = (part_mark[j],)
                        else:
                            DV.wait(part_mark[j])
                            e = DV.did(nc.vector.scalar_tensor_tensor(mixt[:, k, 0:n_out], sg[:, sl, 0:n_out], 0.5,
                                                                      mixt[:, k, 0:n_out], ALU.mult, ALU.add))
                            sfree[sl] = (e,)
            AC.wait(PE.last)
            DV.wait(PE.last, e)
            for k in range(KT):
                a_, z_ = split_into(H_hi[:, k, 0:n_out], H_lo[:, k, 0:n_out], mixt[:, k, 0:n_out], e)
                PE.wait(a_, z_)
            x_done = add_residual(Hs, KT, n_out, 4)

        stage("out")
        fence()
        c = R
        Y2, c = place("y2", [P, 2, S], F32, c)
        rows_out, c = place("rows_out", [P, TT, D], F32, c)
        m = mean_square(lambda k: X[:, k, 0:S], S, KT, 4, *x_done)
        r = root_reciprocal(rstd[:, 0:S], bank[:, 4, :], 1.0 / D, m)
        yfree = [(), ()]
        turn = Slots([0, 1, 2, 3])
        for k in range(KT):
            DV.wait(r, *yfree[k % 2])
            e = DV.did(nc.vector.scalar_tensor_tensor(Y2[:, k % 2, :], X[:, k, 0:S], param("fin2", k), rstd[:, 0:S], ALU.mult, ALU.mult))
            b, i = turn.take(PE)
            PE.wait(e)
            for t in range(TT):
                ins = nc.tensor.transpose(bank[:, b, t * P:(t + 1) * P], Y2[:, k % 2, t * P:(t + 1) * P], ident[:, :])
            m = PE.did(ins)
            yfree[k % 2] = (m,)
            e = evacuate(rows_out[:, :, k * P:(k + 1) * P], bank[:, b, :].rearrange("p (t f) -> p t f", t=TT), m)
            turn.free(i, e)
        out_sem = new_sem("out_written")
        SP.wait(e)
        n = 0
        out_v = A["out"].rearrange("(r c) d -> c r d", r=ROWS)
        for t in range(TT):
            for cc in range(QB):
                nc.sync.dma_start(out_v[t * QB + cc, :, :], rows_out[cc * ROWS:(cc + 1) * ROWS, t, :]).then_inc(out_sem, 16)
                n += 16
        nc.sync.wait_ge(out_sem, n)


def bass_windows(src):
    ap = src.ap if not callable(src.ap) else src.ap()
    part = list(ap)[0]
    return bass.AP(tensor=src.tensor, offset=src.offset, ap=[part, [1, CB], [CS, NC]])


def kernel(**inputs):
    import numpy as _np
    import concourse.bacc as _bacc
    from concourse import mybir as _mybir
    from concourse.bass_utils import run_bass_kernel_spmd as _run

    f = {k: _np.asarray(v) for k, v in inputs.items()}

    def by_feature(v):
        return _np.reshape(v, (-1, 128)).T

    def twice(v):
        return _np.concatenate([v, v], axis=0)

    gate_b = _np.zeros((128, 2), _np.float32)
    gate_b[0:4, 0] = f["mlstm_gate_bias"][0, 0:4]
    gate_b[0:4, 1] = f["mlstm_gate_bias"][0, 4:8]
    cols = {
        "ln1": by_feature(f["ln1_g"]), "ln2": by_feature(f["ln2_g"]), "ple": by_feature(f["ple_norm_g"]),
        "fin1": by_feature(f["final_g"]), "conv_w": by_feature(f["conv_w"]), "conv_b": by_feature(f["conv_b"]),
        "mnorm": by_feature(f["mlstm_norm_g"]), "pe_k": twice(f["cmp_pos_k"][0].T), "pe_v": twice(f["cmp_pos_v"][0].T),
        "gate_b": gate_b, "norm_a": by_feature(f["norm_g_2"][0]), "norm_b": by_feature(f["norm_g_2"][1]),
        "fin2": by_feature(f["final_norm_g_2"]),
        "qg_a": twice(f["q_norm_g_2"][0][:, None]), "qg_b": twice(f["q_norm_g_2"][1][:, None]),
        "kg_a": twice(f["k_norm_g_2"][0][:, None]), "kg_b": twice(f["k_norm_g_2"][1][:, None]),
    }
    params = _np.ascontiguousarray(_np.concatenate([cols[n] for n, _ in PARAMS], axis=1))
    rpb = f["na_rpb_2"]
    rel = _np.zeros((2, 8, 8, DCP, 8), _np.float32)
    for r in range(8):
        rel[:, :, r, 8:8 + 31, :] = rpb[:, :, 7 - r:15 - r, :].transpose(0, 1, 3, 2)
    tables = constants()
    const_at, _ = offsets([(k, v.shape[1]) for k, v in tables.items()])
    consts = _np.ascontiguousarray(_np.concatenate(list(tables.values()), axis=1))
    arrays = {
        "x": f["x"][0], "p": f["p"][0, 0], "params": params, "consts": consts,
        "na_rel": rel.reshape(2, 8, 8, DCP * 8), "meta": f["meta_tokens_2"],
        "w_in": f["w_in"][0], "cmp_k_w1": f["cmp_k_w1"][0], "cmp_k_w2": f["cmp_k_w2"][0],
        "cmp_v_w1": f["cmp_v_w1"][0], "cmp_v_w2": f["cmp_v_w2"][0], "w_out": f["w_out"][0], "w_up": f["w_up"][0],
        "w_down": f["w_down"][0], "w_ple_gate": f["w_ple_gate"][0], "w_ple_proj": f["w_ple_proj"][0],
        "w_in_2": f["w_in_2"], "w_o_attn_2": f["w_o_attn_2"], "w_o_na_2": f["w_o_na_2"], "w_out_2": f["w_out_2"],
    }
    arrays = {k: _np.ascontiguousarray(v) for k, v in arrays.items()}
    nc = _bacc.Bacc("TRN2", target_bir_lowering=False, num_devices=1)
    A = {k: nc.dram_tensor(k, v.shape, _mybir.dt.float32, kind="ExternalInput").ap() for k, v in arrays.items()}
    A["const_at"] = const_at
    A["out"] = nc.dram_tensor("out", (S, D), _mybir.dt.float32, kind="ExternalOutput").ap()
    program(nc, A)
    r = _run(nc, [arrays], core_ids=[0])
    return r.results[0]["out"].reshape(1, S, D)
```

```python
import math
from contextlib import ExitStack

import concourse.bass as bass
import numpy as np
from concourse import mybir

F32, F32R, BF16 = mybir.dt.float32, mybir.dt.float32r, mybir.dt.bfloat16
ALU, ACT, AX = mybir.AluOpType, mybir.ActivationFunctionType, mybir.AxisListType

P = 128
S, D = 512, 1024
KT, TT = D // P, S // P
EPS, NEG = 1e-6, -1e30
PLE, FF = 256, 2048
MH, MD = 4, 128
AH, AG, AD = 8, 2, 64
NH = 8
CB, CS, CH = 32, 16, 128
NC = (S - CB) // CS + 1
MW, AW, KW = MH * MD, AH * AD, AG * AD
Z_MQ, Z_MK, Z_MV, Z_MO = 0, MW, 2 * MW, 3 * MW
Z_MI = 4 * MW
Z_AQ = Z_MI + 2 * MH
Z_KC = Z_AQ + AW
Z_VC, Z_KS, Z_VS, Z_KX, Z_VX = (Z_KC + i * KW for i in range(1, 6))
Z_AG = Z_KC + 6 * KW
META = 16
T2 = S + META
HALF = T2 // 2
GW, ROWS = 64, S // 64
NAW = 16
QB = P // ROWS
C_QA, C_KA, C_VA, C_ZA = 0, 512, 640, 768
C_QB, C_KB, C_VB, C_ZB, C_GA, C_GB = 1280, 1792, 2304, 2816, 3328, 4352
DCP = 2 * NAW - 1 + 16


def constants():
    q = np.arange(P)
    out = {"ident": np.eye(P)}
    dist = (S - P) + q[:, None] - np.arange(S)[None, :]
    out["ndist"] = np.where(dist >= 0, -dist, NEG)
    head = (q[:, None] // AD) * (AH // AG) + np.arange(AH // AG)[None, :]
    out["qscale"] = AD ** -0.5 * 2.0 ** (head + 1.0)
    out["later"] = np.where(q[None, :] >= q[:, None], 0.0, NEG)
    t = (np.arange(TT)[None, :] * P + q[:, None])[:, :, None, None]
    end = np.arange(32)[None, None, None, :] * CS + CB - 1
    slope = (2.0 ** -(np.arange(AH) + 1.0))[None, None, :, None]
    ok = (end <= t) & (np.arange(32) < NC)
    out["cbias"] = np.where(ok, -slope * (t - end), NEG) + 0 * slope
    out["cvalid"] = (ok + 0 * end)[:, :, 0, :]
    out["hsel"] = (q[:, None] // AD == np.arange(2)[None, :])
    blk = q[:, None] // META
    out["own_pair"] = (blk % 2 * 4 + blk // 2 == np.arange(AH)[None, :])
    out["own_head"] = (blk == np.arange(AH)[None, :])
    out["spread"] = ((q[:, None] % 64 == q[None, :] % META) & (q[:, None] % 64 < META))
    rot = np.zeros((P, P))
    for h in range(2):
        for a in range(2):
            for i in range(16):
                lo, hi = h * 64 + a * 32 + i, h * 64 + a * 32 + 16 + i
                rot[hi, lo] = -1.0
                rot[lo, hi] = 1.0
    out["rot"] = rot
    inv = (np.float32(10000.0) ** (-np.arange(0, 32, 2, dtype=np.float32) / np.float32(32))).astype(np.float32)
    n = np.arange(S)
    row = np.concatenate([n % ROWS, np.zeros(META, int)]).astype(np.float32)
    col = np.concatenate([n // ROWS, np.zeros(META, int)]).astype(np.float32)
    ang = np.concatenate([row[None] * inv[:, None]] * 2 + [col[None] * inv[:, None]] * 2)
    out["cos"] = np.tile(np.cos(ang), (2, 1))
    out["sin"] = np.tile(np.sin(ang), (2, 1))
    cc, jj = (q // ROWS)[:, None], (np.arange(2 * P) // ROWS)[None, :]
    for name, b in (("na_first", 0), ("na_inner", 1), ("na_last", GW // QB - 1)):
        c, j = QB * b + cc, QB * b - 8 + jj
        start = np.clip(c - NAW // 2, 0, GW - NAW)
        out[name] = np.where((j >= start) & (j < start + NAW), 0.0, NEG)
    sel = np.zeros((P, MH, P))
    for h in range(MH):
        sel[h, h] = 1.0
    out["pick"] = sel
    return {k: np.asarray(v, np.float32).reshape(P, -1) for k, v in out.items()}


PARAMS = [("ln1", 8), ("ln2", 8), ("ple", 8), ("fin1", 8), ("conv_w", 48), ("conv_b", 16), ("mnorm", 4),
          ("pe_k", 32), ("pe_v", 32), ("gate_b", 2), ("norm_a", 8), ("norm_b", 8), ("fin2", 8),
          ("qg_a", 1), ("qg_b", 1), ("kg_a", 1), ("kg_b", 1)]


def offsets(pairs):
    at, out = 0, {}
    for name, n in pairs:
        out[name] = (at, n)
        at += n
    return out, at


class Lane:

    def __init__(self, new_sem, engine, name):
        self.new_sem, self.engine, self.name = new_sem, engine, name
        self.seen = {}
        self.last = None
        self.stage("start")

    def stage(self, stage):
        self.sem, self.count = self.new_sem(f"{self.name}_{stage}"), 0

    def did(self, instruction):
        instruction.then_inc(self.sem, 1)
        self.count += 1
        self.last = (self.sem, self.count)
        return self.last

    def wait(self, *marks):
        for mark in marks:
            if mark is not None and self.seen.get(mark[0].name, 0) < mark[1]:
                self.engine.wait_ge(*mark)
                self.seen[mark[0].name] = mark[1]


class Slots:

    def __init__(self, buffers):
        self.buffers, self.free_at, self.n = buffers, [() for _ in buffers], 0

    def take(self, *lanes):
        i = self.n % len(self.buffers)
        self.n += 1
        assert self.free_at[i] is not None, "the slot is still in use"
        for lane in lanes:
            lane.wait(*self.free_at[i])
        self.free_at[i] = None
        return self.buffers[i], i

    def free(self, i, *marks):
        self.free_at[i] = marks


def program(nc, A):
    ctx = ExitStack()
    sems = {}

    def new_sem(name):
        sems[name] = ctx.enter_context(nc.semaphore(name))
        return sems[name]

    with ctx:
        PE, AC, DV, PO, SP = (Lane(new_sem, e, n) for e, n in (
            (nc.tensor, "pe"), (nc.scalar, "act"), (nc.vector, "dve"), (nc.gpsimd, "pool"), (nc.sync, "sp")))
        compute = (PE, AC, DV, PO)

        def stage(name):
            for lane in compute:
                lane.stage(name)

        def fence():
            lasts = [lane.last for lane in compute]
            for lane in (*compute, SP):
                lane.wait(*lasts)

        cursor = [nc.sbuf_base + (-nc.sbuf_base) % 64]

        def region(size):
            at = cursor[0]
            cursor[0] += size + (-size) % 64
            assert cursor[0] <= nc.sbuf_usable_end, (cursor[0], nc.sbuf_usable_end)
            return at

        def place(name, shape, dt, at):
            t = nc.alloc_sbuf_tensor_at(name, shape, dt, offset=at)
            n = 2 if dt == BF16 else 4
            return t, at + n * math.prod(shape[1:]) + (-n * math.prod(shape[1:])) % 64

        def fixed(name, shape, dt=F32):
            at = region((2 if dt == BF16 else 4) * math.prod(shape[1:]))
            return place(name, shape, dt, at)[0]

        X = fixed("x_feature_major", [P, KT, T2])
        H_hi, H_lo = fixed("h_hi", [P, KT, T2], F32R), fixed("h_lo", [P, KT, T2], F32R)
        g_at = region(2 * 4 * KT * T2)
        G_hi, g_mid = place("g_hi", [P, KT, T2], F32R, g_at)
        G_lo, _ = place("g_lo", [P, KT, T2], F32R, g_mid)
        UNIT = 2048
        raw = [fixed(f"w_raw{i}", [P, UNIT]) for i in range(3)]
        whi = [fixed(f"w_hi{i}", [P, UNIT], F32R) for i in range(2)]
        wlo = [fixed(f"w_lo{i}", [P, UNIT], F32R) for i in range(2)]
        prm_at, prm_n = offsets(PARAMS)
        prm = fixed("params", [P, prm_n])
        ident = fixed("identity", [P, P])
        ones = fixed("ones", [P, P])
        rot = fixed("rot", [P, P])
        spread = fixed("spread", [P, P])
        small_consts = fixed("small_consts", [P, 4 + 2 + 2 * AH])
        qscale, hsel = small_consts[:, 0:4], small_consts[:, 4:6]
        own_pair, own_head = small_consts[:, 6:6 + AH], small_consts[:, 6 + AH:6 + 2 * AH]
        kcT = fixed("kc", [P, 32])
        vcn = fixed("vc", [32, KW])
        var = fixed("variance", [P, 3, TT + 1])
        half = fixed("minus_half", [P, 16])
        work_at = cursor[0]
        sq = [fixed(f"squares{i}", [P, T2]) for i in range(2)]
        acc = fixed("square_sum", [P, T2])
        tmp = fixed("h_rounded_from", [P, T2])
        R = cursor[0]
        R_END = nc.sbuf_usable_end

        bank = ctx.enter_context(nc.psum_tensor("bank", [P, 8, 512], F32))

        load = new_sem("load_small")
        loads = [0]

        def small(dst, src):
            nc.sync.dma_start(dst, src).then_inc(load, 16)
            loads[0] += 16
            return (load, loads[0])

        cst = A["consts"]
        widths = A["const_at"]

        def table(name, dst):
            at, n = widths[name]
            return small(dst, cst[:, at:at + n])

        small(prm[:, :], A["params"][:, :])
        table("ident", ident[:, :])
        table("rot", rot[:, :])
        table("spread", spread[:, :])
        for name, dst in (("qscale", qscale), ("hsel", hsel), ("own_pair", own_pair), ("own_head", own_head)):
            table(name, dst)

        x_rows, _ = place("x_rows", [P, TT, D], F32, g_at)
        loaded = small(x_rows[:, :, :], A["x"].rearrange("(t p) d -> p t d", p=P))
        PO.did(nc.gpsimd.memset(ones[:, :], 1.0))
        PO.did(nc.gpsimd.memset(half[:, :], -0.5))
        m_ones = PO.did(nc.gpsimd.memset(var[:, :, :], 1.0))

        def param(name, i=0, n=1, parts=slice(0, P)):
            at = prm_at[name][0] + i
            return prm[parts, at:at + n]

        units = []

        def plan(w, k0, kts, cols, split=True):
            src = w.rearrange("(k p) n -> p k n", p=P)
            n = sum(b - a for a, b in cols)
            pieces, at = [], 0
            for a, b in cols:
                pieces.append((at, b - a, src[:, k0:k0 + kts, a:b]))
                at += b - a
            assert kts * n <= UNIT
            units.append((pieces, kts, n, split))

        def plan_cols(w, c0, c1, k0=0, kts=KT, step=256):
            for c in range(c0, c1, step):
                plan(w, k0, kts, [(c, min(c + step, c1))])

        def head_pairs(c, a):
            return [(c + AD * h, c + AD * h + AD) for j in range(2) for h in (2 * a + j, 4 + 2 * a + j)]

        w_in = A["w_in"]
        plan(w_in, 0, KT, [(Z_MI, Z_MI + 2 * MH), (Z_AG, Z_AG + 3 * AH)])
        plan_cols(w_in, Z_MQ, Z_MI)
        plan(w_in, 0, KT, [(Z_KC, Z_KC + 2 * KW)])
        for w1 in ("cmp_k_w1", "cmp_v_w1"):
            for part in range(2):
                src = A[w1].rearrange("(j d) n -> d j n", d=AD)[:, 16 * part:16 * part + 16, :]
                units.append(([(None, None, src)], 16, CH, False))
        for a in range(2):
            plan(w_in, 0, KT, head_pairs(Z_AQ, a))
        plan_cols(w_in, Z_KS, Z_AG)
        plan_cols(A["w_out"], 0, D)
        for part in range(2):
            for c in range(part * FF // 2, (part + 1) * FF // 2, 128):
                plan(A["w_up"], 0, KT, [(c, c + 128), (FF + c, FF + c + 128)])
            plan_cols(A["w_down"], 0, D, k0=KT * part)
        for c in range(0, D, 256):
            plan(A["w_ple_gate"], 0, KT, [(c, c + 256)])
            plan(A["w_ple_proj"], 0, 2, [(c, c + 256)])
        for layer in range(2):
            w = A["w_in_2"][layer, :, :]
            plan_cols(w, C_KA, C_ZA)
            for a in range(2):
                plan(w, 0, KT, head_pairs(C_QA, a))
            plan_cols(w, C_ZA, C_QB)
            plan_cols(w, C_QB, C_ZB)
            plan_cols(w, C_ZB, C_GA)
            for c in range(0, D, 256):
                plan(w, 0, KT, [(C_GA + c, C_GA + c + 256)])
                plan(A["w_o_attn_2"][layer, :, :], 0, 4, [(c, c + 256)])
                plan(w, 0, KT, [(C_GB + c, C_GB + c + 256)])
                plan(A["w_o_na_2"][layer, :, :], 0, 4, [(c, c + 256)])
            plan_cols(A["w_out_2"][layer, :, :], 0, D)

        raw_sem = [new_sem(f"w_arrived{i}") for i in range(3)]
        raw_n = [0, 0, 0]
        arrived, split_done, used = {}, {}, {}
        state = {"dma": 0, "split": 0, "use": 0}

        def released(u):
            return split_done.get(u) if units[u][3] else used.get(u)

        def fetch():
            while state["dma"] < len(units):
                u = state["dma"]
                i = u % 3
                if u >= 3:
                    marks = released(u - 3)
                    if marks is None:
                        return
                    SP.wait(*marks)
                pieces, kts, n, _ = units[u]
                dst = raw[i][:, 0:kts * n].rearrange("p (k n) -> p k n", k=kts)
                for at, width, src in pieces:
                    if at is None:
                        for half in range(2):
                            nc.sync.dma_start(dst[64 * half:64 * half + 64, :, :], src).then_inc(raw_sem[i], 16)
                            raw_n[i] += 16
                    else:
                        nc.sync.dma_start(dst[:, :, at:at + width], src).then_inc(raw_sem[i], 16)
                        raw_n[i] += 16
                arrived[u] = (raw_sem[i], raw_n[i])
                state["dma"] += 1

        def split(u):
            if u >= len(units) or u in split_done or not units[u][3]:
                return
            _, kts, n, _ = units[u]
            i = u % 2
            prior = used.get(u - 2, ())
            AC.wait(arrived[u], *prior)
            hi = AC.did(nc.scalar.activation(whi[i][:, 0:kts * n], raw[u % 3][:, 0:kts * n], ACT.Copy))
            PO.wait(arrived[u], *prior, hi)
            lo = PO.did(nc.gpsimd.tensor_tensor(wlo[i][:, 0:kts * n], raw[u % 3][:, 0:kts * n],
                                                whi[i][:, 0:kts * n].bitcast(F32), ALU.subtract))
            split_done[u] = (hi, lo)

        def weights():
            u = state["use"]
            state["use"] += 1
            fetch()
            split(u)
            fetch()
            _, kts, n, do_split = units[u]
            if not do_split:
                PE.wait(arrived[u])
                split(u + 1)
                return raw[u % 3][:, 0:kts * n].rearrange("p (k n) -> p k n", k=kts), None, u
            PE.wait(*split_done[u])
            views = [t[u % 2][:, 0:kts * n].rearrange("p (k n) -> p k n", k=kts) for t in (whi, wlo)]
            return views[0], views[1], u

        def weights_done(u, mark):
            used[u] = (mark,)
            fetch()
            if u + 1 < len(units):
                split(u + 1)
                fetch()

        def prefetch_split(u):
            split(u)

        def product(outs, stationary, moving, k, first, last):
            ins = None
            terms = ((0, 0), (0, 1), (1, 0))
            for n, (a, b) in enumerate(terms):
                for i, out in enumerate(outs):
                    ins = nc.tensor.matmul(out, stationary[a](k), moving[b](k)[i],
                                           start=first and n == 0, stop=last and n == 2)
            return ins

        def chunks(n):
            return [(0, n)] if n <= 512 else [(0, HALF), (HALF, n)]

        def to_features(act, kts, wviews, cols, n, out_banks):
            return tiles_to_features(act, kts, wviews, [cols], n, [out_banks])

        def tiles_to_features(act, kts, wviews, cols, n, out_banks):
            ch = chunks(n)
            mv = [lambda k, t=t: [t[:, k, a:b] for a, b in ch] for t in act[:2]]
            for k in range(kts):
                PE.wait(*act[2][k])
                for c, b0 in zip(cols, out_banks):
                    outs = [bank[:, b0 + i, 0:b - a] for i, (a, b) in enumerate(ch)]
                    st = [lambda k, t=t, c=c: c(t, k) for t in wviews]
                    ins = product(outs, st, mv, k, k == 0, k == kts - 1)
            return PE.did(ins)

        def columns(c):
            return lambda t, k: t[:, k, c:c + P]

        def feature_view(b, n):
            if n <= 512:
                return bank[:, b, 0:n]
            return bank[:, b:b + 2, 0:HALF]

        def dest(ap, n):
            return ap if n <= 512 else ap.rearrange("p (c t) -> p c t", c=2)

        def to_tokens(act, t0, tn, wviews, c0, cn, out):
            st = [lambda k, t=t: t[:, k, t0:t0 + tn] for t in act[:2]]
            mv = [lambda k, t=t: [t[:, k, c0:c0 + cn]] for t in wviews]
            for k in range(KT):
                PE.wait(*act[2][k])
                ins = product([out], st, mv, k, k == 0, k == KT - 1)
            return PE.did(ins)

        def split_into(hi, lo, src, *marks, lane=None):
            lane = lane or DV
            AC.wait(*marks)
            a = AC.did(nc.scalar.activation(hi, src, ACT.Copy))
            lane.wait(*marks, a)
            b = lane.did(lane.engine.tensor_tensor(lo, src, hi.bitcast(F32), ALU.subtract))
            return a, b

        sq_free = [(), ()]
        state["acc"] = None

        def add_square(k, n, *ready):
            AC.wait(*ready, *sq_free[k % 2])
            if k == 0:
                AC.wait(*acc_free)
                state["acc"] = AC.did(nc.scalar.activation(acc[:, 0:n], X[:, k, 0:n], ACT.Square))
                return
            m = AC.did(nc.scalar.activation(sq[k % 2][:, 0:n], X[:, k, 0:n], ACT.Square))
            DV.wait(m, state["acc"])
            state["acc"] = DV.did(nc.vector.tensor_tensor(acc[:, 0:n], acc[:, 0:n], sq[k % 2][:, 0:n], ALU.add))
            sq_free[k % 2] = (state["acc"],)

        acc_free = []

        def tok_tiles(n):
            return [(t * P, P) for t in range(TT)] + ([(S, META)] if n > S else [])

        def reciprocal_root(n):
            PE.wait(state["acc"], m_ones)
            for t, (t0, tn) in enumerate(tok_tiles(n)):
                ins = nc.tensor.matmul(bank[0:tn, 7, t:t + 1], acc[:, t0:t0 + tn], ones[:, 0:1], start=True, stop=True)
            m = PE.did(ins)
            acc_free[:] = [m]
            DV.wait(m, m_ones)
            m = DV.did(nc.vector.tensor_scalar(var[:, 0, 0:TT], bank[:, 7, 0:TT], 1.0 / D, EPS, ALU.mult, ALU.add))
            if n > S:
                m = DV.did(nc.vector.tensor_scalar(var[0:META, 0, TT:TT + 1], bank[0:META, 7, TT:TT + 1], 1.0 / D, EPS,
                                                   ALU.mult, ALU.add))
            PO.wait(m)
            m = PO.did(nc.gpsimd.tensor_tensor(var[:, 1, :], var[:, 0, :], half[:, 0:TT + 1], ALU.pow))
            DV.wait(m, *sq_free[0])
            m = DV.did(nc.vector.tensor_tensor(sq[0][:, 0:S].rearrange("p (t q) -> p t q", t=TT),
                                               ident[:, :].unsqueeze(1).broadcast_to([P, TT, P]),
                                               var[:, 1, 0:TT].unsqueeze(2).broadcast_to([P, TT, P]), ALU.mult))
            if n > S:
                m = DV.did(nc.vector.tensor_scalar(sq[0][:, S:T2], ident[:, 0:META], var[:, 1, TT:TT + 1], None, ALU.mult))
            PE.wait(m)
            for i, (a, z) in enumerate(chunks(n)):
                ins = nc.tensor.matmul(bank[:, 4 + i, 0:z - a], ones[:, :], sq[0][:, a:z], start=True, stop=True)
            m = PE.did(ins)
            sq_free[0] = (m,)
            return m

        def rms_norm_split(gain, n, *ready):
            r = reciprocal_root(n)
            DV.wait(*ready, PE.last)
            AC.wait(*ready, PE.last)
            PO.wait(PE.last)
            bufs = (tmp, sq[0], sq[1])
            freed = {}
            marks = []
            for k in range(KT):
                t = bufs[k % 3]
                DV.wait(r, *freed.get(k % 3, ()))
                c = DV.did(nc.vector.scalar_tensor_tensor(dest(t[:, 0:n], n), dest(X[:, k, 0:n], n), param(gain, k),
                                                          feature_view(4, n), ALU.mult, ALU.mult))
                m = split_into(H_hi[:, k, 0:n], H_lo[:, k, 0:n], t[:, 0:n], c, lane=PO if k % 2 else DV)
                freed[k % 3] = m
                marks.append(m)
            sq_free[0], sq_free[1] = marks[-1] + marks[-2] + marks[-3], marks[-1] + marks[-2] + marks[-3]
            return H_hi, H_lo, marks

        def pipeline(items, *stages):
            for step in range(len(items) + len(stages) - 1):
                for n, stage_ in enumerate(stages):
                    if 0 <= step - n < len(items):
                        stage_(items[step - n])

        def evacuate(dst, src, mark, scale=None, lane=None):
            if lane is DV:
                DV.wait(mark)
                if scale is None:
                    return DV.did(nc.vector.tensor_copy(dst, src))
                return DV.did(nc.vector.tensor_scalar(dst, src, scale, None, ALU.mult))
            AC.wait(mark)
            if scale is None:
                return AC.did(nc.scalar.activation(dst, src, ACT.Copy))
            return AC.did(nc.scalar.activation(dst, src, ACT.Copy, scale=scale))

        def features_steps(dsts, n, act, scale=None, together=False, then=None):
            hi, lo, u = weights()
            if together:
                (b, i), (b2, i2) = dense.take(PE), dense.take(PE)
                m = tiles_to_features(act, KT, (hi, lo), [columns(0), columns(P)], n, [b, b2])
                weights_done(u, m)
                got = [(b, i, m), (b2, i2, m)]
            for j, dst in enumerate(dsts):
                if together:
                    b, i, m = got[j]
                else:
                    b, i = dense.take(PE)
                    m = to_features(act, KT, (hi, lo), columns(j * P), n, b)
                    if j == len(dsts) - 1:
                        weights_done(u, m)
                e = evacuate(dest(dst, n), feature_view(b, n), m, scale(j) if callable(scale) else scale,
                             DV if j % 2 else AC)
                dense.free(i, e)
                done.append(e)
                yield

        def tokens_steps(dst_of, tiles, act, func=None, c0=0, cn=256, unit=None, finish_unit=True):
            hi, lo, u = unit or weights()
            for t, (t0, tn) in enumerate(tiles):
                b, i = dense.take(PE)
                m = to_tokens(act, t0, tn, (hi, lo), c0, cn, bank[0:tn, b, 0:cn])
                if t == len(tiles) - 1 and finish_unit:
                    weights_done(u, m)
                dst, shape = dst_of(t)
                src = shape(bank[0:tn, b, 0:cn])
                if func is None:
                    e = evacuate(dst, src, m, None, DV if t % 2 else AC)
                else:
                    AC.wait(m)
                    e = AC.did(nc.scalar.activation(dst, src, func, scale=0.5))
                dense.free(i, e)
                done.append(e)
                yield

        done = []

        def all_of(*gens):
            for g in gens:
                yield from g

        def drain(gen):
            for _ in gen:
                pass

        dense = Slots([0, 1, 2, 3])
        stage("x_in")
        fetch()
        small_loaded = (load, loads[0])
        for lane in compute:
            lane.wait(small_loaded)
        split(0)
        turn = Slots([0, 1, 2, 3, 4, 5, 6])
        for k in range(KT):
            b, i = turn.take(PE)
            for t in range(TT):
                ins = nc.tensor.transpose(bank[:, b, t * P:(t + 1) * P], x_rows[:, t, k * P:(k + 1) * P], ident[:, :])
            m = PE.did(ins)
            DV.wait(m)
            m = DV.did(nc.vector.tensor_copy(X[:, k, 0:S], bank[:, b, :]))
            turn.free(i, m)
            add_square(k, S, m)
        stage("norm1")
        Hs = rms_norm_split("ln1", S)

        c = R
        mqT, c = place("mq", [P, MH, S], F32, c)
        mkT, c = place("mk", [P, MH, S], F32, c)
        mv, c = place("mv", [P, TT, MH, MD + 1], F32, c)
        mo, c = place("mo_gate", [P, TT, MW], F32, c)
        g4, c = place("gate_rows", [MH, 5, S], F32, c)
        negM, c = place("neg_M", [P, S], F32, c)
        decay, c = place("decay", [P, S], F32, c)
        WT, c = place("mlstm_weights", [P, TT, S], F32, c)
        assert c <= R_END, c
        gate_row = {n: g4[:, i, :] for i, n in enumerate(("f", "a", "b", "i", "m"))}
        c2 = g_at
        aqT, c2 = place("aq", [P, 4, S], F32, c2)
        kvT, c2 = place("kv", [P, 4, S], F32, c2)
        vs, c2 = place("vs", [P, 2, TT, KW], F32, c2)
        ag, c2 = place("ag", [P, TT, 3 * AH], F32, c2)
        col4, c2 = place("gate_columns", [P, 3, TT, MH], F32, c2)
        msq, c2 = place("m_square", [P, 2, TT, MH], F32, c2)
        late, c2 = place("later", [P, P], F32, c2)
        pick, c2 = place("pick", [P, MH, P], F32, c2)
        den, c2 = place("mlstm_den", [P, 4], F32, c2)
        diag0, c2 = place("diag0", [P, P], F32, c2)
        ndist, c2 = place("distance", [P, S], F32, c2)
        cb, c2 = place("cmp_bias", [P, TT, AH * 32], F32, c2)
        cv, c2 = place("cmp_valid", [P, TT, 32], F32, c2)
        assert c2 <= g_at + 2 * 4 * KT * T2, c2 - g_at
        c2 = work_at
        block, c2 = place("cmp_blocks", [P, CB, NC], F32, c2)
        hid, c2 = place("cmp_hidden", [P, 4, 32], F32, c2)
        cw2, c2 = place("cmp_w2", [P, 2, 2 * AD], F32, c2)
        assert c2 <= R

        stage("project1")
        SP.wait(PE.last)
        table("later", late[:, :])
        table("pick", pick[:, :, :].rearrange("p h q -> p (h q)"))
        table("ndist", ndist[:, :])
        table("cbias", cb[:, :, :].rearrange("p t x -> p (t x)"))
        tables1 = table("cvalid", cv[:, :, :].rearrange("p t x -> p (t x)"))

        hi, lo, u = weights()
        (b, i), (b2, i2) = dense.take(PE), dense.take(PE)
        for k in range(KT):
            PE.wait(*Hs[2][k])
            for n in range(2):
                ins = product([bank[0:MH, (b, b2)[n], 0:S]],
                              [lambda k, t=t: t[:, k, MH * n:MH * n + MH] for t in (hi, lo)],
                              [lambda k, t=t: [t[:, k, 0:S]] for t in Hs[:2]], k, k == 0, k == KT - 1)
        m = PE.did(ins)
        AC.wait(m)
        mi = AC.did(nc.scalar.activation(gate_row["i"], bank[0:MH, b, 0:S], ACT.Identity, bias=param("gate_b", 0, 1, slice(0, MH))))
        mf = AC.did(nc.scalar.activation(gate_row["f"], bank[0:MH, b2, 0:S], ACT.Identity, bias=param("gate_b", 1, 1, slice(0, MH))))
        dense.free(i, mi)
        dense.free(i2, mf)
        b, i = dense.take(PE)
        for t in range(TT):
            m = to_tokens(Hs, t * P, P, (hi, lo), 2 * MH, 3 * AH, bank[:, b, t * 3 * AH:(t + 1) * 3 * AH])
        weights_done(u, m)
        AC.wait(m)
        m = AC.did(nc.scalar.activation(ag[:, :, :].rearrange("p t g -> p (t g)"), bank[:, b, 0:TT * 3 * AH], ACT.Tanh, scale=0.5))
        dense.free(i, m)
        DV.wait(m)
        ag_done = DV.did(nc.vector.tensor_scalar(ag[:, :, :], ag[:, :, :], 0.5, 0.5, ALU.mult, ALU.add))

        gr = gate_row
        DV.wait(mf, mi)
        m = DV.did(nc.vector.scalar_tensor_tensor(gr["a"], gr["f"], -1.0, gr["f"], ALU.mult, ALU.min))
        AC.wait(m)
        m = AC.did(nc.scalar.activation(gr["a"], gr["a"], ACT.Exp))
        AC.wait(m, m_ones)
        m = AC.did(nc.scalar.activation(gr["a"], gr["a"], ACT.Ln, bias=ones[0:MH, 0:1]))
        DV.wait(m)
        m = DV.did(nc.vector.scalar_tensor_tensor(gr["f"], gr["f"], 0.0, gr["a"], ALU.min, ALU.subtract))
        DV.wait(m)
        m = DV.did(nc.vector.memset(gr["m"], 1.0))
        DV.wait(m)
        m = DV.did(nc.vector.tensor_tensor_scan(gr["b"], gr["m"], gr["f"], 0.0, ALU.mult, ALU.add))
        DV.wait(m)
        m = DV.did(nc.vector.tensor_tensor(gr["i"], gr["i"], gr["b"], ALU.subtract))
        DV.wait(m)
        m = DV.did(nc.vector.tensor_tensor_scan(gr["a"], gr["i"], gr["i"], 0.0, ALU.max, ALU.max))
        DV.wait(m)
        m = DV.did(nc.vector.tensor_tensor(gr["m"], gr["b"], gr["a"], ALU.add))
        DV.wait(m)
        m_rows = DV.did(nc.vector.tensor_scalar(gr["f"], gr["a"], -1.0, None, ALU.mult))

        tiles1 = [(t * P, P) for t in range(TT)]
        done.clear()
        for a in range(2):
            drain(features_steps([mqT[:, 2 * a + j, :] for j in range(2)], S, Hs, scale=MD ** -0.5))
        PE.wait(m_rows)
        b, i = dense.take(PE)
        for n, name in enumerate(("i", "m")):
            for t in range(TT):
                ins = nc.tensor.transpose(bank[:, b, (n * TT + t) * MH:(n * TT + t + 1) * MH],
                                          gr[name][:, t * P:(t + 1) * P], ident[0:MH, 0:MH])
        m = PE.did(ins)
        DV.wait(m)
        m = DV.did(nc.vector.tensor_copy(col4[:, 0:2, :, :].rearrange("p a t h -> p (a t h)"), bank[:, b, 0:2 * TT * MH]))
        dense.free(i, m)
        AC.wait(m)
        em_done = AC.did(nc.scalar.activation(col4[:, 2, :, :], col4[:, 1, :, :], ACT.Exp, scale=-1.0))
        for a in range(2):
            drain(features_steps([mkT[:, 2 * a + j, :] for j in range(2)], S, Hs))
        for a in range(2):
            drain(tokens_steps(lambda t: (mv[:, t, 2 * a:2 * a + 2, 0:MD], lambda x: x.rearrange("p (h d) -> p h d", h=2)),
                               tiles1, Hs))
        done.append(PO.did(nc.gpsimd.memset(mv[:, :, :, MD:MD + 1], 1.0)))
        mlstm_in = tuple(done)

        mo_in = []

        def mlstm_steps():
            scores, outs_ = Slots([4, 5]), Slots([6, 7])
            wt_free = neg_free = ()
            sq_mark = None
            PE.wait(*mlstm_in, tables1)
            DV.wait(tables1)
            for h in range(MH):
                b, i = dense.take(PE)
                m = PE.did(nc.tensor.matmul(bank[:, b, 0:S], pick[0:MH, h, :], gr["f"], start=True, stop=True))
                AC.wait(*neg_free)
                DV.wait(*neg_free)
                mneg = evacuate(negM[:, :], bank[:, b, 0:S], m)
                dense.free(i, mneg)
                wmarks = []
                decays = ()
                yield
                for s in range(TT):
                    n = S - s * P
                    b, i = scores.take(PE)
                    mqk = PE.did(nc.tensor.matmul(bank[:, b, 0:n], mkT[:, h, s * P:(s + 1) * P], mqT[:, h, s * P:S],
                                                  start=True, stop=True))
                    DV.wait(mneg, *wt_free, *decays)
                    md = DV.did(nc.vector.tensor_tensor(diag0[:, :], negM[:, s * P:(s + 1) * P], late[:, :], ALU.add))
                    AC.wait(md, em_done, *wmarks[-1:], *([sq_mark] if sq_mark else []))
                    me = AC.did(nc.scalar.activation(decay[:, 0:P], diag0[:, :], ACT.Exp, bias=col4[:, 0, s, h:h + 1]))
                    decays = (me,)
                    if n > P:
                        me = AC.did(nc.scalar.activation(decay[:, P:n], negM[:, (s + 1) * P:S], ACT.Exp,
                                                         bias=col4[:, 0, s, h:h + 1]))
                    DV.wait(me, mqk)
                    mw = DV.did(nc.vector.tensor_tensor(WT[:, s, s * P:S], bank[:, b, 0:n], decay[:, 0:n], ALU.mult))
                    scores.free(i, mw)
                    wmarks.append(mw)
                    yield
                neg_free = (me,)
                PE.wait(*wmarks)
                for l in range(TT):
                    b, i = outs_.take(PE)
                    for s in range(l + 1):
                        ins = nc.tensor.matmul(bank[:, b, 0:MD + 1], WT[:, s, l * P:(l + 1) * P], mv[:, s, h, :],
                                               start=s == 0, stop=s == l)
                    m = PE.did(ins)
                    DV.wait(m, em_done)
                    d1 = DV.did(nc.vector.scalar_tensor_tensor(den[:, 0:1], bank[:, b, MD:MD + 1], -1.0, col4[:, 2, l, h:h + 1],
                                                               ALU.mult, ALU.max))
                    DV.wait(d1)
                    d1 = DV.did(nc.vector.tensor_tensor(den[:, 1:2], bank[:, b, MD:MD + 1], den[:, 0:1], ALU.max))
                    DV.wait(d1)
                    d1 = DV.did(nc.vector.reciprocal(den[:, 2:3], den[:, 1:2]))
                    DV.wait(d1)
                    hmv = mqT[:, h, l * P:(l + 1) * P]
                    d1 = DV.did(nc.vector.tensor_scalar(hmv, bank[:, b, 0:MD], den[:, 2:3], None, ALU.mult))
                    outs_.free(i, d1)
                    AC.wait(d1, *([sq_mark] if sq_mark else []), *wmarks[-1:])
                    sq_mark = AC.did(nc.scalar.activation(decay[:, 0:P], hmv, ACT.Square, accum_out=msq[:, 0, l, h:h + 1]))
                    yield
                wt_free = (m,)
            DV.wait(sq_mark)
            r = DV.did(nc.vector.tensor_scalar(msq[:, 1, :, :], msq[:, 0, :, :], 4.0 / MD, 4.0 * EPS, ALU.mult, ALU.add))
            PO.wait(r)
            r = PO.did(nc.gpsimd.tensor_tensor(msq[:, 0, :, :].rearrange("p t h -> p (t h)"),
                                               msq[:, 1, :, :].rearrange("p t h -> p (t h)"), half[:, 0:TT * MH], ALU.pow))
            DV.wait(r, *mo_in)
            hm_v = mqT[:, :, :].rearrange("p h (t d) -> p t h d", t=TT)
            for t in range(TT):
                g = mo[:, t, :].rearrange("p (h d) -> p h d", h=MH)
                m = DV.did(nc.vector.scalar_tensor_tensor(g, g, 1.0, hm_v[:, t, :, :], ALU.add, ALU.mult))
                DV.wait(m)
                DV.did(nc.vector.tensor_tensor(g, g, msq[:, 0, t, :].unsqueeze(2).broadcast_to([P, MH, MD]), ALU.mult))
                yield

        def compress_steps(cmp_in, w2_in):
            m = None
            for n in range(2):
                src = kvT[:, n, :]
                DV.wait(*cmp_in)
                if m is not None:
                    DV.wait(m)
                win = bass_windows(src)
                pe = param("pe_k" if n == 0 else "pe_v", 0, CB)
                mb = DV.did(nc.vector.tensor_tensor(block[:, :, :], win, pe.unsqueeze(2).broadcast_to([P, CB, NC]), ALU.add))
                PE.wait(mb)
                (b, i), (b2, i2) = dense.take(PE), dense.take(PE)
                for part in range(2):
                    w1, _, u = weights()
                    for g in range(AG):
                        rows = slice(g * AD, (g + 1) * AD)
                        for j in range(16):
                            jj = 16 * part + j
                            ins = nc.tensor.matmul(bank[:, (b, b2)[g], 0:NC], w1[rows, j, :], block[rows, jj, :],
                                                   start=jj == 0, stop=jj == CB - 1)
                    m = PE.did(ins)
                    weights_done(u, m)
                    if part == 0:
                        yield
                hx, h3 = hid[:, 0:2, 0:NC], hid[:, 2:4, 0:NC]
                AC.wait(m)
                e = AC.did(nc.scalar.activation(hid[:, 0, 0:NC], bank[:, b, 0:NC], ACT.Copy))
                dense.free(i, e)
                e = AC.did(nc.scalar.activation(hid[:, 1, 0:NC], bank[:, b2, 0:NC], ACT.Copy))
                dense.free(i2, e)
                AC.wait(e)
                e = AC.did(nc.scalar.activation(h3, hx, ACT.Square))
                DV.wait(e)
                e = DV.did(nc.vector.tensor_scalar(h3, h3, 0.044715, 1.0, ALU.mult, ALU.add))
                DV.wait(e)
                e = DV.did(nc.vector.tensor_tensor(h3, h3, hx, ALU.mult))
                AC.wait(e)
                e = AC.did(nc.scalar.activation(h3, h3, ACT.Tanh, scale=math.sqrt(2 / math.pi)))
                yield
                DV.wait(e)
                e = DV.did(nc.vector.scalar_tensor_tensor(h3, h3, 1.0, hx, ALU.add, ALU.mult))
                DV.wait(e)
                e = DV.did(nc.vector.tensor_scalar(hx, h3, 0.5, None, ALU.mult))
                PE.wait(e, w2_in)
                (b, i), (b2, i2) = dense.take(PE), dense.take(PE)
                for g in range(AG):
                    if n == 0:
                        ins = nc.tensor.matmul(bank[:, (b, b2)[g], 0:NC], cw2[:, 0, :], hid[:, g, 0:NC], start=True, stop=True)
                    else:
                        ins = nc.tensor.matmul(bank[0:NC, b, g * AD:(g + 1) * AD], hid[:, g, 0:NC], cw2[:, 1, 0:AD],
                                               start=True, stop=True)
                m = PE.did(ins)
                if n == 0:
                    for g in range(AG):
                        rows = slice(g * AD, (g + 1) * AD)
                        e = evacuate(kcT[rows, 0:NC], bank[rows, (b, b2)[g], 0:NC], m)
                else:
                    e = evacuate(vcn[0:NC, :], bank[0:NC, b, 0:KW], m)
                dense.free(i, e)
                dense.free(i2, e)
                done.append(e)
                yield

        stage("mlstm")
        SP.wait(*Hs[2][-1], *Hs[2][-2], *Hs[2][-3])
        PO.wait(*Hs[2][-1])
        done.append(PO.did(nc.gpsimd.memset(kcT[:, :], 0.0)))
        for n, w2 in enumerate(("cmp_k_w2", "cmp_v_w2")):
            for part in range(2):
                w2_in = small(cw2[:, n, part * AD:part * AD + AD], A[w2][:, :])

        def rest_steps():
            done.clear()
            for a in range(2):
                yield from tokens_steps(lambda t: (mo[:, t, 256 * a:256 * a + 256], lambda x: x), tiles1, Hs, func=ACT.Tanh)
            mo_in.extend(done)
            done.clear()
            yield from features_steps([kvT[:, j, :] for j in range(2)], S, Hs)
            yield from compress_steps(tuple(done), w2_in)
            for a in range(2):
                yield from features_steps([aqT[:, 2 * a + j, :] for j in range(2)], S, Hs,
                                          scale=lambda j: qscale[:, 2 * a + j:2 * a + j + 1])
            for n in range(2):
                unit = weights()
                b, i = dense.take(PE)
                m = to_features(Hs, KT, unit[:2], columns(0), S, b)
                e = evacuate(kvT[:, 2 + n, :], bank[:, b, 0:S], m)
                dense.free(i, e)
                done.append(e)
                yield
                b, i = dense.take(PE)
                for t in range(TT):
                    m = to_tokens(Hs, t * P, P, unit[:2], P, KW, bank[:, b, t * KW:(t + 1) * KW])
                weights_done(unit[2], m)
                e = evacuate(vs[:, n, :, :].rearrange("p t c -> p (t c)"), bank[:, b, :], m, None, DV)
                dense.free(i, e)
                done.append(e)
                yield

        rest = rest_steps()
        for step, _ in enumerate(mlstm_steps()):
            if step % 3 != 2:
                next(rest, None)
        drain(rest)
        nsa_in = tuple(done)

        stage("nsa")
        fence()
        c = R
        a_rows, c = place("a_rows", [P, TT, AW], F32, c)
        sc_s, pr_s, pt_s = [None] * 2, [None] * 2, [None] * 2
        for n in range(2):
            pr_s[n], c = place(f"probs{n}", [P, S], F32, c)
            pt_s[n], c = place(f"probsT{n}", [P, TT, P], F32, c)
        assert c <= R + 2 * 8192
        c = R + 2 * 8192 + 4 * TT * MH * (MD + 1) + 8192
        stat, c = place("softmax_stats", [P, 5, 3, AH], F32, c)
        mixed, c = place("branch_part", [P, 512], F32, c)
        for n in range(2):
            sc_s[n], c = place(f"scores{n}", [P, S], F32, c)
        pt_s.append(place("probsT2", [P, TT, P], F32, c)[0])
        assert c + 2048 <= R_END, c
        PE.wait(*nsa_in)
        DV.wait(ag_done)
        scores, turned, outb = Slots([2, 3]), Slots([4, 5]), Slots([6, 7])
        sc, pr, pt = Slots(sc_s), Slots(pr_s), Slots(pt_s)
        gates_of = [ag[:, t, :].rearrange("p (h b) -> p b h", b=3) for t in range(TT)]

        def qk_rows(h):
            return slice(AD * (h // 4), AD * (h // 4) + AD)

        pair_order = [0, 4, 1, 5, 2, 6, 3, 7]
        items = [(t, br, h) for t in range(TT) for br in range(3) for h in ([0] if br == 0 else pair_order)]
        live = {}
        stat_free = {br: () for br in range(3)}
        a_sum = {}

        def nsa_score(item):
            t, br, h = item
            n = (t + 1) * P
            if br == 0:
                (b, i), (b2, i2) = scores.take(PE), scores.take(PE)
                for x in range(AH):
                    ins = nc.tensor.matmul(bank[:, (b, b2)[x // 4], x % 4 * 32:x % 4 * 32 + NC + 1],
                                           aqT[qk_rows(x), x % 4, t * P:(t + 1) * P], kcT[qk_rows(x), 0:NC + 1],
                                           start=True, stop=True)
                m = PE.did(ins)
                s_, si = sc.take(DV)
                DV.wait(m, *stat_free[0])
                for x in range(AH):
                    e = DV.did(nc.vector.scalar_tensor_tensor(s_[:, 32 * x:32 * x + 32], bank[:, (b, b2)[x // 4], x % 4 * 32:x % 4 * 32 + 32],
                                                              2.0 ** -(x + 1), cb[:, t, 32 * x:32 * x + 32], ALU.mult, ALU.add))
                scores.free(i, e)
                scores.free(i2, e)
                DV.wait(e)
                s3 = s_[:, 0:256].rearrange("p (h n) -> p h n", h=AH)
                e = DV.did(nc.vector.reduce_max(stat[:, 0, 0, :], s3, AX.X))
                DV.wait(e)
                e = DV.did(nc.vector.tensor_tensor(s3, s3, stat[:, 0, 0, :].unsqueeze(2).broadcast_to([P, AH, 32]), ALU.subtract))
                AC.wait(e)
                e = AC.did(nc.scalar.activation(s_[:, 0:256], s_[:, 0:256], ACT.Exp))
                p_, pi = pr.take(DV)
                p3 = p_[:, 0:256].rearrange("p (h n) -> p h n", h=AH)
                DV.wait(e)
                es = DV.did(nc.vector.reduce_sum(stat[:, 1, 0, :], s3, AX.X))
                e = DV.did(nc.vector.tensor_tensor(p3, s3, cv[:, t, :].unsqueeze(1).broadcast_to([P, AH, 32]), ALU.mult))
                sc.free(si, e)
                live[item] = (p_, pi, (e, es))
                return
            b, i = scores.take(PE)
            m = PE.did(nc.tensor.matmul(bank[:, b, 0:n], aqT[qk_rows(h), h % 4, t * P:(t + 1) * P],
                                        kvT[qk_rows(h), 1 + br, 0:n], start=True, stop=True))
            s_, si = sc.take(DV)
            DV.wait(m, *stat_free[br])
            e = DV.did(nc.vector.tensor_tensor_reduce(s_[:, 0:n], bank[:, b, 0:n], ndist[:, S - n:S], -2.0 ** -(h + 1), 3e38,
                                                      ALU.add, ALU.min, stat[:, 0, br, h:h + 1]))
            scores.free(i, e)
            p_, pi = pr.take(AC)
            AC.wait(e)
            e = AC.did(nc.scalar.activation(p_[:, 0:n], s_[:, 0:n], ACT.Exp, bias=stat[:, 0, br, h:h + 1], scale=-1.0,
                                            accum_out=stat[:, 1, br, h:h + 1]))
            sc.free(si, e)
            live[item] = (p_, pi, (e,))

        def nsa_turn(item):
            t, br, h = item
            p_, pi, ready = live[item]
            PE.wait(*ready)
            if br == 0:
                got = []
                for g in range(2):
                    b, i = turned.take(PE)
                    for x in range(4):
                        ins = nc.tensor.transpose(bank[0:32, b, x * P:(x + 1) * P], p_[:, (4 * g + x) * 32:(4 * g + x + 1) * 32],
                                                  ident[:, :])
                    m = PE.did(ins)
                    q_, qi = pt.take(AC)
                    e = evacuate(q_[0:NC, :, :].rearrange("p t q -> p (t q)"), bank[0:NC, b, :], m)
                    turned.free(i, e)
                    got.append((q_, qi, e))
                pr.free(pi, m)
                live[item] = (got, ready)
                return
            b, i = turned.take(PE)
            for k in range(t + 1):
                ins = nc.tensor.transpose(bank[:, b, k * P:(k + 1) * P], p_[:, k * P:(k + 1) * P], ident[:, :])
            m = PE.did(ins)
            pr.free(pi, m)
            lane = DV if h % 2 == 1 else AC
            q_, qi = pt.take(lane)
            e = evacuate(q_[:, 0:t + 1, :].rearrange("p t q -> p (t q)"), bank[:, b, 0:(t + 1) * P], m, None, lane)
            turned.free(i, e)
            live[item] = (q_, qi, e, ready)

        def nsa_value(item):
            t, br, h = item
            if br == 0:
                got, ready = live.pop(item)
                ob, oi = outb.take(PE)
                for g in range(2):
                    q_, qi, e = got[g]
                    PE.wait(e)
                    for x in range(4):
                        ins = nc.tensor.matmul(bank[:, ob, (4 * g + x) * AD:(4 * g + x + 1) * AD], q_[0:NC, x, :],
                                               vcn[0:NC, g * AD:(g + 1) * AD], start=True, stop=True)
                    m = PE.did(ins)
                    pt.free(qi, m)
            else:
                q_, qi, e, ready = live.pop(item)
                if h == pair_order[0]:
                    live["o"] = outb.take(PE)
                ob, oi = live["o"]
                PE.wait(e)
                for k in range(t + 1):
                    ins = nc.tensor.matmul(bank[:, ob, h * AD:(h + 1) * AD], q_[:, k, :],
                                           vs[:, br - 1, k, (h // 4) * AD:(h // 4 + 1) * AD], start=k == 0, stop=k == t)
                m = PE.did(ins)
                pt.free(qi, m)
                if h != pair_order[-1]:
                    return
            DV.wait(*ready)
            e = DV.did(nc.vector.reciprocal(stat[:, 2, br, :], stat[:, 1, br, :]))
            stat_free[br] = (e,)
            AC.wait(e)
            DV.wait(e)
            e = DV.did(nc.vector.tensor_tensor(stat[:, 2, br, :], stat[:, 2, br, :], gates_of[t][:, br, :], ALU.mult))
            DV.wait(e, m)
            dst = a_rows[:, t, :] if br == 0 else mixed[:, :]
            e = DV.did(nc.vector.tensor_tensor(dst.rearrange("p (h d) -> p h d", h=AH),
                                               bank[:, ob, :].rearrange("p (h d) -> p h d", h=AH),
                                               stat[:, 2, br, :].unsqueeze(2).broadcast_to([P, AH, AD]), ALU.mult))
            outb.free(oi, e)
            if br:
                DV.wait(e)
                DV.did(nc.vector.tensor_tensor(a_rows[:, t, :], a_rows[:, t, :], mixed[:, :], ALU.add))

        pipeline(items, nsa_score, nsa_turn, nsa_value)

        stage("mix_out")
        fence()
        marks = []
        for k in range(KT):
            rows = mo if k < 4 else a_rows
            b, i = dense.take(PE)
            for t in range(TT):
                ins = nc.tensor.transpose(bank[:, b, t * P:(t + 1) * P], rows[:, t, (k % 4) * P:(k % 4 + 1) * P], ident[:, :])
            m = PE.did(ins)
            if k < 4:
                s_, si = sc.take(AC)
                AC.wait(m)
                m = AC.did(nc.scalar.activation(s_[:, :], bank[:, b, :], ACT.Copy, scale=param("mnorm", k)))
                dense.free(i, m)
                got = split_into(H_hi[:, k, 0:S], H_lo[:, k, 0:S], s_[:, :], m, lane=PO if k % 2 else DV)
                sc.free(si, *got)
            else:
                got = split_into(H_hi[:, k, 0:S], H_lo[:, k, 0:S], bank[:, b, :], m)
                dense.free(i, *got)
            marks.append(got)
        Hs = (H_hi, H_lo, marks)

        def add_residual(act, kts, n, square=True):
            out = []
            for uu in range(KT // 2):
                hi, lo, u = weights()
                for j in range(2):
                    k = 2 * uu + j
                    b, i = dense.take(PE)
                    m = to_features(act, kts, (hi, lo), columns(j * P), n, b)
                    if j:
                        weights_done(u, m)
                    DV.wait(m)
                    e = DV.did(nc.vector.tensor_tensor(dest(X[:, k, 0:n], n), feature_view(b, n), dest(X[:, k, 0:n], n), ALU.add))
                    dense.free(i, e)
                    if square:
                        add_square(k, n, e)
                    else:
                        DV.wait(e)
            return out

        add_residual(Hs, KT, S)

        stage("ffn")
        c = R + 3 * 8192 + 4 * TT * MH * (MD + 1)
        p_rows, c = place("p_rows", [P, TT, PLE], F32, c)
        Hs = rms_norm_split("ln2", S)
        fence()
        p_in = small(p_rows[:, :, :], A["p"].rearrange("(t q) d -> q t d", q=P))
        c = R
        NB = 3
        conv, acc_, th = [None] * NB, [None] * NB, [None] * NB
        for n in range(NB):
            conv[n], c = place(f"conv_in{n}", [P, S + 2], F32, c)
            acc_[n], c = place(f"conv_out{n}", [P, S], F32, c)
            th[n], c = place(f"conv_tanh{n}", [P, S], F32, c)
        gate, c = place("ple_gate", [P, 2, S], F32, c)
        assert c <= R + 3 * 8192 + 4 * TT * MH * (MD + 1)
        zero = [PO.did(nc.gpsimd.memset(conv[n][:, 0:2], 0.0)) for n in range(NB)]
        DV.wait(*zero)
        cv_s = Slots(list(range(NB)))
        for part in range(2):
            g_ready = []

            def ffn_in(jj):
                j = part * KT + jj
                hi, lo, u = weights()
                (bg, ig), (bv, iv) = dense.take(PE), dense.take(PE)
                if part == 0 and jj == 0:
                    mg = mvv = tiles_to_features(Hs, KT, (hi, lo), [columns(0), columns(P)], S, [bg, bv])
                else:
                    mg = to_features(Hs, KT, (hi, lo), columns(0), S, bg)
                    mvv = to_features(Hs, KT, (hi, lo), columns(P), S, bv)
                weights_done(u, mvv)
                n, ni = cv_s.take(AC)
                AC.wait(mg)
                e1 = AC.did(nc.scalar.activation(conv[n][:, 2:S + 2], bank[:, bg, :], ACT.Copy))
                e2 = AC.did(nc.scalar.activation(acc_[n][:, :], bank[:, bg, :], ACT.Identity, scale=param("conv_w", 32 + j),
                                                 bias=param("conv_b", j)))
                dense.free(ig, e2)
                DV.wait(e1, e2)
                e = DV.did(nc.vector.scalar_tensor_tensor(acc_[n][:, :], conv[n][:, 1:S + 1], param("conv_w", 16 + j), acc_[n][:, :],
                                                          ALU.mult, ALU.add))
                DV.wait(e)
                e = DV.did(nc.vector.scalar_tensor_tensor(acc_[n][:, :], conv[n][:, 0:S], param("conv_w", j), acc_[n][:, :],
                                                          ALU.mult, ALU.add))
                AC.wait(e)
                e = AC.did(nc.scalar.activation(th[n][:, :], acc_[n][:, :], ACT.Tanh, scale=0.5))
                live[jj] = (n, ni, bv, iv, mvv, e)

            def ffn_gate(jj):
                n, ni, bv, iv, mvv, e = live.pop(jj)
                DV.wait(e)
                e = DV.did(nc.vector.scalar_tensor_tensor(th[n][:, :], th[n][:, :], 1.0, acc_[n][:, :], ALU.add, ALU.mult))
                DV.wait(e, mvv)
                e = DV.did(nc.vector.scalar_tensor_tensor(th[n][:, :], th[n][:, :], 0.5, bank[:, bv, :], ALU.mult, ALU.mult))
                dense.free(iv, e)
                if jj == 0 and part:
                    AC.wait(g_read)
                    DV.wait(g_read)
                got = split_into(G_hi[:, jj, 0:S], G_lo[:, jj, 0:S], th[n][:, :], e)
                cv_s.free(ni, *got)
                g_ready.append(got)

            pipeline(list(range(KT)), ffn_in, ffn_gate)
            add_residual((G_hi, G_lo, g_ready), KT, S, square=part == 1)
            g_read = PE.last

        stage("ple")
        PE.wait(p_in)
        AC.wait(g_read)
        DV.wait(g_read)
        marks = []
        for k in range(2):
            b, i = dense.take(PE)
            for t in range(TT):
                ins = nc.tensor.transpose(bank[:, b, t * P:(t + 1) * P], p_rows[:, t, k * P:(k + 1) * P], ident[:, :])
            m = PE.did(ins)
            got = split_into(G_hi[:, k, 0:S], G_lo[:, k, 0:S], bank[:, b, :], m)
            dense.free(i, *got)
            marks.append(got)
        Gs = (G_hi, G_lo, marks)
        Hs = rms_norm_split("ple", S)
        gfree = [(), ()]
        for q in range(4):
            hi, lo, u = weights()
            gm = []
            got = [dense.take(PE), dense.take(PE)]
            m = tiles_to_features(Hs, KT, (hi, lo), [columns(0), columns(P)], S, [got[0][0], got[1][0]])
            weights_done(u, m)
            for j, (b, i) in enumerate(got):
                AC.wait(m, *gfree[j])
                e = AC.did(nc.scalar.activation(gate[:, j, :], bank[:, b, :], ACT.Tanh, scale=0.5))
                dense.free(i, e)
                gm.append(e)
            hi, lo, u = weights()
            for j in range(2):
                k = 2 * q + j
                b, i = dense.take(PE)
                m = to_features(Gs, 2, (hi, lo), columns(j * P), S, b)
                if j:
                    weights_done(u, m)
                DV.wait(gm[j], m)
                e = DV.did(nc.vector.scalar_tensor_tensor(gate[:, j, :], gate[:, j, :], 1.0, bank[:, b, :], ALU.add, ALU.mult))
                dense.free(i, e)
                DV.wait(e)
                e = DV.did(nc.vector.scalar_tensor_tensor(X[:, k, 0:S], gate[:, j, :], 0.5, X[:, k, 0:S], ALU.mult, ALU.add))
                gfree[j] = (e,)
                add_square(k, S, e)

        stage("between")
        c = R + 3 * 8192 + 4 * TT * MH * (MD + 1)
        meta, c = place("meta_rows", [META, D], F32, c)
        SP.wait(*marks[0], *marks[1])
        meta_in = small(meta[:, :], A["meta"][:, :])
        PE.wait(meta_in)
        b, i = dense.take(PE)
        for k in range(KT):
            ins = nc.tensor.transpose(bank[:, b, k * META:(k + 1) * META], meta[:, k * P:(k + 1) * P], ident[0:META, 0:META])
        m = PE.did(ins)
        AC.wait(m)
        e = AC.did(nc.scalar.activation(X[:, :, S:T2], bank[:, b, 0:KT * META].rearrange("p (k m) -> p k m", k=KT), ACT.Copy))
        dense.free(i, e)
        meta_done = e
        r = reciprocal_root(S)
        yfree = [(), ()]
        for k in range(KT):
            DV.wait(r, *yfree[k % 2], *gfree[0], *gfree[1])
            Y = gate[:, k % 2, :]
            e = DV.did(nc.vector.scalar_tensor_tensor(Y, X[:, k, 0:S], param("fin1", k), bank[:, 4, :], ALU.mult, ALU.mult))
            AC.wait(e)
            e = AC.did(nc.scalar.activation(X[:, k, 0:S].rearrange("p (c r) -> p r c", r=ROWS),
                                            Y.rearrange("p (r c) -> p r c", r=ROWS), ACT.Copy))
            yfree[k % 2] = (e,)
            add_square(k, T2, e, meta_done)

        def slots(buffers, *marks):
            ring = Slots(buffers)
            ring.free_at = [marks for _ in buffers]
            return ring

        pair_of = [(x // 2, x % 2) for x in range(AH)]
        c = R_END - 3 * 2 * 2 * P - 2 * P
        c -= c % 64
        mask_at = c
        maskb, c = place("na_mask16", [P, 3, 2 * P], BF16, c)
        idb, c = place("ident16", [P, P], BF16, c)
        masks, _ = place("na_masks", [P, 3, 2 * P], F32, R)
        fence()
        for n, name in enumerate(("na_first", "na_inner", "na_last")):
            masks_in = table(name, masks[:, n, :])
        PO.wait(masks_in)
        PO.did(nc.gpsimd.tensor_copy(maskb[:, :, :], masks[:, :, :]))
        PO.did(nc.gpsimd.tensor_copy(idb[:, :], ident[:, :]))

        for layer in range(2):
            L = "ab"[layer]
            last = layer == 1
            nq = TT if last else TT + 1
            n_out = S if last else T2
            stage(f"qkv_{L}")
            fence()
            oa_hi, g_c = place(f"oa_hi_{L}", [P, 4, T2], F32R, g_at)
            oa_lo, g_c = place(f"oa_lo_{L}", [P, 4, T2], F32R, g_c)
            ob_at = g_c
            ob_hi, g_c = place(f"ob_hi_{L}", [P, 4, T2], F32R, g_c)
            ob_lo, g_c = place(f"ob_lo_{L}", [P, 4, T2], F32R, g_c)
            vb, c = place(f"vb_{L}", [P, 5, NH * AD], F32, ob_at)
            cos, c = place(f"cos_{L}", [P, T2], F32, c)
            sin, c = place(f"sin_{L}", [P, T2], F32, c)
            v_own, c = place(f"v_own_{L}", [P, NH * AD], F32, c)
            assert c <= ob_at + 2 * 4 * 4 * T2
            qT, c = place(f"q_{L}", [P, 4, T2], F32, R)
            kT, c = place(f"k_{L}", [P, T2], F32, c)
            va, c = place(f"va_{L}", [P, 5, KW], F32, c)
            qb, c = place(f"qb_{L}", [P, 4, T2], F32, c)
            kb, c = place(f"kb_{L}", [P, 4, T2], F32, c)
            z, c = place(f"z_{L}", [P, 4, T2], F32, c)
            orow, c = place(f"o_rows_{L}", [P, TT, NH * AD], F32, c)
            omT, c = place(f"o_meta_features_{L}", [P, 4, META], F32, c)
            k_own, c = place(f"k_own_{L}", [P, 4, 2 * META], F32, c)
            q_own, c = place(f"q_own_{L}", [P, P], F32, c)
            sq_own, c = place(f"sq_own_{L}", [P, P], F32, c)
            pm, pmT = [None] * 2, [None] * 2
            for n in range(2):
                pm[n], c = place(f"meta_probs{n}_{L}", [P, AH, META], F32, c)
                pmT[n], c = place(f"meta_probsT{n}_{L}", [P, P], F32, c)
            stat, c = place(f"attn_stats_{L}", [P, 2, 6, AH], F32, c)
            rs, c = place(f"q_rms_{L}", [P, 2, TT + 1, AH], F32, c)
            ks, c = place(f"k_rms_{L}", [P, 2, TT + 1, 2], F32, c)
            tail = c
            rsin, c = place(f"rot_sin_{L}", [P, T2], F32, c)
            assert c <= mask_at, (c, mask_at)
            tiles2 = [(t * P, P) for t in range(TT)] + [(S, META)]

            table("cos", cos[:, :])
            rope_in = table("sin", sin[:, :])
            PO.did(nc.gpsimd.memset(ks[:, :, :, :], 1.0))
            PO.did(nc.gpsimd.memset(rs[:, :, :, :], 1.0))
            PO.did(nc.gpsimd.memset(k_own[:, :, :], 0.0))
            PO.did(nc.gpsimd.memset(q_own[:, :], 0.0))
            zeroed = PO.did(nc.gpsimd.memset(sq_own[:, :], 0.0))
            dense = Slots([0, 2])
            Hs = rms_norm_split(f"norm_{L}", T2)

            squares, gained = (sq[0], sq[1]), (tmp, acc)
            rope_free = [(PE.last, *Hs[2][-1], *Hs[2][-2], *Hs[2][-3])] * 2
            rope_n = [0]
            turned = slots([4], *Hs[2][-1])

            def rope(dst, b, i, m, gain, sums):
                n = rope_n[0] % 2
                rope_n[0] += 1
                sq_, g_ = squares[n], gained[n]
                fv = feature_view(b, T2)
                AC.wait(m, *rope_free[n])
                e1 = AC.did(nc.scalar.activation(dest(sq_[:, :], T2), fv, ACT.Square))
                e2 = AC.did(nc.scalar.activation(dest(g_[:, :], T2), fv, ACT.Copy, scale=param(gain)))
                dense.free(i, e2)
                b4, i4 = turned.take(PE)
                PE.wait(e1)
                m_sum = sums(sq_)
                PE.wait(e2)
                for c_, (a_, z_) in enumerate(chunks(T2)):
                    ins = nc.tensor.matmul(bank[:, b4 + c_, 0:HALF], rot[:, :], g_[:, a_:z_], start=True, stop=True)
                m_rot = PE.did(ins)
                DV.wait(e2, rope_in)
                t1 = DV.did(nc.vector.tensor_tensor(dst, g_[:, :], cos[:, :], ALU.mult))
                DV.wait(m_rot, *rope_done)
                t2 = DV.did(nc.vector.tensor_tensor(dest(rsin[:, :], T2), bank[:, 4:6, 0:HALF], dest(sin[:, :], T2), ALU.mult))
                turned.free(i4, t2)
                DV.wait(t2, t1)
                t1 = DV.did(nc.vector.tensor_tensor(dst, dst, rsin[:, :], ALU.add))
                rope_done[:] = [t1]
                rope_free[n] = (m_sum, m_rot, t1)
                return e1, m_sum, t1

            rope_done = []
            hi, lo, u = weights()
            b, i = dense.take(PE)
            m = to_features(Hs, KT, (hi, lo), columns(0), T2, b)
            bv, iv = dense.take(PE)
            for t, (t0, tn) in enumerate(tiles2):
                out = bank[:, bv, t * KW:(t + 1) * KW] if t < TT else bank[0:META, bv + 1, 0:KW]
                mv_ = to_tokens(Hs, t0, tn, (hi, lo), P, KW, out)
            weights_done(u, mv_)

            def k_sums(sq_):
                for t, (t0, tn) in enumerate(tiles2):
                    ins = nc.tensor.matmul(bank[0:tn, 7, 2 * t:2 * t + 2], sq_[:, t0:t0 + tn], hsel, start=True, stop=True)
                return PE.did(ins)

            _, m_sum, k_rot = rope(kT[:, :], b, i, m, f"kg_{L}", k_sums)
            e1 = evacuate(va[:, 0:TT, :], bank[:, bv, :].rearrange("p (t c) -> p t c", t=TT), mv_)
            v_in = evacuate(va[0:META, TT, :], bank[0:META, bv + 1, 0:KW], mv_)
            dense.free(iv, v_in)
            DV.wait(m_sum, zeroed)
            e = DV.did(nc.vector.tensor_scalar(ks[:, 0, 0:TT, :], bank[:, 7, 0:2 * TT].rearrange("p (t g) -> p t g", t=TT),
                                               1.0 / AD, EPS, ALU.mult, ALU.add))
            e = DV.did(nc.vector.tensor_scalar(ks[0:META, 0, TT, :], bank[0:META, 7, 2 * TT:2 * TT + 2], 1.0 / AD, EPS,
                                               ALU.mult, ALU.add))
            sums_read = [e]
            PO.wait(e)
            k_pow = PO.did(nc.gpsimd.tensor_tensor(ks[:, 1, :, :], ks[:, 0, :, :],
                                                   half[:, 0:2 * TT + 2].rearrange("p (t g) -> p t g", g=2), ALU.pow))

            def q_sums(j):
                def f(sq_):
                    PE.wait(sums_read[-1])
                    for t in range(TT):
                        at = 16 + t * AH + 2 * j
                        ins = nc.tensor.matmul(bank[:, 7, at:at + 2], sq_[:, t * P:(t + 1) * P], hsel, start=True, stop=True)
                    return PE.did(ins)
                return f

            q_rot = []
            for a in range(2):
                hi, lo, u = weights()
                for jj in range(2):
                    j = 2 * a + jj
                    b, i = dense.take(PE)
                    m = to_features(Hs, KT, (hi, lo), columns(jj * P), T2, b)
                    if jj:
                        weights_done(u, m)
                    e1, m_sum, e = rope(qT[:, j, :], b, i, m, f"qg_{L}", q_sums(j))
                    q_rot.append(e)
                    if not last:
                        DV.wait(e1, zeroed)
                        for g in range(2):
                            rows = slice(g * AD, (g + 1) * AD)
                            at = g * AD + j * META
                            e = DV.did(nc.vector.tensor_copy(sq_own[rows, at:at + META], squares[(rope_n[0] - 1) % 2][rows, S:T2]))
                        rope_free[(rope_n[0] - 1) % 2] += (e,)
                    if a == 0 and jj == 0:
                        kw = z[:, :, 0:P]
                        DV.wait(k_pow)
                        e = DV.did(nc.vector.tensor_copy(kw.rearrange("p t (g d) -> p t g d", g=2),
                                                         ks[:, 1, 0:TT, :].unsqueeze(3).broadcast_to([P, TT, 2, AD])))
                        e = DV.did(nc.vector.tensor_copy(z[:, 0, P:2 * P].rearrange("p (g d) -> p g d", g=2),
                                                         ks[:, 1, TT, :].unsqueeze(2).broadcast_to([P, 2, AD])))
                        b4, i4 = turned.take(PE)
                        PE.wait(e)
                        for t in range(TT):
                            nc.tensor.transpose(bank[:, b4, t * P:(t + 1) * P], kw[:, t, :], ident[:, :])
                        m = PE.did(nc.tensor.transpose(bank[:, b4 + 1, 0:META], z[0:META, 0, P:2 * P], ident[0:META, 0:META]))
                        DV.wait(m, k_rot)
                        DV.did(nc.vector.tensor_tensor(kT[:, 0:S], kT[:, 0:S], bank[:, b4, :], ALU.mult))
                        k_done = DV.did(nc.vector.tensor_tensor(kT[:, S:T2], kT[:, S:T2], bank[:, b4 + 1, 0:META], ALU.mult))
                        turned.free(i4, k_done)
                cols = slice(4 * a, 4 * a + 4)
                DV.wait(m_sum)
                e = DV.did(nc.vector.tensor_scalar(rs[:, 0, 0:TT, cols], bank[:, 7, 16:16 + TT * AH].rearrange("p (t x) -> p t x", t=TT)[:, :, cols],
                                                   AD * EPS, None, ALU.add))
                sums_read.append(e)
                PO.wait(e)
                q_pow = PO.did(nc.gpsimd.tensor_tensor(rs[:, 1, 0:TT, cols], rs[:, 0, 0:TT, cols],
                                                       half[:, 0:4 * TT].rearrange("p (t x) -> p t x", t=TT), ALU.pow))
            AC.wait(k_done, zeroed)
            for g in range(2):
                rows = slice(g * AD, (g + 1) * AD)
                k_own_in = AC.did(nc.scalar.activation(k_own[rows, 0, g * META:(g + 1) * META], kT[rows, S:T2], ACT.Copy))
            b, i = dense.take(PE)
            PE.wait(v_in)
            m = PE.did(nc.tensor.matmul(bank[:, b, 0:KW], spread[0:META, :], va[0:META, TT, :], start=True, stop=True))
            DV.wait(m)
            for g in range(2):
                v_own_in = DV.did(nc.vector.tensor_tensor(
                    v_own[:, g * 4 * AD:(g + 1) * 4 * AD].rearrange("p (h d) -> p h d", h=4),
                    bank[:, b, g * AD:(g + 1) * AD].unsqueeze(1).broadcast_to([P, 4, AD]),
                    own_pair[:, 4 * g:4 * g + 4].unsqueeze(2).broadcast_to([P, 4, AD]), ALU.mult))
            dense.free(i, v_own_in)
            if not last:
                AC.wait(*q_rot)
                for g in range(2):
                    rows = slice(g * AD, (g + 1) * AD)
                    q_own_in = AC.did(nc.scalar.activation(q_own[rows, g * AD:(g + 1) * AD].rearrange("p (j m) -> p j m", j=4),
                                                           qT[rows, :, S:T2], ACT.Copy))

            stage(f"gqa_{L}")
            fence()
            dense = Slots([0])
            c = work_at
            pr_s, pt_s = [None] * 3, [None] * 3
            for n in range(2):
                pr_s[n], c = place(f"gqa_probs{n}_{L}", [P, S], F32, c)
                pt_s[n], c = place(f"gqa_probsT{n}_{L}", [P, TT, P], F32, c)
            assert c <= R
            pr_s[2], c = place(f"gqa_probs2_{L}", [P, S], F32, tail)
            pt_s[2], c = place(f"gqa_probsT2_{L}", [P, TT, P], F32, c)
            assert c <= mask_at, (c, mask_at)
            pr, pt, scores, turned, outb = Slots(pr_s), Slots(pt_s), Slots([2, 3]), Slots([4, 5]), Slots([6])
            shifted = [(0, 64)] + [(64 + P * t, P) for t in range(3)] + [(S - 64, 64 + META)]
            done.clear()

            def z_steps(marks_out):
                for a in range(2):
                    hi, lo, u = weights()
                    for jj in range(2):
                        k = 2 * a + jj
                        b, i = dense.take(PE)
                        m = to_features(Hs, KT, (hi, lo), columns(jj * P), n_out, b)
                        if jj:
                            weights_done(u, m)
                        zs = dest(z[:, k, 0:n_out], n_out)
                        AC.wait(m, *z_free)
                        e = AC.did(nc.scalar.activation(zs, feature_view(b, n_out), ACT.Tanh, scale=0.5))
                        DV.wait(e, m)
                        e = DV.did(nc.vector.scalar_tensor_tensor(zs, zs, 1.0, feature_view(b, n_out), ALU.add, ALU.mult))
                        dense.free(i, e)
                        marks_out.append(e)
                        yield

            def qkv_b_steps():
                for a in range(2):
                    yield from features_steps([qb[:, 2 * a + j, :] for j in range(2)], T2, Hs, scale=AD ** -0.5)
                for a in range(2):
                    yield from features_steps([kb[:, 2 * a + j, :] for j in range(2)], T2, Hs)
                for a in range(2):
                    yield from tokens_steps(lambda t: (vb[0:shifted[t][1], t, 256 * a:256 * a + 256], lambda x: x), shifted, Hs)

            z_free = ()
            z_marks = []
            fill = all_of(z_steps(z_marks), qkv_b_steps())
            live = {}
            tile_done = {-2: (), -1: ()}
            bank7_read = [()]

            def meta_scores(t, qn, q_of, k_of):
                at = t % 2 * P
                PE.wait(*tile_done[t - 2], *bank7_read[0])
                for j in range(4):
                    ins = nc.tensor.matmul(bank[0:qn, 7, at + 2 * META * j:at + 2 * META * (j + 1)], q_of(j), k_of(j),
                                           start=True, stop=True)
                m = PE.did(ins)
                DV.wait(m, *tile_done[t - 2])
                AC.wait(*tile_done[t - 2])
                sm = bank[0:qn, 7, at:at + P].rearrange("p (x m) -> p x m", x=AH)
                live["meta", t] = DV.did(nc.vector.reduce_max(stat[0:qn, t % 2, 4, :], sm, AX.X, negate=True))
                bank7_read[0] = (live["meta", t],)

            def meta_probs(t, qn, *ready, scale=None):
                at, st, pm_ = t % 2 * P, stat[0:qn, t % 2, :, :], pm[t % 2]
                sm = bank[0:qn, 7, at:at + P].rearrange("p (x m) -> p x m", x=AH)
                DV.wait(*ready)
                e = None
                if scale is not None:
                    e = DV.did(nc.vector.tensor_tensor(pm_[0:qn, :, :], sm, scale.unsqueeze(2).broadcast_to([qn, AH, META]), ALU.mult))
                    DV.wait(e)
                    sm = pm_[0:qn, :, :]
                e = DV.did(nc.vector.tensor_tensor(pm_[0:qn, :, :], sm, st[:, 1, :].unsqueeze(2).broadcast_to([qn, AH, META]), ALU.add))
                bank7_read[0] = (e,)
                AC.wait(e)
                e = AC.did(nc.scalar.activation(pm_[0:qn, :, :], pm_[0:qn, :, :], ACT.Exp))
                DV.wait(e)
                live["meta sum", t] = DV.did(nc.vector.reduce_sum(st[:, 3, :], pm_[0:qn, :, :], AX.X))
                live["meta exp", t] = e

            def meta_turn(t, qn):
                at = 2 * P + t % 2 * P
                PE.wait(live.pop(("meta exp", t)), *bank7_read[0])
                m = PE.did(nc.tensor.transpose(bank[:, 7, at:at + qn], pm[t % 2][0:qn, :, :].rearrange("p x m -> p (x m)"),
                                               ident[0:qn, 0:qn]))
                live["meta turned", t] = evacuate(pmT[t % 2][:, 0:qn], bank[:, 7, at:at + qn], m)
                bank7_read[0] = (live["meta turned", t],)

            def tile_out(t, qn, ob, oi, first, dst, natural, ready):
                st = stat[0:qn, t % 2, :, :]
                PE.wait(live.pop(("meta turned", t)))
                m = PE.did(nc.tensor.matmul(bank[0:qn, ob, 0:NH * AD], pmT[t % 2][:, 0:qn], v_own[:, :], start=first, stop=True,
                                            skip_group_check=True))
                DV.wait(live.pop(("meta sum", t)), *ready)
                if first:
                    src = st[:, 3, :]
                else:
                    src = st[:, 5, :]
                    e = DV.did(nc.vector.tensor_tensor(src, st[:, 2, :], st[:, 3, :], ALU.add))
                    DV.wait(e)
                e = DV.did(nc.vector.reciprocal(src, src))
                DV.wait(e, m)
                by_head = (src if natural else src.rearrange("p (j g) -> p g j", g=2))
                if natural:
                    e = DV.did(nc.vector.tensor_tensor(dst.rearrange("p (h d) -> p h d", h=AH),
                                                       bank[0:qn, ob, 0:NH * AD].rearrange("p (h d) -> p h d", h=AH),
                                                       by_head.unsqueeze(2).broadcast_to([qn, AH, AD]), ALU.mult))
                else:
                    for g in range(2):
                        half_ = slice(g * 4 * AD, (g + 1) * 4 * AD)
                        e = DV.did(nc.vector.tensor_tensor(dst[:, half_].rearrange("p (h d) -> p h d", h=4),
                                                           bank[0:qn, ob, half_].rearrange("p (h d) -> p h d", h=4),
                                                           by_head[:, g, :].unsqueeze(2).broadcast_to([qn, 4, AD]), ALU.mult))
                outb.free(oi, e)
                tile_done[t] = (e,)
                return e

            def gqa_meta(t):
                meta_scores(t, P, lambda j: qT[:, j, t * P:(t + 1) * P], lambda j: k_own[:, 0, :])

            def gqa_score(item):
                t, x = item
                j, g = pair_of[x]
                rows = slice(AD * g, AD * g + AD)
                st = stat[:, t % 2, :, :]
                if item == (0, 0):
                    gqa_meta(0)
                if x == 4 and t + 1 < TT:
                    gqa_meta(t + 1)
                b, i = scores.take(PE)
                m = PE.did(nc.tensor.matmul(bank[:, b, :], qT[rows, j, t * P:(t + 1) * P], kT[rows, 0:S], start=True, stop=True))
                DV.wait(m)
                e = DV.did(nc.vector.reduce_max(st[:, 0, x:x + 1], bank[:, b, :], AX.X, negate=True))
                DV.wait(e, live["meta", t])
                e = DV.did(nc.vector.scalar_tensor_tensor(st[:, 1, x:x + 1], st[:, 0, x:x + 1], st[:, 4, x:x + 1],
                                                          rs[:, 1, t, x:x + 1], ALU.min, ALU.mult))
                p_, pi = pr.take(AC)
                AC.wait(e, m)
                e2 = AC.did(nc.scalar.activation(p_[:, :], bank[:, b, :], ACT.Exp, bias=st[:, 1, x:x + 1],
                                                 scale=rs[:, 1, t, x:x + 1], accum_out=st[:, 2, x:x + 1]))
                scores.free(i, e2)
                live[item] = (p_, pi, e2)
                if x == AH - 1:
                    meta_probs(t, P, e, scale=rs[:, 1, t, :])

            def gqa_turn(item):
                t, x = item
                p_, pi, ready = live[item]
                b, i = turned.take(PE)
                PE.wait(ready)
                for k in range(TT):
                    ins = nc.tensor.transpose(bank[:, b, k * P:(k + 1) * P], p_[:, k * P:(k + 1) * P], ident[:, :])
                m = PE.did(ins)
                pr.free(pi, m)
                lane = DV if x % 2 else AC
                q_, qi = pt.take(lane)
                e = evacuate(q_[:, :, :].rearrange("p k q -> p (k q)"), bank[:, b, :], m, None, lane)
                turned.free(i, e)
                live[item] = (q_, qi, e, ready)
                if x == AH - 1:
                    meta_turn(t, P)

            def gqa_value(item):
                t, x = item
                j, g = pair_of[x]
                h = 4 * g + j
                q_, qi, e, ready = live.pop(item)
                if x == 0:
                    live["o"] = outb.take(PE)
                ob, oi = live["o"]
                PE.wait(e)
                for k in range(TT):
                    ins = nc.tensor.matmul(bank[:, ob, h * AD:(h + 1) * AD], q_[:, k, :], va[:, k, g * AD:(g + 1) * AD],
                                           start=x == 0 and k == 0, stop=False, skip_group_check=True)
                m = PE.did(ins)
                pt.free(qi, m)
                if x == AH - 1:
                    tile_out(t, P, ob, oi, False, orow[:, t, :], False, [ready])

            def filled(items, total, stages_):
                given = [0]

                def give(item):
                    n = items.index(item) + 1
                    while given[0] < total * n // len(items):
                        next(fill, None)
                        given[0] += 1
                pipeline(items, stages_[0], give, *stages_[1:])

            filled([(t, x) for t in range(TT) for x in range(AH)], 22, (gqa_score, gqa_turn, gqa_value))
            drain(fill)
            om_in = None
            PE.wait(*bank7_read[0])
            if not last:
                b, i = scores.take(PE)
                b5, i5 = turned.take(PE)
                PE.wait(*tile_done[TT - 1], *tile_done[TT - 2])
                nc.tensor.matmul(bank[:, b, :], q_own[:, :], kT[:, 0:S], start=True, stop=True)
                nc.tensor.matmul(bank[:, 7, 0:META], q_own[:, :], kT[:, S:T2], start=True, stop=True)
                m = PE.did(nc.tensor.matmul(bank[:, 7, META:META + 1], sq_own[:, :], ones[:, 0:1], start=True, stop=True))
                DV.wait(m, *tile_done[TT - 1], *tile_done[TT - 2])
                AC.wait(*tile_done[TT - 1], *tile_done[TT - 2])
                st = stat[:, 0, :, :]
                DV.did(nc.vector.reduce_max(st[:, 0, 0:1], bank[:, b, :], AX.X, negate=True))
                DV.did(nc.vector.reduce_max(st[:, 0, 1:2], bank[:, 7, 0:META], AX.X, negate=True))
                e = DV.did(nc.vector.tensor_scalar(st[:, 0, 2:3], bank[:, 7, META:META + 1], AD * EPS, None, ALU.add))
                PO.wait(e)
                e = PO.did(nc.gpsimd.tensor_tensor(st[:, 0, 3:4], st[:, 0, 2:3], half[:, 0:1], ALU.pow))
                DV.wait(e)
                e = DV.did(nc.vector.scalar_tensor_tensor(st[:, 1, 0:1], st[:, 0, 0:1], st[:, 0, 1:2], st[:, 0, 3:4], ALU.min, ALU.mult))
                p_, pi = pr.take(AC)
                AC.wait(e)
                AC.did(nc.scalar.activation(p_[:, :], bank[:, b, :], ACT.Exp, bias=st[:, 1, 0:1], scale=st[:, 0, 3:4],
                                            accum_out=st[:, 2, 0:1]))
                e2 = AC.did(nc.scalar.activation(pm[0][:, 0, :], bank[:, 7, 0:META], ACT.Exp, bias=st[:, 1, 0:1], scale=st[:, 0, 3:4],
                                                 accum_out=st[:, 2, 1:2]))
                scores.free(i, e2)
                DV.wait(e2)
                e = DV.did(nc.vector.tensor_tensor(st[:, 2, 2:3], st[:, 2, 0:1], st[:, 2, 1:2], ALU.add))
                DV.wait(e)
                e = DV.did(nc.vector.reciprocal(st[:, 2, 3:4], st[:, 2, 2:3]))
                PE.wait(e2)
                for k in range(TT):
                    nc.tensor.transpose(bank[:, b5, k * P:(k + 1) * P], p_[:, k * P:(k + 1) * P], ident[:, :])
                m = PE.did(nc.tensor.transpose(bank[0:META, 7, P:2 * P], pm[0][:, 0, :], ident[:, :]))
                pr.free(pi, m)
                q_, qi = pt.take(AC)
                e3 = evacuate(q_[:, :, :].rearrange("p k q -> p (k q)"), bank[:, b5, :], m)
                e3 = evacuate(pmT[0][0:META, :], bank[0:META, 7, P:2 * P], m)
                turned.free(i5, e3)
                ob, oi = outb.take(PE)
                PE.wait(e3)
                for k in range(TT):
                    nc.tensor.matmul(bank[:, ob, 0:KW], q_[:, k, :], va[:, k, :], start=k == 0, stop=False)
                m = PE.did(nc.tensor.matmul(bank[:, ob, 0:KW], pmT[0][0:META, :], va[0:META, TT, :], start=False, stop=True))
                pt.free(qi, m)
                q_, qi = pt.take(DV)
                DV.wait(m, e)
                for g in range(2):
                    rows = slice(g * AD, (g + 1) * AD)
                    for n in range(2):
                        e = DV.did(nc.vector.tensor_scalar(q_[rows, 0, n * AD:(n + 1) * AD], bank[rows, ob, g * AD:(g + 1) * AD],
                                                           st[rows, 2, 3:4], None, ALU.mult))
                outb.free(oi, e)
                b5, i5 = turned.take(PE)
                PE.wait(e)
                m = PE.did(nc.tensor.transpose(bank[:, b5, 0:P], q_[:, 0, :], ident[:, :]))
                pt.free(qi, m)
                for n in range(2):
                    rows = slice(n * AD, (n + 1) * AD)
                    om_in = evacuate(omT[rows, :, :].rearrange("p (g jj) m -> p g jj m", g=2),
                                     bank[rows, b5, 0:P].rearrange("p (g jj n m) -> p n g jj m", g=2, jj=2, n=2)[:, n, :, :, :], m)
                turned.free(i5, om_in)

            def gated_features(hi_dst, lo_dst, meta_of, z_marks):
                marks = []
                for k in range(4):
                    b, i = turned.take(PE)
                    for t in range(TT):
                        ins = nc.tensor.transpose(bank[:, b, t * P:(t + 1) * P], orow[:, t, k * P:(k + 1) * P], ident[:, :])
                    m = PE.did(ins)
                    zk = z[:, k, 0:n_out]
                    DV.wait(m, z_marks[k])
                    e = DV.did(nc.vector.scalar_tensor_tensor(z[:, k, 0:S], z[:, k, 0:S], 0.5, bank[:, b, :], ALU.mult, ALU.mult))
                    turned.free(i, e)
                    if n_out > S:
                        src, mm = meta_of(k)
                        DV.wait(mm)
                        e = DV.did(nc.vector.scalar_tensor_tensor(z[:, k, S:T2], z[:, k, S:T2], 0.5, src, ALU.mult, ALU.mult))
                    marks.append(split_into(hi_dst[:, k, 0:n_out], lo_dst[:, k, 0:n_out], zk, e, lane=PO if k % 2 else DV))
                return marks

            PE.wait(*tile_done[TT - 1], *tile_done[TT - 2])
            oa_marks = gated_features(oa_hi, oa_lo, lambda k: (omT[:, k, :], om_in), z_marks)

            stage(f"na_{L}")
            fence()
            bias, c = place(f"na_bias_{L}", [P, NH, 2 * P], F32, R)
            assert c <= R + 4 * 4 * T2
            bias_in = new_sem(f"na_bias_in_{L}")
            for cc in range(QB):
                off = (NAW - 1 - cc) * ROWS
                nc.sync.dma_start(bias[cc * ROWS:(cc + 1) * ROWS, :, :],
                                  A["na_rel"][layer, :, :, off:off + 2 * P].rearrange("h r x -> r h x")).then_inc(bias_in, 16)
            b_in = (bias_in, 16 * QB)
            ometa, c = place(f"o_meta_{L}", [META, NH * AD], F32, R + 4 * 4 * T2)
            c = work_at
            pr_s, pt_s = [None] * 4, [None] * 2
            for n in range(2):
                pr_s[n], c = place(f"na_probs{n}_{L}", [P, 2, 2 * P], F32, c)
                pt_s[n], c = place(f"na_probsT{n}_{L}", [P, 4, P], F32, c)
            assert c <= R
            c = tail
            for n in range(2, 4):
                pr_s[n], c = place(f"na_probs{n}_{L}", [P, 2, 2 * P], F32, c)
            assert c <= mask_at
            pr, pt, scores, turned, outb = Slots(pr_s), Slots(pt_s), Slots([2, 3]), Slots([4, 5]), Slots([6])
            for n in range(2):
                rows = slice(n * AD, (n + 1) * AD)
                k_own_in = AC.did(nc.scalar.activation(k_own[rows, :, n * META:(n + 1) * META], kb[rows, :, S:T2], ACT.Copy))
            b, i = outb.take(PE)
            m = PE.did(nc.tensor.matmul(bank[:, b, :], spread[64:64 + META, :], vb[64:64 + META, 4, :], start=True, stop=True))
            DV.wait(m)
            v_own_in = DV.did(nc.vector.tensor_tensor(v_own[:, :].rearrange("p (h d) -> p h d", h=NH),
                                                      bank[:, b, :].rearrange("p (h d) -> p h d", h=NH),
                                                      own_head.unsqueeze(2).broadcast_to([P, NH, AD]), ALU.mult))
            outb.free(i, v_own_in)
            PE.wait(k_own_in)
            z_free = (oa_marks[-1] + oa_marks[-2])
            z_marks = []
            fill = z_steps(z_marks)
            tile_done = {-2: (), -1: ()}
            heads2 = [(0, 2), (1, 3), (4, 6), (5, 7)]
            spans = [(0, 192, 64, 0), (64, 256, 0, 1), (192, 256, 0, 1), (320, 192, 0, 2)]
            parts = [[(0, 64, 0), (64, P, 1)], [(0, P, 1), (P, P, 2)], [(0, P, 2), (P, P, 3)], [(0, P, 3), (P, 64, 4)]]

            def na_meta(t):
                meta_scores(t, P, lambda j: qb[:, j, t * P:(t + 1) * P], lambda j: k_own[:, j, :])

            def na_score(item):
                t, y = item
                st = stat[:, t % 2, :, :]
                if item == (0, 0):
                    na_meta(0)
                if y == 3 and t + 1 < TT:
                    na_meta(t + 1)
                k0, kn, m0, which = spans[t]
                b, i = scores.take(PE)
                view = bank[:, b, 0:2 * kn].rearrange("p (n k) -> p n k", n=2)
                nc.tensor.matmul(view, idb[:, :], maskb[:, which, m0:m0 + kn].unsqueeze(1).broadcast_to([P, 2, kn]), start=True,
                                 stop=False, skip_group_check=True)
                for n, h in enumerate(heads2[y]):
                    rows = slice(AD * (h % 2), AD * (h % 2) + AD)
                    ins = nc.tensor.matmul(view[:, n, :], qb[rows, h // 2, t * P:(t + 1) * P], kb[rows, h // 2, k0:k0 + kn],
                                           start=False, stop=True, skip_group_check=True)
                m = PE.did(ins)
                s_, si = pr.take(DV)
                DV.wait(m, b_in)
                for n, h in enumerate(heads2[y]):
                    e = DV.did(nc.vector.tensor_tensor_reduce(s_[:, n, 0:kn], view[:, n, :], bias[:, h, m0:m0 + kn], -1.0, 3e38,
                                                              ALU.add, ALU.min, st[:, 0, h:h + 1]))
                scores.free(i, e)
                two = slice(heads2[y][0], heads2[y][0] + 3, 2)
                DV.wait(e, live["meta", t])
                e1 = DV.did(nc.vector.tensor_tensor(st[:, 1, two], st[:, 0, two], st[:, 4, two], ALU.min))
                AC.wait(e1)
                for n, h in enumerate(heads2[y]):
                    e = AC.did(nc.scalar.activation(s_[:, n, 0:kn], s_[:, n, 0:kn], ACT.Exp, bias=st[:, 1, h:h + 1], scale=-1.0,
                                                    accum_out=st[:, 2, h:h + 1]))
                live[item] = (s_, si, e)
                if y == 3:
                    meta_probs(t, P, e1)

            def na_turn(item):
                t, y = item
                p_, pi, ready = live[item]
                b, i = turned.take(PE)
                PE.wait(ready)
                for r, (p0, pn, _) in enumerate(parts[t]):
                    for n in range(2):
                        at = (2 * r + n) * P
                        ins = nc.tensor.transpose(bank[0:pn, b, at:at + P], p_[:, n, p0:p0 + pn], ident[:, :])
                m = PE.did(ins)
                pr.free(pi, m)
                q_, qi = pt.take(AC, DV)
                es = []
                if parts[t][0][1] == parts[t][1][1]:
                    lane = DV if y % 2 else AC
                    es.append(evacuate(q_[:, :, :].rearrange("p k q -> p (k q)"), bank[:, b, :], m, None, lane))
                else:
                    for r, (p0, pn, _) in enumerate(parts[t]):
                        es.append(evacuate(q_[0:pn, 2 * r:2 * r + 2, :].rearrange("p k q -> p (k q)"),
                                           bank[0:pn, b, 2 * r * P:2 * (r + 1) * P], m))
                turned.free(i, *es)
                live[item] = (q_, qi, es, ready)
                if y == 3:
                    meta_turn(t, P)

            def na_value(item):
                t, y = item
                q_, qi, es, ready = live.pop(item)
                if y == 0:
                    live["o"] = outb.take(PE)
                ob, oi = live["o"]
                PE.wait(*es)
                for n, h in enumerate(heads2[y]):
                    for r, (_, pn, vt) in enumerate(parts[t]):
                        ins = nc.tensor.matmul(bank[:, ob, h * AD:(h + 1) * AD], q_[0:pn, 2 * r + n, :],
                                               vb[0:pn, vt, h * AD:(h + 1) * AD], start=y == 0 and n == 0 and r == 0, stop=False,
                                               skip_group_check=True)
                m = PE.did(ins)
                pt.free(qi, m)
                if y == 3:
                    tile_out(t, P, ob, oi, False, orow[:, t, :], True, [ready])

            filled([(t, y) for t in range(TT) for y in range(4)], 4, (na_score, na_turn, na_value))
            om_in = None
            if not last:
                meta_scores(TT, META, lambda j: qb[:, j, S:T2], lambda j: k_own[:, j, :])
                DV.wait(live["meta", TT])
                e = DV.did(nc.vector.tensor_copy(stat[0:META, 0, 1, :], stat[0:META, 0, 4, :]))
                meta_probs(TT, META, e)
                meta_turn(TT, META)
                ob, oi = outb.take(PE)
                e = tile_out(TT, META, ob, oi, True, ometa[:, :], True, [])
                PE.wait(e)
                for k in range(4):
                    ins = nc.tensor.transpose(bank[:, 7, k * META:(k + 1) * META], ometa[:, k * P:(k + 1) * P],
                                              ident[0:META, 0:META])
                om_in = PE.did(ins)
            drain(fill)
            PE.wait(*tile_done[TT - 1], *tile_done[TT - 2])
            AC.wait(PE.last)
            DV.wait(PE.last)
            PO.wait(PE.last)
            ob_marks = gated_features(ob_hi, ob_lo, lambda k: (bank[:, 7, k * META:(k + 1) * META], om_in), z_marks)

            stage(f"mixed_{L}")
            fence()
            c = R
            M_hi, c = place(f"mixed_hi_{L}", [P, KT, T2], F32R, c)
            M_lo, c = place(f"mixed_lo_{L}", [P, KT, T2], F32R, c)
            sg, c = place(f"gates_{L}", [P, 4, T2], F32, c)
            assert c <= mask_at
            dense = Slots([0, 2, 4, 6])
            sfree = [()] * 4
            first_part = [None, None]
            m_marks = []
            for q in range(4):
                for which, act in ((0, (oa_hi, oa_lo, oa_marks)), (1, (ob_hi, ob_lo, ob_marks))):
                    hi, lo, u = weights()
                    gm = []
                    for j in range(2):
                        b, i = dense.take(PE)
                        m = to_features(Hs, KT, (hi, lo), columns(j * P), n_out, b)
                        if j:
                            weights_done(u, m)
                        sl = 2 * which + j
                        AC.wait(m, *sfree[sl])
                        e = AC.did(nc.scalar.activation(dest(sg[:, sl, 0:n_out], n_out), feature_view(b, n_out), ACT.Tanh, scale=0.5))
                        dense.free(i, e)
                        gm.append(e)
                    hi, lo, u = weights()
                    for j in range(2):
                        k = 2 * q + j
                        sl = 2 * which + j
                        b, i = dense.take(PE)
                        m = to_features(act, 4, (hi, lo), columns(j * P), n_out, b)
                        if j:
                            weights_done(u, m)
                        gs = dest(sg[:, sl, 0:n_out], n_out)
                        DV.wait(gm[j], m)
                        e = DV.did(nc.vector.scalar_tensor_tensor(gs, gs, 1.0, feature_view(b, n_out), ALU.add, ALU.mult))
                        dense.free(i, e)
                        if which == 0:
                            first_part[j] = e
                            continue
                        DV.wait(e, first_part[j])
                        s0 = sg[:, j, 0:n_out]
                        e = DV.did(nc.vector.tensor_tensor(s0, s0, sg[:, sl, 0:n_out], ALU.add))
                        sfree[sl] = (e,)
                        AC.wait(e)
                        a_ = AC.did(nc.scalar.activation(M_hi[:, k, 0:n_out], s0, ACT.Copy, scale=0.5))
                        DV.wait(a_)
                        z_ = DV.did(nc.vector.scalar_tensor_tensor(M_lo[:, k, 0:n_out], s0, 0.5, M_hi[:, k, 0:n_out].bitcast(F32),
                                                                   ALU.mult, ALU.subtract))
                        sfree[j] = (a_, z_)
                        m_marks.append((a_, z_))
            add_residual((M_hi, M_lo, m_marks), KT, n_out)

        stage("out")
        fence()
        Y, c = place("gained", [P, KT, S], F32, R)
        rows_out, c = place("rows_out", [P, TT, D], F32, c)
        assert c <= mask_at
        gained_at = []
        for k in range(KT):
            gained_at.append(AC.did(nc.scalar.activation(Y[:, k, :], X[:, k, 0:S], ACT.Copy, scale=param("fin2", k))))
        reciprocal_root(S)
        m_root = DV.last
        out_sem = new_sem("out_written")
        n = 0
        out_v = A["out"].rearrange("(r c) d -> c r d", r=ROWS)
        turn = Slots([0, 1, 2, 3])
        for t in range(TT):
            marks = []
            for f in range(2):
                b, i = turn.take(PE)
                for k in range(4):
                    PE.wait(gained_at[4 * f + k])
                    ins = nc.tensor.transpose(bank[:, b, k * P:(k + 1) * P], Y[:, 4 * f + k, t * P:(t + 1) * P], ident[:, :])
                m = PE.did(ins)
                AC.wait(m_root)
                e = evacuate(rows_out[:, t, 512 * f:512 * f + 512], bank[:, b, :], m, var[:, 1, t:t + 1], DV if f else AC)
                turn.free(i, e)
                marks.append(e)
            SP.wait(*marks)
            for cc in range(QB):
                nc.sync.dma_start(out_v[t * QB + cc, :, :], rows_out[cc * ROWS:(cc + 1) * ROWS, t, :]).then_inc(out_sem, 16)
                n += 16
        nc.sync.wait_ge(out_sem, n)


def bass_windows(src):
    ap = src.ap if not callable(src.ap) else src.ap()
    part = list(ap)[0]
    return bass.AP(tensor=src.tensor, offset=src.offset, ap=[part, [1, CB], [CS, NC]])


def kernel(**inputs):
    import numpy as _np
    import concourse.bacc as _bacc
    from concourse import mybir as _mybir
    from concourse.bass_utils import run_bass_kernel_spmd as _run

    f = {k: _np.asarray(v) for k, v in inputs.items()}

    def by_feature(v):
        return _np.reshape(v, (-1, 128)).T

    def twice(v):
        return _np.concatenate([v, v], axis=0)

    gate_b = _np.zeros((128, 2), _np.float32)
    gate_b[0:4, 0] = f["mlstm_gate_bias"][0, 0:4]
    gate_b[0:4, 1] = f["mlstm_gate_bias"][0, 4:8]
    cols = {
        "ln1": by_feature(f["ln1_g"]), "ln2": by_feature(f["ln2_g"]), "ple": by_feature(f["ple_norm_g"]),
        "fin1": by_feature(f["final_g"]), "conv_w": by_feature(f["conv_w"]), "conv_b": by_feature(f["conv_b"]),
        "mnorm": by_feature(f["mlstm_norm_g"]), "pe_k": twice(f["cmp_pos_k"][0].T), "pe_v": twice(f["cmp_pos_v"][0].T),
        "gate_b": gate_b, "norm_a": by_feature(f["norm_g_2"][0]), "norm_b": by_feature(f["norm_g_2"][1]),
        "fin2": by_feature(f["final_norm_g_2"]),
        "qg_a": twice(f["q_norm_g_2"][0][:, None]), "qg_b": twice(f["q_norm_g_2"][1][:, None]),
        "kg_a": twice(f["k_norm_g_2"][0][:, None]), "kg_b": twice(f["k_norm_g_2"][1][:, None]),
    }
    params = _np.ascontiguousarray(_np.concatenate([cols[n] for n, _ in PARAMS], axis=1))
    rpb = f["na_rpb_2"]
    rel = _np.zeros((2, 8, 8, DCP, 8), _np.float32)
    for r in range(8):
        rel[:, :, r, 8:8 + 31, :] = rpb[:, :, 7 - r:15 - r, :].transpose(0, 1, 3, 2)
    tables = constants()
    const_at, _ = offsets([(k, v.shape[1]) for k, v in tables.items()])
    consts = _np.ascontiguousarray(_np.concatenate(list(tables.values()), axis=1))
    arrays = {
        "x": f["x"][0], "p": f["p"][0, 0], "params": params, "consts": consts,
        "na_rel": rel.reshape(2, 8, 8, DCP * 8), "meta": f["meta_tokens_2"],
        "w_in": f["w_in"][0], "cmp_k_w1": f["cmp_k_w1"][0], "cmp_k_w2": f["cmp_k_w2"][0],
        "cmp_v_w1": f["cmp_v_w1"][0], "cmp_v_w2": f["cmp_v_w2"][0], "w_out": f["w_out"][0], "w_up": f["w_up"][0],
        "w_down": f["w_down"][0], "w_ple_gate": f["w_ple_gate"][0], "w_ple_proj": f["w_ple_proj"][0],
        "w_in_2": f["w_in_2"], "w_o_attn_2": f["w_o_attn_2"], "w_o_na_2": f["w_o_na_2"], "w_out_2": f["w_out_2"],
    }
    arrays = {k: _np.ascontiguousarray(v) for k, v in arrays.items()}
    nc = _bacc.Bacc("TRN2", target_bir_lowering=False, num_devices=1)
    A = {k: nc.dram_tensor(k, v.shape, _mybir.dt.float32, kind="ExternalInput").ap() for k, v in arrays.items()}
    A["const_at"] = const_at
    A["out"] = nc.dram_tensor("out", (S, D), _mybir.dt.float32, kind="ExternalOutput").ap()
    program(nc, A)
    r = _run(nc, [arrays], core_ids=[0])
    return r.results[0]["out"].reshape(1, S, D)
```

```python
import math
from contextlib import ExitStack

import concourse.bass as bass
import numpy as np
from concourse import mybir

F32, F32R, BF16 = mybir.dt.float32, mybir.dt.float32r, mybir.dt.bfloat16
ALU, ACT, AX = mybir.AluOpType, mybir.ActivationFunctionType, mybir.AxisListType

P = 128
S, D = 512, 1024
KT, TT = D // P, S // P
EPS, NEG = 1e-6, -1e30
PLE, FF = 256, 2048
MH, MD = 4, 128
AH, AG, AD = 8, 2, 64
NH = 8
CB, CS, CH = 32, 16, 128
NC = (S - CB) // CS + 1
MW, AW, KW = MH * MD, AH * AD, AG * AD
Z_MQ, Z_MK, Z_MV, Z_MO = 0, MW, 2 * MW, 3 * MW
Z_MI = 4 * MW
Z_AQ = Z_MI + 2 * MH
Z_KC = Z_AQ + AW
Z_VC, Z_KS, Z_VS, Z_KX, Z_VX = (Z_KC + i * KW for i in range(1, 6))
Z_AG = Z_KC + 6 * KW
FOUR_ROWS = 4 * 4 * S
META = 16
T2 = S + META
HALF = T2 // 2
GW, ROWS = 64, S // 64
NAW = 16
QB = P // ROWS
C_QA, C_KA, C_VA, C_ZA = 0, 512, 640, 768
C_QB, C_KB, C_VB, C_ZB, C_GA, C_GB = 1280, 1792, 2304, 2816, 3328, 4352
DCP = 2 * NAW - 1 + 16


def constants():
    q = np.arange(P)
    out = {"ident": np.eye(P)}
    dist = (S - P) + q[:, None] - np.arange(S)[None, :]
    out["ndist"] = np.where(dist >= 0, -dist, NEG)
    head = (q[:, None] // AD) * (AH // AG) + np.arange(AH // AG)[None, :]
    out["qscale"] = AD ** -0.5 * 2.0 ** (head + 1.0)
    out["later"] = np.where(q[None, :] >= q[:, None], 0.0, NEG)
    t = (np.arange(TT)[None, :] * P + q[:, None])[:, :, None, None]
    end = np.arange(32)[None, None, None, :] * CS + CB - 1
    slope = (2.0 ** -(np.arange(AH) + 1.0))[None, None, :, None]
    ok = (end <= t) & (np.arange(32) < NC)
    out["cbias"] = np.where(ok, -slope * (t - end), NEG) + 0 * slope
    out["cvalid"] = (ok + 0 * end)[:, :, 0, :]
    out["hsel"] = (q[:, None] // AD == np.arange(2)[None, :])
    blk = q[:, None] // META
    out["own_pair"] = (blk % 2 * 4 + blk // 2 == np.arange(AH)[None, :])
    out["own_head"] = (blk == np.arange(AH)[None, :])
    out["spread"] = ((q[:, None] % 64 == q[None, :] % META) & (q[:, None] % 64 < META))
    rot = np.zeros((P, P))
    for h in range(2):
        for a in range(2):
            for i in range(16):
                lo, hi = h * 64 + a * 32 + i, h * 64 + a * 32 + 16 + i
                rot[hi, lo] = -1.0
                rot[lo, hi] = 1.0
    out["rot"] = rot
    inv = (np.float32(10000.0) ** (-np.arange(0, 32, 2, dtype=np.float32) / np.float32(32))).astype(np.float32)
    n = np.arange(S)
    row = np.concatenate([n % ROWS, np.zeros(META, int)]).astype(np.float32)
    col = np.concatenate([n // ROWS, np.zeros(META, int)]).astype(np.float32)
    ang = np.concatenate([row[None] * inv[:, None]] * 2 + [col[None] * inv[:, None]] * 2)
    out["cos"] = np.tile(np.cos(ang), (2, 1))
    out["sin"] = np.tile(np.sin(ang), (2, 1))
    cc, jj = (q // ROWS)[:, None], (np.arange(2 * P) // ROWS)[None, :]
    for name, b in (("na_first", 0), ("na_inner", 1), ("na_last", GW // QB - 1)):
        c, j = QB * b + cc, QB * b - 8 + jj
        start = np.clip(c - NAW // 2, 0, GW - NAW)
        out[name] = np.where((j >= start) & (j < start + NAW), 0.0, NEG)
    sel = np.zeros((P, MH, P))
    for h in range(MH):
        sel[h, h] = 1.0
    out["pick"] = sel
    return {k: np.asarray(v, np.float32).reshape(P, -1) for k, v in out.items()}


PARAMS = [("ln1", 8), ("ln2", 8), ("ple", 8), ("fin1", 8), ("conv_w", 48), ("conv_b", 16), ("mnorm", 4),
          ("pe_k", 32), ("pe_v", 32), ("gate_b", 2), ("norm_a", 8), ("norm_b", 8), ("fin2", 8),
          ("qg_a", 1), ("qg_b", 1), ("kg_a", 1), ("kg_b", 1)]


def offsets(pairs):
    at, out = 0, {}
    for name, n in pairs:
        out[name] = (at, n)
        at += n
    return out, at


class Lane:

    def __init__(self, new_sem, engine, name):
        self.new_sem, self.engine, self.name = new_sem, engine, name
        self.seen = {}
        self.last = None
        self.stage("start")

    def stage(self, stage):
        self.sem, self.count = self.new_sem(f"{self.name}_{stage}"), 0

    def did(self, instruction, stream=False):
        instruction.then_inc(self.sem, 1)
        self.count += 1
        if not stream:
            self.last = (self.sem, self.count)
        return self.sem, self.count

    def wait(self, *marks):
        for mark in marks:
            if mark is not None and self.seen.get(mark[0].name, 0) < mark[1]:
                self.engine.wait_ge(*mark)
                self.seen[mark[0].name] = mark[1]


class Slots:

    def __init__(self, buffers):
        self.buffers, self.free_at, self.n = buffers, [() for _ in buffers], 0

    def take(self, *lanes):
        i = self.n % len(self.buffers)
        self.n += 1
        assert self.free_at[i] is not None, "the slot is still in use"
        for lane in lanes:
            lane.wait(*self.free_at[i])
        self.free_at[i] = None
        return self.buffers[i], i

    def free(self, i, *marks):
        self.free_at[i] = marks


def program(nc, A):
    ctx = ExitStack()
    sems = {}

    def new_sem(name):
        sems[name] = ctx.enter_context(nc.semaphore(name))
        return sems[name]

    with ctx:
        PE, AC, DV, PO, SP = (Lane(new_sem, e, n) for e, n in (
            (nc.tensor, "pe"), (nc.scalar, "act"), (nc.vector, "dve"), (nc.gpsimd, "pool"), (nc.sync, "sp")))
        compute = (PE, AC, DV, PO)

        def stage(name):
            for lane in compute:
                lane.stage(name)

        def fence(waiting=None):
            lasts = [lane.last for lane in compute]
            for lane in waiting or (*compute, SP):
                lane.wait(*lasts)

        cursor = [nc.sbuf_base + (-nc.sbuf_base) % 64]

        def region(size):
            at = cursor[0]
            cursor[0] += size + (-size) % 64
            assert cursor[0] <= nc.sbuf_usable_end, (cursor[0], nc.sbuf_usable_end)
            return at

        def place(name, shape, dt, at):
            t = nc.alloc_sbuf_tensor_at(name, shape, dt, offset=at)
            n = 2 if dt == BF16 else 4
            return t, at + n * math.prod(shape[1:]) + (-n * math.prod(shape[1:])) % 64

        def fixed(name, shape, dt=F32):
            at = region((2 if dt == BF16 else 4) * math.prod(shape[1:]))
            return place(name, shape, dt, at)[0]

        X = fixed("x_feature_major", [P, KT, T2])
        H_hi, H_lo = fixed("h_hi", [P, KT, T2], F32R), fixed("h_lo", [P, KT, T2], F32R)
        g_at = region(2 * 4 * KT * T2)
        G_hi, g_mid = place("g_hi", [P, KT, T2], F32R, g_at)
        G_lo, _ = place("g_lo", [P, KT, T2], F32R, g_mid)
        UNIT = 2048
        RING, AHEAD = 3, 2
        raw_at = [region(4 * UNIT) for _ in range(RING)]
        raw = [place(f"w_raw{i}", [P, UNIT], F32, raw_at[i])[0] for i in range(RING)]
        wlo = [place(f"w_lo{i}", [P, UNIT], F32R, raw_at[i])[0] for i in range(RING)]
        whi = [fixed(f"w_hi{i}", [P, UNIT], F32R) for i in range(RING)]
        prm_at, prm_n = offsets(PARAMS)
        prm = fixed("params", [P, prm_n])
        ident = fixed("identity", [P, P])
        ones = fixed("ones", [P, P])
        rot = fixed("rot", [P, P])
        spread = fixed("spread", [P, P])
        small_consts = fixed("small_consts", [P, 4 + 2 + 2 * AH])
        qscale, hsel = small_consts[:, 0:4], small_consts[:, 4:6]
        own_pair, own_head = small_consts[:, 6:6 + AH], small_consts[:, 6 + AH:6 + 2 * AH]
        kcT = fixed("kc", [P, 32])
        vcn = fixed("vc", [32, KW])
        var = fixed("variance", [P, 3, TT + 1])
        half = fixed("minus_half", [P, 16])
        work_at = cursor[0]
        sq = [fixed(f"squares{i}", [P, T2]) for i in range(2)]
        acc = fixed("square_sum", [P, T2])
        tmp = fixed("h_rounded_from", [P, T2])
        x_squares, _ = place("x_squares", [P, D], F32, work_at)
        R = cursor[0]
        R_END = nc.sbuf_usable_end

        bank = ctx.enter_context(nc.psum_tensor("bank", [P, 8, 512], F32))

        load = new_sem("load_small")
        loads = [0]

        def small(dst, src):
            nc.sync.dma_start(dst, src).then_inc(load, 16)
            loads[0] += 16
            return (load, loads[0])

        cst = A["consts"]
        widths = A["const_at"]

        def table(name, dst):
            at, n = widths[name]
            return small(dst, cst[:, at:at + n])

        ident_sem = new_sem("ident_in")
        nc.sync.dma_start(ident[:, :], cst[:, widths["ident"][0]:widths["ident"][0] + P]).then_inc(ident_sem, 16)
        ident_in = (ident_sem, 16)
        x_rows, _ = place("x_rows", [P, TT, D], F32, g_at)
        x_in = [[new_sem(f"x_in{t}_{f}") for f in range(2)] for t in range(TT)]
        for t in range(TT):
            for f in range(2):
                cols = slice(512 * f, 512 * f + 512)
                nc.sync.dma_start(x_rows[:, t, cols], A["x"][t * P:(t + 1) * P, cols]).then_inc(x_in[t][f], 16)
        small(prm[:, :], A["params"][:, :])
        table("rot", rot[:, :])
        table("spread", spread[:, :])
        for name, dst in (("qscale", qscale), ("hsel", hsel), ("own_pair", own_pair), ("own_head", own_head)):
            table(name, dst)

        PO.did(nc.gpsimd.memset(ones[:, :], 1.0))
        PO.did(nc.gpsimd.memset(half[:, :], -0.5))
        m_ones = PO.did(nc.gpsimd.memset(var[:, 0:2, :], 1.0))

        def param(name, i=0, n=1, parts=slice(0, P)):
            at = prm_at[name][0] + i
            return prm[parts, at:at + n]

        units = []

        def plan(w, k0, kts, cols, split=True):
            src = w.rearrange("(k p) n -> p k n", p=P)
            n = sum(b - a for a, b in cols)
            pieces, at = [], 0
            for a, b in cols:
                pieces.append((at, b - a, src[:, k0:k0 + kts, a:b]))
                at += b - a
            assert kts * n <= UNIT
            units.append((pieces, kts, n, split))

        def plan_cols(w, c0, c1, k0=0, kts=KT, step=256):
            for c in range(c0, c1, step):
                plan(w, k0, kts, [(c, min(c + step, c1))])

        def head_pairs(c, a):
            return [(c + AD * h, c + AD * h + AD) for j in range(2) for h in (2 * a + j, 4 + 2 * a + j)]

        w_in = A["w_in"]
        plan(w_in, 0, KT, [(Z_MI, Z_MI + 32), (Z_MI + MH, Z_MI + MH + 32), (Z_AG - 8, Z_AG + 3 * AH)])
        plan_cols(w_in, Z_MQ, Z_MI)
        plan(w_in, 0, KT, [(Z_KC, Z_KC + 2 * KW)])
        for a, w1 in enumerate(("cmp_k_w1", "cmp_v_w1")):
            plan(w_in, 0, KT, head_pairs(Z_AQ, a))
            for part in range(2):
                src = A[w1].rearrange("(j d) n -> d j n", d=AD)[:, 16 * part:16 * part + 16, :]
                units.append(([(None, None, src)], 16, CH, False))
        plan_cols(w_in, Z_KS, Z_AG)
        for half_k in (0, 4):
            plan_cols(A["w_out"], 0, D, k0=half_k, kts=4)
        for part in range(2):
            for c in range(part * FF // 2, (part + 1) * FF // 2, 128):
                plan(A["w_up"], 0, KT, [(c, c + 128), (FF + c, FF + c + 128)])
            plan_cols(A["w_down"], 0, D, k0=KT * part)
        plan(A["w_ple_proj"], 0, 2, [(0, D)])
        plan_cols(A["w_ple_gate"], 0, D)
        for layer in range(2):
            w = A["w_in_2"][layer, :, :]
            plan_cols(w, C_KA, C_ZA)
            for a in range(2):
                plan(w, 0, KT, head_pairs(C_QA, a))
            plan_cols(w, C_ZA, C_QB)
            plan_cols(w, C_QB, C_ZB)
            plan_cols(w, C_ZB, C_GA)
            for c in range(0, D, 256):
                plan(w, 0, KT, [(C_GA + c, C_GA + c + 256)])
                plan(A["w_o_attn_2"][layer, :, :], 0, 4, [(c, c + 256)])
                plan(w, 0, KT, [(C_GB + c, C_GB + c + 256)])
                plan(A["w_o_na_2"][layer, :, :], 0, 4, [(c, c + 256)])
            plan_cols(A["w_out_2"][layer, :, :], 0, D)

        raw_sem = [new_sem(f"w_arrived{i}") for i in range(RING)]
        raw_n = [0] * RING
        arrived, split_done, used = {}, {}, {}
        state = {"dma": 0, "split": 0, "use": 0}

        def fetch():
            while state["dma"] < len(units):
                u = state["dma"]
                i = u % RING
                if u >= RING:
                    if u - RING not in used:
                        return
                    SP.wait(*used[u - RING])
                pieces, kts, n, _ = units[u]
                dst = raw[i][:, 0:kts * n].rearrange("p (k n) -> p k n", k=kts)
                for at, width, src in pieces:
                    if at is None:
                        for part in range(2):
                            nc.sync.dma_start(dst[64 * part:64 * part + 64, :, :], src).then_inc(raw_sem[i], 16)
                            raw_n[i] += 16
                    else:
                        nc.sync.dma_start(dst[:, :, at:at + width], src).then_inc(raw_sem[i], 16)
                        raw_n[i] += 16
                arrived[u] = (raw_sem[i], raw_n[i])
                state["dma"] += 1

        def split():
            u = state["split"]
            if u >= state["dma"]:
                return
            state["split"] += 1
            _, kts, n, do_split = units[u]
            if not do_split:
                return
            i = u % RING
            AC.wait(arrived[u])
            hi = AC.did(nc.scalar.activation(whi[i][:, 0:kts * n], raw[i][:, 0:kts * n], ACT.Copy), stream=True)
            PO.wait(arrived[u], hi)
            lo = PO.did(nc.gpsimd.tensor_tensor(wlo[i][:, 0:kts * n], raw[i][:, 0:kts * n],
                                                whi[i][:, 0:kts * n].bitcast(F32), ALU.subtract), stream=True)
            split_done[u] = (hi, lo)

        def weights():
            u = state["use"]
            state["use"] += 1
            fetch()
            while state["split"] <= min(u + 1, state["dma"] - 1):
                split()
            _, kts, n, do_split = units[u]
            i = u % RING
            if not do_split:
                PE.wait(arrived[u])
                return raw[i][:, 0:kts * n].rearrange("p (k n) -> p k n", k=kts), None, u
            PE.wait(*split_done[u])
            views = [t[i][:, 0:kts * n].rearrange("p (k n) -> p k n", k=kts) for t in (whi, wlo)]
            return views[0], views[1], u

        def weights_done(u, mark):
            used[u] = (mark,)
            fetch()
            if state["split"] <= u + AHEAD:
                split()

        def product(outs, stationary, moving, k, first, last):
            ins = None
            terms = ((0, 0), (0, 1), (1, 0))
            for n, (a, b) in enumerate(terms):
                for i, out in enumerate(outs):
                    ins = nc.tensor.matmul(out, stationary[a](k), moving[b](k)[i],
                                           start=first and n == 0, stop=last and n == 2)
            return ins

        def chunks(n):
            return [(0, n)] if n <= 512 else [(0, HALF), (HALF, n)]

        def to_features(act, kts, wviews, cols, n, out_banks):
            return tiles_to_features(act, kts, wviews, [cols], n, [out_banks])

        def tiles_to_features(act, kts, wviews, cols, n, out_banks):
            ch = chunks(n)
            mv = [lambda k, t=t: [t[:, k, a:b] for a, b in ch] for t in act[:2]]
            for k in range(kts):
                PE.wait(*act[2][k])
                for c, b0 in zip(cols, out_banks):
                    outs = [bank[:, b0 + i, 0:b - a] for i, (a, b) in enumerate(ch)]
                    st = [lambda k, t=t, c=c: c(t, k) for t in wviews]
                    ins = product(outs, st, mv, k, k == 0, k == kts - 1)
            return PE.did(ins)

        def columns(c):
            return lambda t, k: t[:, k, c:c + P]

        def feature_view(b, n):
            if n <= 512:
                return bank[:, b, 0:n]
            return bank[:, b:b + 2, 0:HALF]

        def dest(ap, n):
            return ap if n <= 512 else ap.rearrange("p (c t) -> p c t", c=2)

        def to_tokens(act, t0, tn, wviews, c0, cn, out):
            st = [lambda k, t=t: t[:, k, t0:t0 + tn] for t in act[:2]]
            mv = [lambda k, t=t: [t[:, k, c0:c0 + cn]] for t in wviews]
            for k in range(KT):
                PE.wait(*act[2][k])
                ins = product([out], st, mv, k, k == 0, k == KT - 1)
            return PE.did(ins)

        def split_into(hi, lo, src, *marks, lane=None):
            lane = lane or DV
            AC.wait(*marks)
            a = AC.did(nc.scalar.activation(hi, src, ACT.Copy))
            lane.wait(*marks, a)
            b = lane.did(lane.engine.tensor_tensor(lo, src, hi.bitcast(F32), ALU.subtract))
            return a, b

        sq_free = [(), ()]
        state["acc"] = None

        def add_square(k, n, *ready):
            AC.wait(*ready, *sq_free[k % 2])
            if k == 0:
                AC.wait(*acc_free)
                state["acc"] = AC.did(nc.scalar.activation(acc[:, 0:n], X[:, k, 0:n], ACT.Square))
                return
            m = AC.did(nc.scalar.activation(sq[k % 2][:, 0:n], X[:, k, 0:n], ACT.Square))
            sum_squares()
            state["square"] = (k, n, m)

        def sum_squares():
            if state.get("square") is None:
                return
            k, n, m = state["square"]
            state["square"] = None
            DV.wait(m, state["acc"])
            state["acc"] = DV.did(nc.vector.tensor_tensor(acc[:, 0:n], acc[:, 0:n], sq[k % 2][:, 0:n], ALU.add))
            sq_free[k % 2] = (state["acc"],)

        acc_free = []

        def tok_tiles(n):
            return [(t * P, P) for t in range(TT)] + ([(S, META)] if n > S else [])

        def reciprocal_root(n, meanwhile=None):
            sum_squares()
            PE.wait(state["acc"], m_ones)
            for t, (t0, tn) in enumerate(tok_tiles(n)):
                ins = nc.tensor.matmul(bank[0:tn, 7, t:t + 1], acc[:, t0:t0 + tn], ones[:, 0:1], start=True, stop=True)
            m = PE.did(ins)
            acc_free[:] = [m]
            DV.wait(m, m_ones)
            m = DV.did(nc.vector.tensor_scalar(var[:, 0, 0:TT], bank[:, 7, 0:TT], 1.0 / D, EPS, ALU.mult, ALU.add))
            if n > S:
                m = DV.did(nc.vector.tensor_scalar(var[0:META, 0, TT:TT + 1], bank[0:META, 7, TT:TT + 1], 1.0 / D, EPS,
                                                   ALU.mult, ALU.add))
            return root_row(n, m, meanwhile)

        def root_row(n, m, meanwhile=None):
            PO.wait(m)
            m = PO.did(nc.gpsimd.tensor_tensor(var[:, 1, :], var[:, 0, :], half[:, 0:TT + 1], ALU.pow))
            DV.wait(m, *sq_free[0])
            m = DV.did(nc.vector.tensor_tensor(sq[0][:, 0:S].rearrange("p (t q) -> p t q", t=TT),
                                               ident[:, :].unsqueeze(1).broadcast_to([P, TT, P]),
                                               var[:, 1, 0:TT].unsqueeze(2).broadcast_to([P, TT, P]), ALU.mult))
            if n > S:
                m = DV.did(nc.vector.tensor_scalar(sq[0][:, S:T2], ident[:, 0:META], var[:, 1, TT:TT + 1], None, ALU.mult))
            if meanwhile:
                meanwhile()
            PE.wait(m)
            for i, (a, z) in enumerate(chunks(n)):
                ins = nc.tensor.matmul(bank[:, 4 + i, 0:z - a], ones[:, :], sq[0][:, a:z], start=True, stop=True)
            m = PE.did(ins)
            sq_free[0] = (m,)
            return m

        def rms_norm_split(gain, n, r=None, before=None, meanwhile=None):
            r = r or reciprocal_root(n, meanwhile)
            DV.wait(PE.last)
            AC.wait(PE.last)
            PO.wait(PE.last)
            bufs = (tmp, sq[0], sq[1])
            freed = {}
            marks = []

            def normed(k):
                t = bufs[k % 3]
                DV.wait(r, x_at.get(k), *freed.get(k % 3, ()))
                c = DV.did(nc.vector.scalar_tensor_tensor(dest(t[:, 0:n], n), dest(X[:, k, 0:n], n), param(gain, k),
                                                          feature_view(4, n), ALU.mult, ALU.mult))
                AC.wait(c)
                freed[k % 3] = AC.did(nc.scalar.activation(H_hi[:, k, 0:n], t[:, 0:n], ACT.Copy))

            def low_part(k):
                lane = PO if k % 2 else DV
                hi = freed[k % 3]
                lane.wait(hi)
                lo = lane.did(lane.engine.tensor_tensor(H_lo[:, k, 0:n], bufs[k % 3][:, 0:n], H_hi[:, k, 0:n].bitcast(F32),
                                                        ALU.subtract))
                freed[k % 3] = (hi, lo)
                marks.append((hi, lo))

            x_at = {}
            if before:
                pipeline(list(range(KT)), lambda k: x_at.update({k: before(k)}), normed, low_part)
            else:
                pipeline(list(range(KT)), normed, low_part)
            sq_free[0], sq_free[1] = marks[-1] + marks[-2] + marks[-3], marks[-1] + marks[-2] + marks[-3]
            return H_hi, H_lo, marks

        def slots(buffers, *marks):
            ring = Slots(buffers)
            ring.free_at = [marks for _ in buffers]
            return ring

        def pipeline(items, *stages):
            for step in range(len(items) + len(stages) - 1):
                for n, stage_ in enumerate(stages):
                    if 0 <= step - n < len(items):
                        stage_(items[step - n])

        def evacuate(dst, src, mark, scale=None, lane=None):
            if lane is DV:
                DV.wait(mark)
                if scale is None:
                    return DV.did(nc.vector.tensor_copy(dst, src))
                return DV.did(nc.vector.tensor_scalar(dst, src, scale, None, ALU.mult))
            AC.wait(mark)
            if scale is None:
                return AC.did(nc.scalar.activation(dst, src, ACT.Copy))
            return AC.did(nc.scalar.activation(dst, src, ACT.Copy, scale=scale))

        def features_steps(dsts, n, act, scale=None, together=False, then=None):
            hi, lo, u = weights()
            if together:
                (b, i), (b2, i2) = dense.take(PE), dense.take(PE)
                m = tiles_to_features(act, KT, (hi, lo), [columns(0), columns(P)], n, [b, b2])
                weights_done(u, m)
                got = [(b, i, m), (b2, i2, m)]
            for j, dst in enumerate(dsts):
                if together:
                    b, i, m = got[j]
                else:
                    b, i = dense.take(PE)
                    m = to_features(act, KT, (hi, lo), columns(j * P), n, b)
                    if j == len(dsts) - 1:
                        weights_done(u, m)
                e = evacuate(dest(dst, n), feature_view(b, n), m, scale(j) if callable(scale) else scale,
                             DV if j % 2 else AC)
                dense.free(i, e)
                done.append(e)
                yield

        def tokens_steps(dst_of, tiles, act, func=None, c0=0, cn=256, unit=None, finish_unit=True):
            hi, lo, u = unit or weights()
            for t, (t0, tn) in enumerate(tiles):
                b, i = dense.take(PE)
                m = to_tokens(act, t0, tn, (hi, lo), c0, cn, bank[0:tn, b, 0:cn])
                if t == len(tiles) - 1 and finish_unit:
                    weights_done(u, m)
                dst, shape = dst_of(t)
                src = shape(bank[0:tn, b, 0:cn])
                if func is None:
                    e = evacuate(dst, src, m, None, DV if t % 2 else AC)
                else:
                    AC.wait(m)
                    e = AC.did(nc.scalar.activation(dst, src, func, scale=0.5))
                dense.free(i, e)
                done.append(e)
                yield

        done = []

        def residual_steps(act, kts, n, square=True):
            for uu in range(KT // 2):
                hi, lo, u = weights()
                for j in range(2):
                    k = 2 * uu + j
                    b, i = dense.take(PE)
                    m = to_features(act, kts, (hi, lo), columns(j * P), n, b)
                    if j:
                        weights_done(u, m)
                    DV.wait(m)
                    e = DV.did(nc.vector.tensor_tensor(dest(X[:, k, 0:n], n), feature_view(b, n), dest(X[:, k, 0:n], n), ALU.add))
                    dense.free(i, e)
                    if square:
                        add_square(k, n, e)
                    else:
                        DV.wait(e)
                    yield

        def add_residual(*args, **how):
            drain(residual_steps(*args, **how))

        def all_of(*gens):
            for g in gens:
                yield from g

        def first_steps(gen, n):
            for _ in range(n):
                yield next(gen)

        def drain(gen):
            for _ in gen:
                pass

        dense = Slots([0, 1, 2, 3])
        stage("x_in")
        fetch()
        small_loaded = (load, loads[0])
        turn = Slots([0, 1, 2, 3, 4, 5, 6])
        m_sq = None
        for t in range(TT):
            AC.wait((x_in[t][0], 16), (x_in[t][1], 16), m_sq)
            m_sq = AC.did(nc.scalar.activation(x_squares[:, :], x_rows[:, t, :], ACT.Square, accum_out=var[:, 2, t:t + 1]))
            for f in range(2):
                PE.wait(ident_in, (x_in[t][f], 16))
                b, i = turn.take(PE)
                for k in range(4):
                    ins = nc.tensor.transpose(bank[:, b, k * P:(k + 1) * P], x_rows[:, t, (4 * f + k) * P:(4 * f + k + 1) * P],
                                              ident[:, :])
                m = PE.did(ins)
                DV.wait(m)
                m = DV.did(nc.vector.tensor_copy(X[:, 4 * f:4 * f + 4, t * P:(t + 1) * P],
                                                 bank[:, b, :].rearrange("p (k q) -> p k q", k=4)))
                turn.free(i, m)
        for lane in compute:
            lane.wait(small_loaded)
        split()
        stage("norm1")
        DV.wait(m_sq, m_ones)
        m = DV.did(nc.vector.tensor_scalar(var[:, 0, 0:TT], var[:, 2, 0:TT], 1.0 / D, EPS, ALU.mult, ALU.add))
        PE.wait(*[mark for marks in turn.free_at for mark in marks])
        Hs = rms_norm_split("ln1", S, root_row(S, m))

        c = R
        mqT, c = place("mq", [P, MH, S], F32, c)
        mkT, c = place("mk", [P, MH, S], F32, c)
        mv, c = place("mv", [P, TT, MH, MD + 1], F32, c)
        mo, c = place("mo_gate", [P, TT, MW], F32, c)
        g4, c = place("gate_rows", [MH, 5, S], F32, c)
        ag_rows, _ = place("branch_gate_rows", [P, S], F32, c)
        negM, c = place("neg_M", [P, S], F32, c)
        decay, c = place("decay", [P, 2, S], F32, c)
        WT, c = place("mlstm_weights", [P, 2, TT, S], F32, c)
        assert c <= R_END, c
        gate_row = {n: g4[:, i, :] for i, n in enumerate(("f", "a", "b", "i", "m"))}
        c2 = g_at
        aqT, c2 = place("aq", [P, 4, S], F32, c2)
        kvT, c2 = place("kv", [P, 4, S], F32, c2)
        vs, c2 = place("vs", [P, 2, TT, KW], F32, c2)
        ag, c2 = place("ag", [P, TT, 3 * AH], F32, c2)
        col4, c2 = place("gate_columns", [P, 3, TT, MH], F32, c2)
        msq, c2 = place("m_square", [P, 2, TT, MH], F32, c2)
        late, c2 = place("later", [P, P], F32, c2)
        pick, c2 = place("pick", [P, MH, P], F32, c2)
        den, c2 = place("mlstm_den", [P, 4], F32, c2)
        diag0, c2 = place("diag0", [P, 2, P], F32, c2)
        msq_of, c2 = place("square_scratch", [P, P], F32, c2)
        ndist, c2 = place("distance", [P, S], F32, c2)
        cb, c2 = place("cmp_bias", [P, TT, AH * 32], F32, c2)
        cv, c2 = place("cmp_valid", [P, TT, 32], F32, c2)
        cw2, c2 = place("cmp_w2", [P, 2, 2 * AD], F32, c2)
        assert c2 <= g_at + 2 * 4 * KT * T2, c2 - g_at
        vT, _ = place("v_features", [P, S], F32, work_at)
        c2 = work_at
        block, c2 = place("cmp_blocks", [P, CB, 2 * NC], F32, c2)
        hid, c2 = place("cmp_hidden", [P, 4, 32], F32, c2)
        assert c2 <= R

        stage("project1")
        SP.wait(PE.last)
        table("later", late[:, :])
        table("pick", pick[:, :, :].rearrange("p h q -> p (h q)"))
        table("ndist", ndist[:, :])
        table("cbias", cb[:, :, :].rearrange("p t x -> p (t x)"))
        tables1 = table("cvalid", cv[:, :, :].rearrange("p t x -> p (t x)"))

        hi, lo, u = weights()
        b, i = dense.take(PE)
        for k in range(KT):
            PE.wait(*Hs[2][k])
            ins = product([bank[0:96, b, 0:S]], [lambda k, t=t: t[:, k, 0:96] for t in (hi, lo)],
                          [lambda k, t=t: [t[:, k, 0:S]] for t in Hs[:2]], k, k == 0, k == KT - 1)
        m = PE.did(ins)
        weights_done(u, m)
        AC.wait(m)
        mi = AC.did(nc.scalar.activation(gate_row["i"], bank[0:MH, b, 0:S], ACT.Identity, bias=param("gate_b", 0, 1, slice(0, MH))))
        mf = AC.did(nc.scalar.activation(gate_row["f"], bank[32:32 + MH, b, 0:S], ACT.Identity, bias=param("gate_b", 1, 1, slice(0, MH))))
        m = AC.did(nc.scalar.activation(ag_rows[64:96, :], bank[64:96, b, 0:S], ACT.Tanh, scale=0.5))
        dense.free(i, m)
        b, i = dense.take(PE)
        PE.wait(m)
        for t in range(TT):
            ins = nc.tensor.transpose(bank[:, b, 32 * t:32 * t + 32], ag_rows[64:96, t * P:(t + 1) * P], ident[64:96, 64:96])
        m = PE.did(ins)
        DV.wait(m)
        ag_done = DV.did(nc.vector.tensor_scalar(ag[:, :, :], bank[:, b, 0:P].rearrange("p (t g) -> p t g", t=TT)[:, :, 8:],
                                                 0.5, 0.5, ALU.mult, ALU.add))
        dense.free(i, ag_done)

        gr = gate_row
        DV.wait(mf, mi)
        m = DV.did(nc.vector.scalar_tensor_tensor(gr["a"], gr["f"], -1.0, gr["f"], ALU.mult, ALU.min))
        AC.wait(m)
        m = AC.did(nc.scalar.activation(gr["a"], gr["a"], ACT.Exp))
        AC.wait(m, m_ones)
        m = AC.did(nc.scalar.activation(gr["a"], gr["a"], ACT.Ln, bias=ones[0:MH, 0:1]))
        DV.wait(m)
        m = DV.did(nc.vector.scalar_tensor_tensor(gr["f"], gr["f"], 0.0, gr["a"], ALU.min, ALU.subtract))
        DV.wait(m)
        m = DV.did(nc.vector.memset(gr["m"], 1.0))
        DV.wait(m)
        m = DV.did(nc.vector.tensor_tensor_scan(gr["b"], gr["m"], gr["f"], 0.0, ALU.mult, ALU.add))
        DV.wait(m)
        m = DV.did(nc.vector.tensor_tensor(gr["i"], gr["i"], gr["b"], ALU.subtract))
        DV.wait(m)
        m = DV.did(nc.vector.tensor_tensor_scan(gr["a"], gr["i"], gr["i"], 0.0, ALU.max, ALU.max))
        DV.wait(m)
        m = DV.did(nc.vector.tensor_tensor(gr["m"], gr["b"], gr["a"], ALU.add))
        DV.wait(m)
        m_rows = DV.did(nc.vector.tensor_scalar(gr["f"], gr["a"], -1.0, None, ALU.mult))

        tiles1 = [(t * P, P) for t in range(TT)]
        done.clear()
        for a in range(2):
            drain(features_steps([mqT[:, 2 * a + j, :] for j in range(2)], S, Hs, scale=MD ** -0.5))
        PE.wait(m_rows)
        b, i = dense.take(PE)
        for n, name in enumerate(("i", "m")):
            for t in range(TT):
                ins = nc.tensor.transpose(bank[:, b, (n * TT + t) * MH:(n * TT + t + 1) * MH],
                                          gr[name][:, t * P:(t + 1) * P], ident[0:MH, 0:MH])
        m = PE.did(ins)
        DV.wait(m)
        m = DV.did(nc.vector.tensor_copy(col4[:, 0:2, :, :].rearrange("p a t h -> p (a t h)"), bank[:, b, 0:2 * TT * MH]))
        dense.free(i, m)
        AC.wait(m)
        em_done = AC.did(nc.scalar.activation(col4[:, 2, :, :], col4[:, 1, :, :], ACT.Exp, scale=-1.0))
        for a in range(2):
            drain(features_steps([mkT[:, 2 * a + j, :] for j in range(2)], S, Hs))
        for a in range(2):
            drain(tokens_steps(lambda t: (mv[:, t, 2 * a:2 * a + 2, 0:MD], lambda x: x.rearrange("p (h d) -> p h d", h=2)),
                               tiles1, Hs))
        done.append(PO.did(nc.gpsimd.memset(mv[:, :, :, MD:MD + 1], 1.0)))
        mlstm_in = tuple(done)

        mo_in, mo_out = [], []

        def mlstm_steps():
            scores, outs_ = Slots([4, 5]), Slots([6, 7])
            head = {}
            wt_free = [(), ()]
            decay_free = [(), ()]
            neg_free = [()]
            sq_mark = [None]
            PE.wait(*mlstm_in, tables1)
            DV.wait(tables1)

            def weights_of(h, s):
                if s == 0:
                    b, i = dense.take(PE)
                    m = PE.did(nc.tensor.matmul(bank[:, b, 0:S], pick[0:MH, h, :], gr["f"], start=True, stop=True))
                    AC.wait(*neg_free[0])
                    mneg = evacuate(negM[:, :], bank[:, b, 0:S], m)
                    dense.free(i, mneg)
                    head[h] = (mneg, [])
                mneg, wmarks = head[h]
                n = S - s * P
                d = s % 2
                b, i = scores.take(PE)
                mqk = PE.did(nc.tensor.matmul(bank[:, b, 0:n], mkT[:, h, s * P:(s + 1) * P], mqT[:, h, s * P:S],
                                              start=True, stop=True))
                DV.wait(mneg, *decay_free[d])
                md = DV.did(nc.vector.tensor_tensor(diag0[:, d, :], negM[:, s * P:(s + 1) * P], late[:, :], ALU.add))
                AC.wait(md, em_done, *decay_free[d])
                me = AC.did(nc.scalar.activation(decay[:, d, 0:P], diag0[:, d, :], ACT.Exp, bias=col4[:, 0, s, h:h + 1]))
                if n > P:
                    me = AC.did(nc.scalar.activation(decay[:, d, P:n], negM[:, (s + 1) * P:S], ACT.Exp,
                                                     bias=col4[:, 0, s, h:h + 1]))
                neg_free[0] = (me, md)
                DV.wait(me, mqk, *wt_free[h % 2])
                mw = DV.did(nc.vector.tensor_tensor(WT[:, h % 2, s, s * P:S], bank[:, b, 0:n], decay[:, d, 0:n], ALU.mult))
                scores.free(i, mw)
                decay_free[d] = (mw,)
                wmarks.append(mw)

            def output_of(h, l):
                PE.wait(*head[h][1])
                b, i = outs_.take(PE)
                for s in range(l + 1):
                    ins = nc.tensor.matmul(bank[:, b, 0:MD + 1], WT[:, h % 2, s, l * P:(l + 1) * P], mv[:, s, h, :],
                                           start=s == 0, stop=s == l)
                m = PE.did(ins)
                wt_free[h % 2] = (m,)
                DV.wait(m, em_done)
                d1 = DV.did(nc.vector.scalar_tensor_tensor(den[:, 0:1], bank[:, b, MD:MD + 1], -1.0, col4[:, 2, l, h:h + 1],
                                                           ALU.mult, ALU.max))
                DV.wait(d1)
                d1 = DV.did(nc.vector.tensor_tensor(den[:, 1:2], bank[:, b, MD:MD + 1], den[:, 0:1], ALU.max))
                DV.wait(d1)
                d1 = DV.did(nc.vector.reciprocal(den[:, 2:3], den[:, 1:2]))
                DV.wait(d1)
                hmv = mqT[:, h, l * P:(l + 1) * P]
                d1 = DV.did(nc.vector.tensor_scalar(hmv, bank[:, b, 0:MD], den[:, 2:3], None, ALU.mult))
                outs_.free(i, d1)
                AC.wait(d1, sq_mark[0])
                sq_mark[0] = AC.did(nc.scalar.activation(msq_of[:, :], hmv, ACT.Square, accum_out=msq[:, 0, l, h:h + 1]))

            for h in range(MH + 1):
                for s in range(TT):
                    if h < MH:
                        weights_of(h, s)
                    if h > 0:
                        output_of(h - 1, s)
                    yield
            sq_mark = sq_mark[0]
            DV.wait(sq_mark)
            r = DV.did(nc.vector.tensor_scalar(msq[:, 1, :, :], msq[:, 0, :, :], 4.0 / MD, 4.0 * EPS, ALU.mult, ALU.add))
            PO.wait(r)
            r = PO.did(nc.gpsimd.tensor_tensor(msq[:, 0, :, :].rearrange("p t h -> p (t h)"),
                                               msq[:, 1, :, :].rearrange("p t h -> p (t h)"), half[:, 0:TT * MH], ALU.pow))
            DV.wait(r, *mo_in)
            hm_v = mqT[:, :, :].rearrange("p h (t d) -> p t h d", t=TT)
            for t in range(TT):
                g = mo[:, t, :].rearrange("p (h d) -> p h d", h=MH)
                m = DV.did(nc.vector.scalar_tensor_tensor(g, g, 1.0, hm_v[:, t, :, :], ALU.add, ALU.mult))
                DV.wait(m)
                mo_out.append(DV.did(nc.vector.tensor_tensor(g, g, msq[:, 0, t, :].unsqueeze(2).broadcast_to([P, MH, MD]), ALU.mult)))
                yield

        def compress_steps(cmp_in, w2_in):
            m = None
            for n in range(2):
                DV.wait(*cmp_in, blocks_zero)
                if m is not None:
                    DV.wait(m)
                pe = param("pe_k" if n == 0 else "pe_v", 0, CB)
                for g in range(AG):
                    rows = slice(g * AD, (g + 1) * AD)
                    mb = DV.did(nc.vector.tensor_tensor(block[rows, :, g * NC:(g + 1) * NC], bass_windows(kvT[rows, n, :]),
                                                        pe[rows].unsqueeze(2).broadcast_to([AD, CB, NC]), ALU.add))
                yield
                PE.wait(mb)
                b, i = dense.take(PE)
                for part in range(2):
                    w1, _, u = weights()
                    for j in range(16):
                        jj = 16 * part + j
                        ins = nc.tensor.matmul(bank[:, b, 0:2 * NC], w1[:, j, :], block[:, jj, :], start=jj == 0, stop=jj == CB - 1)
                    m = PE.did(ins)
                    weights_done(u, m)
                    if part == 0:
                        yield
                hx, h3 = hid[:, 0:2, 0:NC], hid[:, 2:4, 0:NC]
                AC.wait(m)
                e = AC.did(nc.scalar.activation(hx, bank[:, b, 0:2 * NC].rearrange("p (g n) -> p g n", g=AG), ACT.Copy))
                dense.free(i, e)
                AC.wait(e)
                e = AC.did(nc.scalar.activation(h3, hx, ACT.Square))
                DV.wait(e)
                e = DV.did(nc.vector.tensor_scalar(h3, h3, 0.044715, 1.0, ALU.mult, ALU.add))
                DV.wait(e)
                e = DV.did(nc.vector.tensor_tensor(h3, h3, hx, ALU.mult))
                AC.wait(e)
                e = AC.did(nc.scalar.activation(h3, h3, ACT.Tanh, scale=math.sqrt(2 / math.pi)))
                yield
                DV.wait(e)
                e = DV.did(nc.vector.scalar_tensor_tensor(h3, h3, 1.0, hx, ALU.add, ALU.mult))
                DV.wait(e)
                e = DV.did(nc.vector.tensor_scalar(hx, h3, 0.5, None, ALU.mult))
                PE.wait(e, w2_in)
                (b, i), (b2, i2) = dense.take(PE), dense.take(PE)
                for g in range(AG):
                    if n == 0:
                        ins = nc.tensor.matmul(bank[:, (b, b2)[g], 0:NC], cw2[:, 0, :], hid[:, g, 0:NC], start=True, stop=True)
                    else:
                        ins = nc.tensor.matmul(bank[0:NC, b, g * AD:(g + 1) * AD], hid[:, g, 0:NC], cw2[:, 1, 0:AD],
                                               start=True, stop=True)
                m = PE.did(ins)
                if n == 0:
                    for g in range(AG):
                        rows = slice(g * AD, (g + 1) * AD)
                        e = evacuate(kcT[rows, 0:NC], bank[rows, (b, b2)[g], 0:NC], m)
                else:
                    e = evacuate(vcn[0:NC, :], bank[0:NC, b, 0:KW], m)
                dense.free(i, e)
                dense.free(i2, e)
                done.append(e)
            yield

        stage("mlstm")
        SP.wait(*Hs[2][-1], *Hs[2][-2], *Hs[2][-3])
        PO.wait(*Hs[2][-1], *Hs[2][-2], *Hs[2][-3])
        PO.did(nc.gpsimd.memset(block[:, :, :], 0.0))
        blocks_zero = PO.last
        done.append(PO.did(nc.gpsimd.memset(kcT[:, :], 0.0)))
        for n, w2 in enumerate(("cmp_k_w2", "cmp_v_w2")):
            for part in range(2):
                w2_in = small(cw2[:, n, part * AD:part * AD + AD], A[w2][:, :])

        def rest_steps():
            done.clear()
            for a in range(2):
                yield from tokens_steps(lambda t: (mo[:, t, 256 * a:256 * a + 256], lambda x: x), tiles1, Hs, func=ACT.Tanh)
            mo_in.extend(done)
            done.clear()
            yield from features_steps([kvT[:, j, :] for j in range(2)], S, Hs)
            compress = compress_steps(tuple(done), w2_in)
            queries = [features_steps([aqT[:, 2 * a + j, :] for j in range(2)], S, Hs,
                                      scale=lambda j, a=a: qscale[:, 2 * a + j:2 * a + j + 1]) for a in range(2)]
            for steps in (compress, queries[0], queries[0], compress, compress, queries[1], compress, queries[1],
                          compress, compress):
                next(steps)
                yield
            for q in queries:
                drain(q)
            v_read = (PE.last,)
            for n in range(2):
                unit = weights()
                b, i = dense.take(PE)
                m = to_features(Hs, KT, unit[:2], columns(0), S, b)
                e = evacuate(kvT[:, 2 + n, :], bank[:, b, 0:S], m)
                dense.free(i, e)
                done.append(e)
                yield
                if n == 0:
                    drain(compress)
                b, i = dense.take(PE)
                m = to_features(Hs, KT, unit[:2], columns(P), S, b)
                weights_done(unit[2], m)
                AC.wait(*v_read)
                e = evacuate(vT[:, :], bank[:, b, 0:S], m)
                dense.free(i, e)
                yield
                b, i = dense.take(PE)
                PE.wait(e)
                for t in range(TT):
                    ins = nc.tensor.transpose(bank[:, b, t * P:(t + 1) * P], vT[:, t * P:(t + 1) * P], ident[:, :])
                m = PE.did(ins)
                v_read = (m,)
                e = evacuate(vs[:, n, :, :].rearrange("p t c -> p (t c)"), bank[:, b, :], m, None, DV)
                dense.free(i, e)
                done.append(e)
                yield

        rest = rest_steps()
        for step, _ in enumerate(mlstm_steps()):
            next(rest, None)
        drain(rest)
        nsa_in = tuple(done)

        stage("nsa")
        fence()
        c = R
        a_rows, c = place("a_rows", [P, TT, AW], F32, c)
        sc_s, pr_s, pt_s = [None] * 2, [None] * 3, [None] * 2
        for n in range(2):
            pr_s[n], c = place(f"probs{n}", [P, S], F32, c)
            pt_s[n], c = place(f"probsT{n}", [P, TT, P], F32, c)
        assert c <= R + 2 * FOUR_ROWS
        c = R + 3 * FOUR_ROWS + 4 * TT * MH * (MD + 1)
        stat, c = place("softmax_stats", [P, 5, 3, AH], F32, c)
        mixed, c = place("branch_part", [P, 512], F32, c)
        for n in range(2):
            sc_s[n], c = place(f"scores{n}", [P, S], F32, c)
        pt2, c = place("probsT2", [P, TT, P], F32, c)
        pt_s.append(pt2)
        pr_s[2], c = place("probs2", [P, S], F32, c)
        m_rows = [None, None]
        for n in range(2):
            m_rows[n], c = place(f"m_features{n}", [P, S], F32, c)
        assert c <= R_END, (c, R_END)
        PE.wait(*nsa_in)
        DV.wait(ag_done)
        scores, turned, outb = Slots([2, 3]), Slots([4, 5]), Slots([6, 7])
        sc, pr, pt = Slots(sc_s), Slots(pr_s), Slots(pt_s)
        gates_of = [ag[:, t, :].rearrange("p (h b) -> p b h", b=3) for t in range(TT)]

        def qk_rows(h):
            return slice(AD * (h // 4), AD * (h // 4) + AD)

        pair_order = [0, 4, 1, 5, 2, 6, 3, 7]
        items = [(t, br, h) for t in range(TT) for br in range(3) for h in ([0] if br == 0 else pair_order)]
        live = {}
        stat_free = {br: () for br in range(3)}

        def nsa_score(item):
            t, br, h = item
            n = (t + 1) * P
            if br == 0:
                (b, i), (b2, i2) = scores.take(PE), scores.take(PE)
                for x in range(AH):
                    ins = nc.tensor.matmul(bank[:, (b, b2)[x // 4], x % 4 * 32:x % 4 * 32 + NC + 1],
                                           aqT[qk_rows(x), x % 4, t * P:(t + 1) * P], kcT[qk_rows(x), 0:NC + 1],
                                           start=True, stop=True)
                m = PE.did(ins)
                s_, si = sc.take(DV)
                DV.wait(m, *stat_free[0])
                for x in range(AH):
                    e = DV.did(nc.vector.scalar_tensor_tensor(s_[:, 32 * x:32 * x + 32], bank[:, (b, b2)[x // 4], x % 4 * 32:x % 4 * 32 + 32],
                                                              2.0 ** -(x + 1), cb[:, t, 32 * x:32 * x + 32], ALU.mult, ALU.add))
                scores.free(i, e)
                scores.free(i2, e)
                DV.wait(e)
                s3 = s_[:, 0:256].rearrange("p (h n) -> p h n", h=AH)
                e = DV.did(nc.vector.reduce_max(stat[:, 0, 0, :], s3, AX.X))
                DV.wait(e)
                e = DV.did(nc.vector.tensor_tensor(s3, s3, stat[:, 0, 0, :].unsqueeze(2).broadcast_to([P, AH, 32]), ALU.subtract))
                AC.wait(e)
                e = AC.did(nc.scalar.activation(s_[:, 0:256], s_[:, 0:256], ACT.Exp))
                p_, pi = pr.take(DV)
                p3 = p_[:, 0:256].rearrange("p (h n) -> p h n", h=AH)
                DV.wait(e)
                es = DV.did(nc.vector.reduce_sum(stat[:, 1, 0, :], s3, AX.X))
                e = DV.did(nc.vector.tensor_tensor(p3, s3, cv[:, t, :].unsqueeze(1).broadcast_to([P, AH, 32]), ALU.mult))
                sc.free(si, e)
                live[item] = (p_, pi, (e, es))
                return
            b, i = scores.take(PE)
            m = PE.did(nc.tensor.matmul(bank[:, b, 0:n], aqT[qk_rows(h), h % 4, t * P:(t + 1) * P],
                                        kvT[qk_rows(h), 1 + br, 0:n], start=True, stop=True))
            s_, si = sc.take(DV)
            DV.wait(m, *stat_free[br])
            e = DV.did(nc.vector.tensor_tensor_reduce(s_[:, 0:n], bank[:, b, 0:n], ndist[:, S - n:S], -2.0 ** -(h + 1), 3e38,
                                                      ALU.add, ALU.min, stat[:, 0, br, h:h + 1]))
            scores.free(i, e)
            p_, pi = pr.take(AC)
            AC.wait(e)
            e = AC.did(nc.scalar.activation(p_[:, 0:n], s_[:, 0:n], ACT.Exp, bias=stat[:, 0, br, h:h + 1], scale=-1.0,
                                            accum_out=stat[:, 1, br, h:h + 1]))
            sc.free(si, e)
            live[item] = (p_, pi, (e,))

        def nsa_turn(item):
            t, br, h = item
            p_, pi, ready = live[item]
            PE.wait(*ready)
            if br == 0:
                got = []
                for g in range(2):
                    b, i = turned.take(PE)
                    for x in range(4):
                        ins = nc.tensor.transpose(bank[0:32, b, x * P:(x + 1) * P], p_[:, (4 * g + x) * 32:(4 * g + x + 1) * 32],
                                                  ident[:, :])
                    m = PE.did(ins)
                    q_, qi = pt.take(AC)
                    e = evacuate(q_[0:NC, :, :].rearrange("p t q -> p (t q)"), bank[0:NC, b, :], m)
                    turned.free(i, e)
                    got.append((q_, qi, e))
                pr.free(pi, m)
                live[item] = (got, ready)
                return
            b, i = turned.take(PE)
            for k in range(t + 1):
                ins = nc.tensor.transpose(bank[:, b, k * P:(k + 1) * P], p_[:, k * P:(k + 1) * P], ident[:, :])
            m = PE.did(ins)
            pr.free(pi, m)
            lane = DV if h % 2 == 1 else AC
            q_, qi = pt.take(lane)
            e = evacuate(q_[:, 0:t + 1, :].rearrange("p t q -> p (t q)"), bank[:, b, 0:(t + 1) * P], m, None, lane)
            turned.free(i, e)
            live[item] = (q_, qi, e, ready)

        def nsa_value(item):
            t, br, h = item
            if br == 0:
                got, ready = live.pop(item)
                ob, oi = outb.take(PE)
                for g in range(2):
                    q_, qi, e = got[g]
                    PE.wait(e)
                    for x in range(4):
                        ins = nc.tensor.matmul(bank[:, ob, (4 * g + x) * AD:(4 * g + x + 1) * AD], q_[0:NC, x, :],
                                               vcn[0:NC, g * AD:(g + 1) * AD], start=True, stop=True)
                    m = PE.did(ins)
                    pt.free(qi, m)
            else:
                q_, qi, e, ready = live.pop(item)
                if h == pair_order[0]:
                    live["o"] = outb.take(PE)
                ob, oi = live["o"]
                PE.wait(e)
                for k in range(t + 1):
                    ins = nc.tensor.matmul(bank[:, ob, h * AD:(h + 1) * AD], q_[:, k, :],
                                           vs[:, br - 1, k, (h // 4) * AD:(h // 4 + 1) * AD], start=k == 0, stop=k == t)
                m = PE.did(ins)
                pt.free(qi, m)
                if h != pair_order[-1]:
                    return
            DV.wait(*ready)
            e = DV.did(nc.vector.reciprocal(stat[:, 2, br, :], stat[:, 1, br, :]))
            stat_free[br] = (e,)
            AC.wait(e)
            DV.wait(e)
            e = DV.did(nc.vector.tensor_tensor(stat[:, 2, br, :], stat[:, 2, br, :], gates_of[t][:, br, :], ALU.mult))
            DV.wait(e, m)
            dst = a_rows[:, t, :] if br == 0 else mixed[:, :]
            e = DV.did(nc.vector.tensor_tensor(dst.rearrange("p (h d) -> p h d", h=AH),
                                               bank[:, ob, :].rearrange("p (h d) -> p h d", h=AH),
                                               stat[:, 2, br, :].unsqueeze(2).broadcast_to([P, AH, AD]), ALU.mult))
            outb.free(oi, e)
            if br:
                DV.wait(e)
                DV.did(nc.vector.tensor_tensor(a_rows[:, t, :], a_rows[:, t, :], mixed[:, :], ALU.add))

        m_feat = Slots(m_rows)
        m_marks = []
        dense = Slots([0, 1])

        def mlstm_out_steps():
            for k in range(4):
                b, i = dense.take(PE)
                for t in range(TT):
                    ins = nc.tensor.transpose(bank[:, b, t * P:(t + 1) * P], mo[:, t, k * P:(k + 1) * P], ident[:, :])
                m = PE.did(ins)
                s_, si = m_feat.take(AC)
                m = evacuate(s_[:, :], bank[:, b, :], m, param("mnorm", k))
                dense.free(i, m)
                got = split_into(H_hi[:, k, 0:S], H_lo[:, k, 0:S], s_[:, :], m, lane=PO)
                m_feat.free(si, *got)
                m_marks.append(got)
                yield
            yield from residual_steps((H_hi, H_lo, m_marks), 4, S, square=False)

        def filled(items, fill, total, *stages_, apart=False):
            given = [0]

            def give(item):
                n = items.index(item) + 1
                while given[0] < total * n // len(items):
                    next(fill, None)
                    given[0] += 1

            def first(item):
                stages_[0](item)
                give(item)

            if apart:
                pipeline(items, stages_[0], give, *stages_[1:])
            else:
                pipeline(items, first, *stages_[1:])
            drain(fill)

        filled(items, mlstm_out_steps(), 12, nsa_score, nsa_turn, nsa_value, apart=True)

        stage("mix_out")
        fence()
        marks = []
        for k in range(4):
            b, i = dense.take(PE)
            for t in range(TT):
                ins = nc.tensor.transpose(bank[:, b, t * P:(t + 1) * P], a_rows[:, t, k * P:(k + 1) * P], ident[:, :])
            m = PE.did(ins)
            got = split_into(H_hi[:, 4 + k, 0:S], H_lo[:, 4 + k, 0:S], bank[:, b, :], m)
            dense.free(i, *got)
            marks.append(got)
        dense = slots([0, 1, 2, 3], *marks[-1], *marks[-2])
        add_residual((H_hi[:, 4:8, :], H_lo[:, 4:8, :], marks), 4, S)

        stage("ffn")
        fence()
        c = R + 3 * FOUR_ROWS + 4 * TT * MH * (MD + 1)
        p_rows, c = place("p_rows", [P, TT, PLE], F32, c)
        meta, c = place("meta_rows", [META, D], F32, c)
        masks, c = place("na_masks", [P, 3, 2 * P], F32, c)
        p_in = small(p_rows[:, :, :], A["p"].rearrange("(t q) d -> q t d", q=P))
        small(meta[:, :], A["meta"][:, :])
        for n, name in enumerate(("na_first", "na_inner", "na_last")):
            p_in = table(name, masks[:, n, :])
        mask_at = R_END - 3 * 2 * 2 * P - 2 * P
        mask_at -= mask_at % 64
        maskb, c2 = place("na_mask16", [P, 3, 2 * P], BF16, mask_at)
        idb, _ = place("ident16", [P, P], BF16, c2)
        after_masks = c
        Hs = rms_norm_split("ln2", S)
        PO.wait(p_in)
        PO.did(nc.gpsimd.tensor_copy(maskb[:, :, :], masks[:, :, :]))
        PO.did(nc.gpsimd.tensor_copy(idb[:, :], ident[:, :]))
        c = R
        NB = 3
        conv, acc_, th = [None] * NB, [None] * NB, [None] * NB
        for n in range(NB):
            conv[n], c = place(f"conv_in{n}", [P, S + 2], F32, c)
            acc_[n], c = place(f"conv_out{n}", [P, S], F32, c)
            th[n], c = place(f"conv_tanh{n}", [P, S], F32, c)
        gate, c = place("ple_gate", [P, 2, S], F32, c)
        pp, c2 = place("p_projected", [P, KT, S], F32, after_masks)
        gain_sq = [None, None]
        for n in range(2):
            gain_sq[n], c2 = place(f"gained_squares{n}", [P, S], F32, c2)
        assert c2 <= mask_at
        assert c <= R + 3 * FOUR_ROWS + 4 * TT * MH * (MD + 1)
        zero = [PO.did(nc.gpsimd.memset(conv[n][:, 0:2], 0.0)) for n in range(NB)]
        DV.wait(*zero)
        cv_s = Slots(list(range(NB)))
        for part in range(2):
            g_ready = []

            def ffn_in(jj):
                j = part * KT + jj
                hi, lo, u = weights()
                (bg, ig), (bv, iv) = dense.take(PE), dense.take(PE)
                if part == 0 and jj == 0:
                    mg = mvv = tiles_to_features(Hs, KT, (hi, lo), [columns(0), columns(P)], S, [bg, bv])
                else:
                    mg = to_features(Hs, KT, (hi, lo), columns(0), S, bg)
                    mvv = to_features(Hs, KT, (hi, lo), columns(P), S, bv)
                weights_done(u, mvv)
                n, ni = cv_s.take(AC)
                AC.wait(mg)
                e1 = AC.did(nc.scalar.activation(conv[n][:, 2:S + 2], bank[:, bg, :], ACT.Copy))
                e2 = AC.did(nc.scalar.activation(acc_[n][:, :], bank[:, bg, :], ACT.Identity, scale=param("conv_w", 32 + j),
                                                 bias=param("conv_b", j)))
                dense.free(ig, e2)
                DV.wait(e1, e2)
                e = DV.did(nc.vector.scalar_tensor_tensor(acc_[n][:, :], conv[n][:, 1:S + 1], param("conv_w", 16 + j), acc_[n][:, :],
                                                          ALU.mult, ALU.add))
                DV.wait(e)
                e = DV.did(nc.vector.scalar_tensor_tensor(acc_[n][:, :], conv[n][:, 0:S], param("conv_w", j), acc_[n][:, :],
                                                          ALU.mult, ALU.add))
                AC.wait(e)
                e = AC.did(nc.scalar.activation(th[n][:, :], acc_[n][:, :], ACT.Tanh, scale=0.5))
                live[jj] = (n, ni, bv, iv, mvv, e)

            def ffn_gate(jj):
                n, ni, bv, iv, mvv, e = live.pop(jj)
                DV.wait(e)
                e = DV.did(nc.vector.scalar_tensor_tensor(th[n][:, :], th[n][:, :], 1.0, acc_[n][:, :], ALU.add, ALU.mult))
                DV.wait(e, mvv)
                e = DV.did(nc.vector.scalar_tensor_tensor(th[n][:, :], th[n][:, :], 0.5, bank[:, bv, :], ALU.mult, ALU.mult))
                dense.free(iv, e)
                if jj == 0 and part:
                    AC.wait(g_read)
                    DV.wait(g_read)
                got = split_into(G_hi[:, jj, 0:S], G_lo[:, jj, 0:S], th[n][:, :], e)
                cv_s.free(ni, *got)
                g_ready.append(got)

            pipeline(list(range(KT)), ffn_in, ffn_gate)
            add_residual((G_hi, G_lo, g_ready), KT, S, square=part == 1)
            g_read = PE.last

        stage("ple")
        PE.wait(p_in)
        AC.wait(g_read)
        DV.wait(g_read)
        marks = []
        for k in range(2):
            b, i = dense.take(PE)
            for t in range(TT):
                ins = nc.tensor.transpose(bank[:, b, t * P:(t + 1) * P], p_rows[:, t, k * P:(k + 1) * P], ident[:, :])
            m = PE.did(ins)
            got = split_into(G_hi[:, k, 0:S], G_lo[:, k, 0:S], bank[:, b, :], m)
            dense.free(i, *got)
            marks.append(got)
        Gs = (G_hi, G_lo, marks)
        b, i = dense.take(PE)
        for k in range(KT):
            ins = nc.tensor.transpose(bank[:, b, k * META:(k + 1) * META], meta[:, k * P:(k + 1) * P], ident[0:META, 0:META])
        m = PE.did(ins)
        AC.wait(m)
        meta_done = AC.did(nc.scalar.activation(X[:, :, S:T2], bank[:, b, 0:KT * META].rearrange("p (k m) -> p k m", k=KT), ACT.Copy))
        dense.free(i, meta_done)
        proj = weights()

        def project_p(ks_):
            for k in ks_:
                b, i = dense.take(PE)
                m = to_features(Gs, 2, proj[:2], columns(k * P), S, b)
                if k == KT - 1:
                    weights_done(proj[2], m)
                e = evacuate(pp[:, k, :], bank[:, b, :], m)
                dense.free(i, e)
                pp_at[k] = e

        pp_at = {}
        Hs = rms_norm_split("ple", S, meanwhile=lambda: project_p(range(4)))
        gfree = [(), ()]
        gsq_free = [(), ()]
        by_column = lambda a: a.rearrange("p (c r) -> p r c", r=ROWS)
        by_row = lambda a: a.rearrange("p (r c) -> p r c", r=ROWS)
        acc_g = tmp
        late_sums = []

        def sum_both():
            while late_sums:
                k, m1, m2 = late_sums.pop()
                DV.wait(m1, m2, *sum_mark)
                DV.did(nc.vector.tensor_tensor(acc[:, 0:S], acc[:, 0:S], sq[k % 2][:, 0:S], ALU.add))
                sum_mark[:] = [DV.did(nc.vector.tensor_tensor(acc_g[:, 0:S], acc_g[:, 0:S], gain_sq[k % 2][:, :], ALU.add))]
                gsq_free[k % 2] = tuple(sum_mark)

        sum_mark = []
        for q in range(4):
            hi, lo, u = weights()
            gm = []
            got = [dense.take(PE), dense.take(PE)]
            m = tiles_to_features(Hs, KT, (hi, lo), [columns(0), columns(P)], S, [got[0][0], got[1][0]])
            weights_done(u, m)
            for j, (b, i) in enumerate(got):
                AC.wait(m, *gfree[j])
                e = AC.did(nc.scalar.activation(gate[:, j, :], bank[:, b, :], ACT.Tanh, scale=0.5))
                dense.free(i, e)
                gm.append(e)
            if q == 0:
                project_p(range(4, KT))
            for j in range(2):
                k = 2 * q + j
                DV.wait(gm[j], pp_at[k])
                e = DV.did(nc.vector.scalar_tensor_tensor(gate[:, j, :], gate[:, j, :], 1.0, pp[:, k, :], ALU.add, ALU.mult))
                DV.wait(e)
                e = DV.did(nc.vector.scalar_tensor_tensor(X[:, k, 0:S], gate[:, j, :], 0.5, X[:, k, 0:S], ALU.mult, ALU.add))
                gfree[j] = (e,)
                if k == 0:
                    AC.wait(e, *acc_free, *Hs[2][-1], *Hs[2][-2], *Hs[2][-3])
                    AC.did(nc.scalar.activation(by_column(acc[:, 0:S]), by_row(X[:, k, 0:S]), ACT.Square))
                    sum_mark[:] = [AC.did(nc.scalar.activation(by_column(acc_g[:, 0:S]), by_row(X[:, k, 0:S]), ACT.Square,
                                                               scale=param("fin1", k)))]
                    continue
                AC.wait(e, *sq_free[k % 2], *gsq_free[k % 2])
                m1 = AC.did(nc.scalar.activation(by_column(sq[k % 2][:, 0:S]), by_row(X[:, k, 0:S]), ACT.Square))
                m2 = AC.did(nc.scalar.activation(by_column(gain_sq[k % 2][:, :]), by_row(X[:, k, 0:S]), ACT.Square,
                                                 scale=param("fin1", k)))
                sum_both()
                late_sums.append((k, m1, m2))
        sum_both()
        AC.wait(*gsq_free[0], *gsq_free[1], meta_done)
        m = AC.did(nc.scalar.activation(gain_sq[0][:, 0:KT * META].rearrange("p (k m) -> p k m", k=KT), X[:, :, S:T2], ACT.Square))
        DV.wait(m)
        meta_sum = DV.did(nc.vector.reduce_sum(gain_sq[1][:, 0:META],
                                               gain_sq[0][:, 0:KT * META].rearrange("p (k m) -> p m k", k=KT), AX.X))

        def both_norms(Y):
            PE.wait(*sum_mark, meta_sum)
            for n, src in enumerate((acc, acc_g)):
                for t in range(TT):
                    nc.tensor.matmul(bank[:, 7, n * TT + t:n * TT + t + 1], src[:, t * P:(t + 1) * P], ones[:, 0:1],
                                     start=True, stop=True)
            m = PE.did(nc.tensor.matmul(bank[0:META, 7, 2 * TT:2 * TT + 1], gain_sq[1][:, 0:META], ones[:, 0:1],
                                        start=True, stop=True))
            DV.wait(m)
            v = DV.did(nc.vector.tensor_scalar(var[:, 2, 0:TT], bank[:, 7, 0:TT], 1.0 / D, EPS, ALU.mult, ALU.add))
            PO.wait(v)
            v = PO.did(nc.gpsimd.tensor_tensor(var[:, 2, 0:TT], var[:, 2, 0:TT], half[:, 0:TT], ALU.pow))
            DV.wait(v)
            v = DV.did(nc.vector.tensor_tensor(var[:, 0, 0:TT], bank[:, 7, TT:2 * TT], var[:, 2, 0:TT], ALU.mult))
            DV.wait(v)
            v = DV.did(nc.vector.scalar_tensor_tensor(var[:, 0, 0:TT], var[:, 0, 0:TT], 1.0 / D, var[:, 2, 0:TT], ALU.mult, ALU.mult))
            DV.wait(v)
            DV.did(nc.vector.tensor_scalar(var[:, 0, 0:TT], var[:, 0, 0:TT], EPS, None, ALU.add))
            v = DV.did(nc.vector.tensor_scalar(var[0:META, 0, TT:TT + 1], bank[0:META, 7, 2 * TT:2 * TT + 1], 1.0 / D, EPS,
                                               ALU.mult, ALU.add))
            d = DV.did(nc.vector.tensor_tensor(sq[1][:, 0:S].rearrange("p (t q) -> p t q", t=TT),
                                               ident[:, :].unsqueeze(1).broadcast_to([P, TT, P]),
                                               var[:, 2, 0:TT].unsqueeze(2).broadcast_to([P, TT, P]), ALU.mult))
            PE.wait(d)
            row1 = PE.did(nc.tensor.matmul(bank[:, 6, :], ones[:, :], sq[1][:, 0:S], start=True, stop=True))
            sq_free[0] = sq_free[1] = (row1,)
            acc_free[:] = [row1]
            row2 = root_row(T2, v)
            y_free = [(), ()]

            def first_norm(k):
                DV.wait(row1, *y_free[k % 2])
                e = DV.did(nc.vector.scalar_tensor_tensor(Y[k % 2].rearrange("p (c r) -> p r c", r=ROWS), by_row(X[:, k, 0:S]),
                                                          param("fin1", k), by_column(bank[:, 6, :]), ALU.mult, ALU.mult))
                AC.wait(e)
                e = AC.did(nc.scalar.activation(X[:, k, 0:S], Y[k % 2], ACT.Copy))
                y_free[k % 2] = (e,)
                return e

            return rms_norm_split("norm_a", T2, row2, before=first_norm)


        pair_of = [(x // 2, x % 2) for x in range(AH)]
        for layer in range(2):
            L = "ab"[layer]
            last = layer == 1
            n_out = S if last else T2
            stage(f"qkv_{L}")
            fence()
            oa_hi, g_c = place(f"oa_hi_{L}", [P, 4, T2], F32R, g_at)
            oa_lo, g_c = place(f"oa_lo_{L}", [P, 4, T2], F32R, g_c)
            ob_at = g_c
            ob_hi, g_c = place(f"ob_hi_{L}", [P, 4, T2], F32R, g_c)
            ob_lo, g_c = place(f"ob_lo_{L}", [P, 4, T2], F32R, g_c)
            vb, c = place(f"vb_{L}", [P, 5, NH * AD], F32, ob_at)
            cos, c = place(f"cos_{L}", [P, T2], F32, c)
            sin, c = place(f"sin_{L}", [P, T2], F32, c)
            v_own, c = place(f"v_own_{L}", [P, NH * AD], F32, c)
            assert c <= ob_at + 2 * 4 * 4 * T2
            qT, c = place(f"q_{L}", [P, 4, T2], F32, R)
            kT, c = place(f"k_{L}", [P, T2], F32, c)
            va, c = place(f"va_{L}", [P, 5, KW], F32, c)
            qb, c = place(f"qb_{L}", [P, 4, T2], F32, c)
            kb, c = place(f"kb_{L}", [P, 4, T2], F32, c)
            z, c = place(f"z_{L}", [P, 4, T2], F32, c)
            orow, c = place(f"o_rows_{L}", [P, TT, NH * AD], F32, c)
            omT, c = place(f"o_meta_features_{L}", [P, 4, META], F32, c)
            k_own, c = place(f"k_own_{L}", [P, 4, 2 * META], F32, c)
            q_own, c = place(f"q_own_{L}", [P, P], F32, c)
            sq_own, c = place(f"sq_own_{L}", [P, P], F32, c)
            pm, pmT = [None] * 2, [None] * 2
            for n in range(2):
                pm[n], c = place(f"meta_probs{n}_{L}", [P, AH, META], F32, c)
                pmT[n], c = place(f"meta_probsT{n}_{L}", [P, P], F32, c)
            stat, c = place(f"attn_stats_{L}", [P, 2, 6, AH], F32, c)
            rs, c = place(f"q_rms_{L}", [P, 2, TT + 1, AH], F32, c)
            ks, c = place(f"k_rms_{L}", [P, 2, TT + 1, 2], F32, c)
            tail = c
            rsin, c = place(f"rot_sin_{L}", [P, T2], F32, c)
            assert c <= mask_at, (c, mask_at)
            tiles2 = [(t * P, P) for t in range(TT)] + [(S, META)]

            table("cos", cos[:, :])
            rope_in = table("sin", sin[:, :])
            PO.did(nc.gpsimd.memset(ks[:, :, :, :], 1.0))
            PO.did(nc.gpsimd.memset(rs[:, :, :, :], 1.0))
            PO.did(nc.gpsimd.memset(k_own[:, :, :], 0.0))
            PO.did(nc.gpsimd.memset(q_own[:, :], 0.0))
            zeroed = PO.did(nc.gpsimd.memset(sq_own[:, :], 0.0))
            dense = Slots([0, 2])
            Hs = rms_norm_split(f"norm_{L}", T2) if layer else both_norms([z[:, 2, 0:S], z[:, 3, 0:S]])

            squares, gained = (sq[0], sq[1]), (tmp, acc)
            rope_free = [(PE.last, *Hs[2][-1], *Hs[2][-2], *Hs[2][-3])] * 2
            rope_n = [0]
            turned = slots([4], *Hs[2][-1])

            def rope(dst, b, i, m, ring, gain, sums):
                n = rope_n[0] % 2
                rope_n[0] += 1
                sq_, g_ = squares[n], gained[n]
                fv = feature_view(b, T2)
                AC.wait(m, *rope_free[n])
                e1 = AC.did(nc.scalar.activation(dest(sq_[:, :], T2), fv, ACT.Square))
                e2 = AC.did(nc.scalar.activation(dest(g_[:, :], T2), fv, ACT.Copy, scale=param(gain)))
                ring.free(i, e2)
                b4, i4 = turned.take(PE)
                PE.wait(e1)
                m_sum = sums(sq_)
                PE.wait(e2)
                for c_, (a_, z_) in enumerate(chunks(T2)):
                    ins = nc.tensor.matmul(bank[:, b4 + c_, 0:HALF], rot[:, :], g_[:, a_:z_], start=True, stop=True)
                m_rot = PE.did(ins)
                DV.wait(e2, rope_in)
                t1 = DV.did(nc.vector.tensor_tensor(dst, g_[:, :], cos[:, :], ALU.mult))
                DV.wait(m_rot, *rope_done)
                t2 = DV.did(nc.vector.tensor_tensor(dest(rsin[:, :], T2), bank[:, 4:6, 0:HALF], dest(sin[:, :], T2), ALU.mult))
                turned.free(i4, t2)
                DV.wait(t2, t1)
                t1 = DV.did(nc.vector.tensor_tensor(dst, dst, rsin[:, :], ALU.add))
                rope_done[:] = [t1]
                rope_free[n] = (m_sum, m_rot, t1)
                return e1, m_sum, t1

            shifted = [(0, 64)] + [(64 + P * t, P) for t in range(3)] + [(S - 64, 64 + META)]
            done.clear()

            def z_steps(marks_out):
                for a in range(2):
                    hi, lo, u = weights()
                    for jj in range(2):
                        k = 2 * a + jj
                        b, i = dense.take(PE)
                        m = to_features(Hs, KT, (hi, lo), columns(jj * P), n_out, b)
                        if jj:
                            weights_done(u, m)
                        zs = dest(z[:, k, 0:n_out], n_out)
                        AC.wait(m, *z_free[k])
                        e = AC.did(nc.scalar.activation(zs, feature_view(b, n_out), ACT.Tanh, scale=0.5))
                        DV.wait(e, m)
                        e = DV.did(nc.vector.scalar_tensor_tensor(zs, zs, 1.0, feature_view(b, n_out), ALU.add, ALU.mult))
                        dense.free(i, e)
                        marks_out.append(e)
                        yield

            def qkv_b_steps():
                for a in range(2):
                    yield from features_steps([qb[:, 2 * a + j, :] for j in range(2)], T2, Hs, scale=AD ** -0.5)
                for a in range(2):
                    yield from features_steps([kb[:, 2 * a + j, :] for j in range(2)], T2, Hs)
                for a in range(2):
                    yield from tokens_steps(lambda t: (vb[0:shifted[t][1], t, 256 * a:256 * a + 256], lambda x: x), shifted, Hs)

            rope_done = []

            def k_sums(sq_):
                for t, (t0, tn) in enumerate(tiles2):
                    ins = nc.tensor.matmul(bank[0:tn, 7, 2 * t:2 * t + 2], sq_[:, t0:t0 + tn], hsel, start=True, stop=True)
                return PE.did(ins)

            def q_sums(j):
                def f(sq_):
                    PE.wait(sums_read[-1])
                    for t in range(TT):
                        at = 16 + t * AH + 2 * j
                        ins = nc.tensor.matmul(bank[:, 7, at:at + 2], sq_[:, t * P:(t + 1) * P], hsel, start=True, stop=True)
                    return PE.did(ins)
                return f

            sums_read = []
            made = {}

            def product_of(n):
                if n in (0, 2, 4):
                    made["unit"] = weights()
                hi, lo, u = made["unit"]
                b, i = dense.take(PE)
                m = to_features(Hs, KT, (hi, lo), columns(n % 2 * P), T2, b)
                if n % 2:
                    weights_done(u, m)
                made[n] = (b, i, m, dense)

            def keys():
                b, i, m, ring = made.pop(0)
                _, m_sum, k_rot = rope(kT[:, :], b, i, m, ring, f"kg_{L}", k_sums)
                DV.wait(m_sum, zeroed)
                DV.did(nc.vector.tensor_scalar(ks[:, 0, 0:TT, :], bank[:, 7, 0:2 * TT].rearrange("p (t g) -> p t g", t=TT),
                                               1.0 / AD, EPS, ALU.mult, ALU.add))
                e = DV.did(nc.vector.tensor_scalar(ks[0:META, 0, TT, :], bank[0:META, 7, 2 * TT:2 * TT + 2], 1.0 / AD, EPS,
                                                   ALU.mult, ALU.add))
                sums_read.append(e)
                PO.wait(e)
                made["k"] = (k_rot, PO.did(nc.gpsimd.tensor_tensor(ks[:, 1, :, :], ks[:, 0, :, :],
                                                                   half[:, 0:2 * TT + 2].rearrange("p (t g) -> p t g", g=2), ALU.pow)))

            def values():
                b, i, m, ring = made.pop(1)
                e = evacuate(dest(z[:, 1, :], T2), feature_view(b, T2), m)
                ring.free(i, e)
                b4, i4 = turned.take(PE)
                PE.wait(e)
                for t in range(TT):
                    nc.tensor.transpose(bank[:, b4, t * P:(t + 1) * P], z[:, 1, t * P:(t + 1) * P], ident[:, :])
                m = PE.did(nc.tensor.transpose(bank[0:META, b4 + 1, 0:P], z[:, 1, S:T2], ident[:, :]))
                evacuate(va[:, 0:TT, :], bank[:, b4, :].rearrange("p (t c) -> p t c", t=TT), m)
                made["v"] = evacuate(va[0:META, TT, :], bank[0:META, b4 + 1, 0:KW], m)
                turned.free(i4, made["v"])

            def scaled_keys():
                k_rot, k_pow = made["k"]
                kw = z[:, :, 0:P]
                DV.wait(k_pow, made["v"])
                DV.did(nc.vector.tensor_copy(kw.rearrange("p t (g d) -> p t g d", g=2),
                                             ks[:, 1, 0:TT, :].unsqueeze(3).broadcast_to([P, TT, 2, AD])))
                e = DV.did(nc.vector.tensor_copy(z[:, 0, P:2 * P].rearrange("p (g d) -> p g d", g=2),
                                                 ks[:, 1, TT, :].unsqueeze(2).broadcast_to([P, 2, AD])))
                b4, i4 = turned.take(PE)
                PE.wait(e)
                for t in range(TT):
                    nc.tensor.transpose(bank[:, b4, t * P:(t + 1) * P], kw[:, t, :], ident[:, :])
                m = PE.did(nc.tensor.transpose(bank[:, b4 + 1, 0:META], z[0:META, 0, P:2 * P], ident[0:META, 0:META]))
                DV.wait(m, k_rot)
                DV.did(nc.vector.tensor_tensor(kT[:, 0:S], kT[:, 0:S], bank[:, b4, :], ALU.mult))
                made["k done"] = DV.did(nc.vector.tensor_tensor(kT[:, S:T2], kT[:, S:T2], bank[:, b4 + 1, 0:META], ALU.mult))
                turned.free(i4, made["k done"])

            q_rot = []

            def queries(j):
                b, i, m, ring = made.pop(2 + j)
                e1, m_sum, e = rope(qT[:, j, :], b, i, m, ring, f"qg_{L}", q_sums(j))
                q_rot.append(e)
                if not last:
                    DV.wait(e1, zeroed)
                    for g in range(2):
                        rows = slice(g * AD, (g + 1) * AD)
                        at = g * AD + j * META
                        e = DV.did(nc.vector.tensor_copy(sq_own[rows, at:at + META], squares[(rope_n[0] - 1) % 2][rows, S:T2]))
                    rope_free[(rope_n[0] - 1) % 2] += (e,)
                if j % 2:
                    cols = slice(2 * j - 2, 2 * j + 2)
                    DV.wait(m_sum)
                    e = DV.did(nc.vector.tensor_scalar(rs[:, 0, 0:TT, cols],
                                                       bank[:, 7, 16:16 + TT * AH].rearrange("p (t x) -> p t x", t=TT)[:, :, cols],
                                                       AD * EPS, None, ALU.add))
                    sums_read.append(e)
                    PO.wait(e)
                    PO.did(nc.gpsimd.tensor_tensor(rs[:, 1, 0:TT, cols], rs[:, 0, 0:TT, cols],
                                                   half[:, 0:4 * TT].rearrange("p (t x) -> p t x", t=TT), ALU.pow))

            def made_of(n):
                if n == 0:
                    keys()
                elif n == 1:
                    values()
                else:
                    queries(n - 2)
                    if n == 2:
                        scaled_keys()

            for n in range(6):
                product_of(n)
                if n:
                    made_of(n - 1)
            k_done, v_in = made["k done"], made["v"]
            z_free = [(k_done,)] * 4
            z_marks = []
            fill = all_of(z_steps(z_marks), qkv_b_steps())
            dense = slots([0], *dense.free_at[0])
            next(fill)
            made_of(5)
            next(fill)
            AC.wait(k_done, zeroed)
            for g in range(2):
                rows = slice(g * AD, (g + 1) * AD)
                k_own_in = AC.did(nc.scalar.activation(k_own[rows, 0, g * META:(g + 1) * META], kT[rows, S:T2], ACT.Copy))
            b, i = turned.take(PE)
            PE.wait(v_in)
            m = PE.did(nc.tensor.matmul(bank[:, b, 0:KW], spread[0:META, :], va[0:META, TT, :], start=True, stop=True))
            DV.wait(m)
            for g in range(2):
                v_own_in = DV.did(nc.vector.tensor_tensor(
                    v_own[:, g * 4 * AD:(g + 1) * 4 * AD].rearrange("p (h d) -> p h d", h=4),
                    bank[:, b, g * AD:(g + 1) * AD].unsqueeze(1).broadcast_to([P, 4, AD]),
                    own_pair[:, 4 * g:4 * g + 4].unsqueeze(2).broadcast_to([P, 4, AD]), ALU.mult))
            turned.free(i, v_own_in)
            if not last:
                AC.wait(*q_rot)
                for g in range(2):
                    rows = slice(g * AD, (g + 1) * AD)
                    AC.did(nc.scalar.activation(q_own[rows, g * AD:(g + 1) * AD].rearrange("p (j m) -> p j m", j=4),
                                                           qT[rows, :, S:T2], ACT.Copy))

            stage(f"gqa_{L}")
            fence()
            c = work_at
            pr_s, pt_s = [None] * 3, [None] * 3
            for n in range(2):
                pr_s[n], c = place(f"gqa_probs{n}_{L}", [P, S], F32, c)
                pt_s[n], c = place(f"gqa_probsT{n}_{L}", [P, TT, P], F32, c)
            assert c <= R
            pr_s[2], c = place(f"gqa_probs2_{L}", [P, S], F32, tail)
            pt_s[2], c = place(f"gqa_probsT2_{L}", [P, TT, P], F32, c)
            assert c <= mask_at, (c, mask_at)
            pr, pt, scores, turned, outb = Slots(pr_s), Slots(pt_s), Slots([2, 3]), Slots([4, 5]), Slots([6])
            live = {}
            tile_done = {-2: (), -1: ()}
            bank7_read = [()]

            def meta_scores(t, qn, q_of, k_of):
                at = t % 2 * P
                PE.wait(*tile_done[t - 2], *bank7_read[0])
                for j in range(4):
                    ins = nc.tensor.matmul(bank[0:qn, 7, at + 2 * META * j:at + 2 * META * (j + 1)], q_of(j), k_of(j),
                                           start=True, stop=True)
                m = PE.did(ins)
                DV.wait(m, *tile_done[t - 2])
                AC.wait(*tile_done[t - 2])
                sm = bank[0:qn, 7, at:at + P].rearrange("p (x m) -> p x m", x=AH)
                live["meta", t] = DV.did(nc.vector.reduce_max(stat[0:qn, t % 2, 4, :], sm, AX.X, negate=True))
                bank7_read[0] = (live["meta", t],)

            def meta_probs(t, qn, *ready, scale=None):
                at, st, pm_ = t % 2 * P, stat[0:qn, t % 2, :, :], pm[t % 2]
                sm = bank[0:qn, 7, at:at + P].rearrange("p (x m) -> p x m", x=AH)
                DV.wait(*ready)
                e = None
                if scale is not None:
                    e = DV.did(nc.vector.tensor_tensor(pm_[0:qn, :, :], sm, scale.unsqueeze(2).broadcast_to([qn, AH, META]), ALU.mult))
                    DV.wait(e)
                    sm = pm_[0:qn, :, :]
                e = DV.did(nc.vector.tensor_tensor(pm_[0:qn, :, :], sm, st[:, 1, :].unsqueeze(2).broadcast_to([qn, AH, META]), ALU.add))
                bank7_read[0] = (e,)
                AC.wait(e)
                e = AC.did(nc.scalar.activation(pm_[0:qn, :, :], pm_[0:qn, :, :], ACT.Exp))
                DV.wait(e)
                live["meta sum", t] = DV.did(nc.vector.reduce_sum(st[:, 3, :], pm_[0:qn, :, :], AX.X))
                live["meta exp", t] = e

            def meta_turn(t, qn):
                at = 2 * P + t % 2 * P
                PE.wait(live.pop(("meta exp", t)), *bank7_read[0])
                m = PE.did(nc.tensor.transpose(bank[:, 7, at:at + qn], pm[t % 2][0:qn, :, :].rearrange("p x m -> p (x m)"),
                                               ident[0:qn, 0:qn]))
                live["meta turned", t] = evacuate(pmT[t % 2][:, 0:qn], bank[:, 7, at:at + qn], m)
                bank7_read[0] = (live["meta turned", t],)

            def tile_out(t, qn, ob, oi, first, dst, natural, ready):
                st = stat[0:qn, t % 2, :, :]
                PE.wait(live.pop(("meta turned", t)))
                m = PE.did(nc.tensor.matmul(bank[0:qn, ob, 0:NH * AD], pmT[t % 2][:, 0:qn], v_own[:, :], start=first, stop=True,
                                            skip_group_check=True))
                DV.wait(live.pop(("meta sum", t)), *ready)
                if first:
                    src = st[:, 3, :]
                else:
                    src = st[:, 5, :]
                    e = DV.did(nc.vector.tensor_tensor(src, st[:, 2, :], st[:, 3, :], ALU.add))
                    DV.wait(e)
                e = DV.did(nc.vector.reciprocal(src, src))
                DV.wait(e, m)
                by_head = (src if natural else src.rearrange("p (j g) -> p g j", g=2))
                if natural:
                    e = DV.did(nc.vector.tensor_tensor(dst.rearrange("p (h d) -> p h d", h=AH),
                                                       bank[0:qn, ob, 0:NH * AD].rearrange("p (h d) -> p h d", h=AH),
                                                       by_head.unsqueeze(2).broadcast_to([qn, AH, AD]), ALU.mult))
                else:
                    for g in range(2):
                        half_ = slice(g * 4 * AD, (g + 1) * 4 * AD)
                        e = DV.did(nc.vector.tensor_tensor(dst[:, half_].rearrange("p (h d) -> p h d", h=4),
                                                           bank[0:qn, ob, half_].rearrange("p (h d) -> p h d", h=4),
                                                           by_head[:, g, :].unsqueeze(2).broadcast_to([qn, 4, AD]), ALU.mult))
                outb.free(oi, e)
                tile_done[t] = (e,)
                return e

            def gqa_meta(t):
                meta_scores(t, P, lambda j: qT[:, j, t * P:(t + 1) * P], lambda j: k_own[:, 0, :])

            def gqa_score(item):
                t, x = item
                j, g = pair_of[x]
                rows = slice(AD * g, AD * g + AD)
                st = stat[:, t % 2, :, :]
                if item == (0, 0):
                    gqa_meta(0)
                if x == 4 and t + 1 < TT:
                    gqa_meta(t + 1)
                b, i = scores.take(PE)
                m = PE.did(nc.tensor.matmul(bank[:, b, :], qT[rows, j, t * P:(t + 1) * P], kT[rows, 0:S], start=True, stop=True))
                DV.wait(m)
                e = DV.did(nc.vector.reduce_max(st[:, 0, x:x + 1], bank[:, b, :], AX.X, negate=True))
                DV.wait(e, live["meta", t])
                e = DV.did(nc.vector.scalar_tensor_tensor(st[:, 1, x:x + 1], st[:, 0, x:x + 1], st[:, 4, x:x + 1],
                                                          rs[:, 1, t, x:x + 1], ALU.min, ALU.mult))
                p_, pi = pr.take(AC)
                AC.wait(e, m)
                e2 = AC.did(nc.scalar.activation(p_[:, :], bank[:, b, :], ACT.Exp, bias=st[:, 1, x:x + 1],
                                                 scale=rs[:, 1, t, x:x + 1], accum_out=st[:, 2, x:x + 1]))
                scores.free(i, e2)
                live[item] = (p_, pi, e2)
                if x == AH - 1:
                    meta_probs(t, P, e, scale=rs[:, 1, t, :])

            def gqa_turn(item):
                t, x = item
                p_, pi, ready = live[item]
                b, i = turned.take(PE)
                PE.wait(ready)
                for k in range(TT):
                    ins = nc.tensor.transpose(bank[:, b, k * P:(k + 1) * P], p_[:, k * P:(k + 1) * P], ident[:, :])
                m = PE.did(ins)
                pr.free(pi, m)
                lane = DV if x % 2 else AC
                q_, qi = pt.take(lane)
                e = evacuate(q_[:, :, :].rearrange("p k q -> p (k q)"), bank[:, b, :], m, None, lane)
                turned.free(i, e)
                live[item] = (q_, qi, e, ready)
                if x == AH - 1:
                    meta_turn(t, P)

            def gqa_value(item):
                t, x = item
                j, g = pair_of[x]
                h = 4 * g + j
                q_, qi, e, ready = live.pop(item)
                if x == 0:
                    live["o"] = outb.take(PE)
                ob, oi = live["o"]
                PE.wait(e)
                for k in range(TT):
                    ins = nc.tensor.matmul(bank[:, ob, h * AD:(h + 1) * AD], q_[:, k, :], va[:, k, g * AD:(g + 1) * AD],
                                           start=x == 0 and k == 0, stop=False, skip_group_check=True)
                m = PE.did(ins)
                pt.free(qi, m)
                if x == AH - 1:
                    tile_out(t, P, ob, oi, False, orow[:, t, :], False, [ready])

            filled([(t, x) for t in range(TT) for x in range(AH)], fill, 20, gqa_score, gqa_turn, gqa_value)
            SP.wait(PE.last)
            bias, c = place(f"na_bias_{L}", [P, NH, 2 * P], F32, R)
            assert c <= R + 4 * 4 * T2
            bias_in = new_sem(f"na_bias_in_{L}")
            for cc in range(QB):
                off = (NAW - 1 - cc) * ROWS
                nc.sync.dma_start(bias[cc * ROWS:(cc + 1) * ROWS, :, :],
                                  A["na_rel"][layer, :, :, off:off + 2 * P].rearrange("h r x -> r h x")).then_inc(bias_in, 16)
            om_in = None
            PE.wait(*bank7_read[0])
            if not last:
                b, i = scores.take(PE)
                b5, i5 = turned.take(PE)
                PE.wait(*tile_done[TT - 1], *tile_done[TT - 2])
                nc.tensor.matmul(bank[:, b, :], q_own[:, :], kT[:, 0:S], start=True, stop=True)
                nc.tensor.matmul(bank[:, 7, 0:META], q_own[:, :], kT[:, S:T2], start=True, stop=True)
                m = PE.did(nc.tensor.matmul(bank[:, 7, META:META + 1], sq_own[:, :], ones[:, 0:1], start=True, stop=True))
                DV.wait(m, *tile_done[TT - 1], *tile_done[TT - 2])
                AC.wait(*tile_done[TT - 1], *tile_done[TT - 2])
                st = stat[:, 0, :, :]
                DV.did(nc.vector.reduce_max(st[:, 0, 0:1], bank[:, b, :], AX.X, negate=True))
                DV.did(nc.vector.reduce_max(st[:, 0, 1:2], bank[:, 7, 0:META], AX.X, negate=True))
                e = DV.did(nc.vector.tensor_scalar(st[:, 0, 2:3], bank[:, 7, META:META + 1], AD * EPS, None, ALU.add))
                PO.wait(e)
                e = PO.did(nc.gpsimd.tensor_tensor(st[:, 0, 3:4], st[:, 0, 2:3], half[:, 0:1], ALU.pow))
                DV.wait(e)
                e = DV.did(nc.vector.scalar_tensor_tensor(st[:, 1, 0:1], st[:, 0, 0:1], st[:, 0, 1:2], st[:, 0, 3:4], ALU.min, ALU.mult))
                p_, pi = pr.take(AC)
                AC.wait(e)
                AC.did(nc.scalar.activation(p_[:, :], bank[:, b, :], ACT.Exp, bias=st[:, 1, 0:1], scale=st[:, 0, 3:4],
                                            accum_out=st[:, 2, 0:1]))
                e2 = AC.did(nc.scalar.activation(pm[0][:, 0, :], bank[:, 7, 0:META], ACT.Exp, bias=st[:, 1, 0:1], scale=st[:, 0, 3:4],
                                                 accum_out=st[:, 2, 1:2]))
                scores.free(i, e2)
                DV.wait(e2)
                e = DV.did(nc.vector.tensor_tensor(st[:, 2, 2:3], st[:, 2, 0:1], st[:, 2, 1:2], ALU.add))
                DV.wait(e)
                e = DV.did(nc.vector.reciprocal(st[:, 2, 3:4], st[:, 2, 2:3]))
                PE.wait(e2)
                for k in range(TT):
                    nc.tensor.transpose(bank[:, b5, k * P:(k + 1) * P], p_[:, k * P:(k + 1) * P], ident[:, :])
                m = PE.did(nc.tensor.transpose(bank[0:META, 7, P:2 * P], pm[0][:, 0, :], ident[:, :]))
                pr.free(pi, m)
                q_, qi = pt.take(AC)
                e3 = evacuate(q_[:, :, :].rearrange("p k q -> p (k q)"), bank[:, b5, :], m)
                e3 = evacuate(pmT[0][0:META, :], bank[0:META, 7, P:2 * P], m)
                turned.free(i5, e3)
                ob, oi = outb.take(PE)
                PE.wait(e3)
                for k in range(TT):
                    nc.tensor.matmul(bank[:, ob, 0:KW], q_[:, k, :], va[:, k, :], start=k == 0, stop=False)
                m = PE.did(nc.tensor.matmul(bank[:, ob, 0:KW], pmT[0][0:META, :], va[0:META, TT, :], start=False, stop=True))
                pt.free(qi, m)
                q_, qi = pt.take(DV)
                DV.wait(m, e)
                for g in range(2):
                    rows = slice(g * AD, (g + 1) * AD)
                    for n in range(2):
                        e = DV.did(nc.vector.tensor_scalar(q_[rows, 0, n * AD:(n + 1) * AD], bank[rows, ob, g * AD:(g + 1) * AD],
                                                           st[rows, 2, 3:4], None, ALU.mult))
                outb.free(oi, e)
                b5, i5 = turned.take(PE)
                PE.wait(e)
                m = PE.did(nc.tensor.transpose(bank[:, b5, 0:P], q_[:, 0, :], ident[:, :]))
                pt.free(qi, m)
                for n in range(2):
                    rows = slice(n * AD, (n + 1) * AD)
                    om_in = evacuate(omT[rows, :, :].rearrange("p (g jj) m -> p g jj m", g=2),
                                     bank[rows, b5, 0:P].rearrange("p (g jj n m) -> p n g jj m", g=2, jj=2, n=2)[:, n, :, :, :], m)
                turned.free(i5, om_in)

            def gated_features(marks, hi_dst, lo_dst, meta_of, z_marks, after):
                for k in range(4):
                    b, i = turned.take(PE)
                    for t in range(TT):
                        ins = nc.tensor.transpose(bank[:, b, t * P:(t + 1) * P], orow[:, t, k * P:(k + 1) * P], ident[:, :])
                    m = PE.did(ins)
                    zk = z[:, k, 0:n_out]
                    DV.wait(m, z_marks[k])
                    e = DV.did(nc.vector.scalar_tensor_tensor(z[:, k, 0:S], z[:, k, 0:S], 0.5, bank[:, b, :], ALU.mult, ALU.mult))
                    turned.free(i, e)
                    if n_out > S:
                        src, mm = meta_of(k)
                        DV.wait(mm)
                        e = DV.did(nc.vector.scalar_tensor_tensor(z[:, k, S:T2], z[:, k, S:T2], 0.5, src, ALU.mult, ALU.mult))
                    marks.append(split_into(hi_dst[:, k, 0:n_out], lo_dst[:, k, 0:n_out], zk, e, lane=PO if k % 2 else DV))
                    after(k)
                return e

            PE.wait(*tile_done[TT - 1], *tile_done[TT - 2])
            oa_marks, za_marks, z_marks = [], z_marks, []
            z_free = oa_marks
            fill = z_steps(z_marks)
            gated_features(oa_marks, oa_hi, oa_lo, lambda k: (omT[:, k, :], om_in), za_marks,
                           lambda k: next(fill) if k % 2 else None)

            stage(f"na_{L}")
            fence()
            b_in = (bias_in, 16 * QB)
            ometa, c = place(f"o_meta_{L}", [META, NH * AD], F32, R + 4 * 4 * T2)
            c = work_at
            pr_s, pt_s = [None] * 4, [None] * 2
            for n in range(2):
                pr_s[n], c = place(f"na_probs{n}_{L}", [P, 2, 2 * P], F32, c)
                pt_s[n], c = place(f"na_probsT{n}_{L}", [P, 4, P], F32, c)
            assert c <= R
            c = tail
            for n in range(2, 4):
                pr_s[n], c = place(f"na_probs{n}_{L}", [P, 2, 2 * P], F32, c)
            sg_at = mask_at - 4 * 4 * T2 - 4 * 4 * T2 % 64
            assert c <= sg_at
            pr, pt, scores, turned, outb = Slots(pr_s), Slots(pt_s), Slots([2, 3]), Slots([4, 5]), Slots([6])
            for n in range(2):
                rows = slice(n * AD, (n + 1) * AD)
                k_own_in = AC.did(nc.scalar.activation(k_own[rows, :, n * META:(n + 1) * META], kb[rows, :, S:T2], ACT.Copy))
            b, i = outb.take(PE)
            m = PE.did(nc.tensor.matmul(bank[:, b, :], spread[64:64 + META, :], vb[64:64 + META, 4, :], start=True, stop=True))
            DV.wait(m)
            v_own_in = DV.did(nc.vector.tensor_tensor(v_own[:, :].rearrange("p (h d) -> p h d", h=NH),
                                                      bank[:, b, :].rearrange("p (h d) -> p h d", h=NH),
                                                      own_head.unsqueeze(2).broadcast_to([P, NH, AD]), ALU.mult))
            outb.free(i, v_own_in)
            PE.wait(k_own_in)
            tile_done = {-2: (), -1: ()}
            sg, _ = place(f"gates_{L}", [P, 4, T2], F32, sg_at)
            M_hi, c = place(f"mixed_hi_{L}", [P, KT, T2], F32R, R)
            M_lo, c = place(f"mixed_lo_{L}", [P, KT, T2], F32R, c)
            assert c <= sg_at
            m_marks, ob_marks = [], []

            def mixed_steps():
                sfree = [()] * 4
                first_part = [None, None]
                for q in range(4):
                    for which, act in ((0, (oa_hi, oa_lo, oa_marks)), (1, (ob_hi, ob_lo, ob_marks))):
                        hi, lo, u = weights()
                        gm = []
                        for j in range(2):
                            b, i = dense.take(PE)
                            m = to_features(Hs, KT, (hi, lo), columns(j * P), n_out, b)
                            if j:
                                weights_done(u, m)
                            sl = 2 * which + j
                            AC.wait(m, *sfree[sl])
                            e = AC.did(nc.scalar.activation(dest(sg[:, sl, 0:n_out], n_out), feature_view(b, n_out), ACT.Tanh, scale=0.5))
                            dense.free(i, e)
                            gm.append(e)
                            yield
                        hi, lo, u = weights()
                        for j in range(2):
                            k = 2 * q + j
                            sl = 2 * which + j
                            b, i = dense.take(PE)
                            m = to_features(act, 4, (hi, lo), columns(j * P), n_out, b)
                            if j:
                                weights_done(u, m)
                            gs = dest(sg[:, sl, 0:n_out], n_out)
                            DV.wait(gm[j], m)
                            e = DV.did(nc.vector.scalar_tensor_tensor(gs, gs, 1.0, feature_view(b, n_out), ALU.add, ALU.mult))
                            dense.free(i, e)
                            if which == 0:
                                first_part[j] = e
                                yield
                                continue
                            DV.wait(e, first_part[j])
                            s0 = sg[:, j, 0:n_out]
                            e = DV.did(nc.vector.tensor_tensor(s0, s0, sg[:, sl, 0:n_out], ALU.add))
                            sfree[sl] = (e,)
                            AC.wait(e)
                            a_ = AC.did(nc.scalar.activation(M_hi[:, k, 0:n_out], s0, ACT.Copy, scale=0.5))
                            DV.wait(a_)
                            z_ = DV.did(nc.vector.scalar_tensor_tensor(M_lo[:, k, 0:n_out], s0, 0.5, M_hi[:, k, 0:n_out].bitcast(F32),
                                                                       ALU.mult, ALU.subtract))
                            sfree[j] = (a_, z_)
                            m_marks.append((a_, z_))
                            yield

            mix = mixed_steps()
            heads2 = [(0, 2), (1, 3), (4, 6), (5, 7)]
            spans = [(0, 192, 64, 0), (64, 256, 0, 1), (192, 256, 0, 1), (320, 192, 0, 2)]
            parts = [[(0, 64, 0), (64, P, 1)], [(0, P, 1), (P, P, 2)], [(0, P, 2), (P, P, 3)], [(0, P, 3), (P, 64, 4)]]

            def na_meta(t):
                meta_scores(t, P, lambda j: qb[:, j, t * P:(t + 1) * P], lambda j: k_own[:, j, :])

            def na_score(item):
                t, y = item
                st = stat[:, t % 2, :, :]
                if item == (0, 0):
                    na_meta(0)
                if y == 3 and t + 1 < TT:
                    na_meta(t + 1)
                k0, kn, m0, which = spans[t]
                b, i = scores.take(PE)
                view = bank[:, b, 0:2 * kn].rearrange("p (n k) -> p n k", n=2)
                nc.tensor.matmul(view, idb[:, :], maskb[:, which, m0:m0 + kn].unsqueeze(1).broadcast_to([P, 2, kn]), start=True,
                                 stop=False, skip_group_check=True)
                for n, h in enumerate(heads2[y]):
                    rows = slice(AD * (h % 2), AD * (h % 2) + AD)
                    ins = nc.tensor.matmul(view[:, n, :], qb[rows, h // 2, t * P:(t + 1) * P], kb[rows, h // 2, k0:k0 + kn],
                                           start=False, stop=True, skip_group_check=True)
                m = PE.did(ins)
                s_, si = pr.take(DV)
                DV.wait(m, b_in)
                for n, h in enumerate(heads2[y]):
                    e = DV.did(nc.vector.tensor_tensor_reduce(s_[:, n, 0:kn], view[:, n, :], bias[:, h, m0:m0 + kn], -1.0, 3e38,
                                                              ALU.add, ALU.min, st[:, 0, h:h + 1]))
                scores.free(i, e)
                two = slice(heads2[y][0], heads2[y][0] + 3, 2)
                DV.wait(e, live["meta", t])
                e1 = DV.did(nc.vector.tensor_tensor(st[:, 1, two], st[:, 0, two], st[:, 4, two], ALU.min))
                AC.wait(e1)
                for n, h in enumerate(heads2[y]):
                    e = AC.did(nc.scalar.activation(s_[:, n, 0:kn], s_[:, n, 0:kn], ACT.Exp, bias=st[:, 1, h:h + 1], scale=-1.0,
                                                    accum_out=st[:, 2, h:h + 1]))
                live[item] = (s_, si, e)
                if y == 3:
                    meta_probs(t, P, e1)

            def na_turn(item):
                t, y = item
                p_, pi, ready = live[item]
                b, i = turned.take(PE)
                PE.wait(ready)
                for r, (p0, pn, _) in enumerate(parts[t]):
                    for n in range(2):
                        at = (2 * r + n) * P
                        ins = nc.tensor.transpose(bank[0:pn, b, at:at + P], p_[:, n, p0:p0 + pn], ident[:, :])
                m = PE.did(ins)
                pr.free(pi, m)
                q_, qi = pt.take(AC, DV)
                es = []
                if parts[t][0][1] == parts[t][1][1]:
                    lane = DV if y % 2 else AC
                    es.append(evacuate(q_[:, :, :].rearrange("p k q -> p (k q)"), bank[:, b, :], m, None, lane))
                else:
                    for r, (p0, pn, _) in enumerate(parts[t]):
                        es.append(evacuate(q_[0:pn, 2 * r:2 * r + 2, :].rearrange("p k q -> p (k q)"),
                                           bank[0:pn, b, 2 * r * P:2 * (r + 1) * P], m))
                turned.free(i, *es)
                live[item] = (q_, qi, es, ready)
                if y == 3:
                    meta_turn(t, P)

            def na_value(item):
                t, y = item
                q_, qi, es, ready = live.pop(item)
                if y == 0:
                    live["o"] = outb.take(PE)
                ob, oi = live["o"]
                PE.wait(*es)
                for n, h in enumerate(heads2[y]):
                    for r, (_, pn, vt) in enumerate(parts[t]):
                        ins = nc.tensor.matmul(bank[:, ob, h * AD:(h + 1) * AD], q_[0:pn, 2 * r + n, :],
                                               vb[0:pn, vt, h * AD:(h + 1) * AD], start=y == 0 and n == 0 and r == 0, stop=False,
                                               skip_group_check=True)
                m = PE.did(ins)
                pt.free(qi, m)
                if y == 3:
                    tile_out(t, P, ob, oi, False, orow[:, t, :], True, [ready])

            filled([(t, y) for t in range(TT) for y in range(4)], all_of(fill, first_steps(mix, 4)), 6, na_score, na_turn, na_value)
            om_in = None
            if not last:
                meta_scores(TT, META, lambda j: qb[:, j, S:T2], lambda j: k_own[:, j, :])
                DV.wait(live["meta", TT])
                e = DV.did(nc.vector.tensor_copy(stat[0:META, 0, 1, :], stat[0:META, 0, 4, :]))
                meta_probs(TT, META, e)
                meta_turn(TT, META)
                ob, oi = outb.take(PE)
                e = tile_out(TT, META, ob, oi, True, ometa[:, :], True, [])
                PE.wait(e)
                for k in range(4):
                    ins = nc.tensor.transpose(bank[:, 7, k * META:(k + 1) * META], ometa[:, k * P:(k + 1) * P],
                                              ident[0:META, 0:META])
                om_in = PE.did(ins)
            PE.wait(*tile_done[TT - 1], *tile_done[TT - 2])
            AC.wait(PE.last)
            DV.wait(PE.last)
            PO.wait(PE.last)
            banks_read = gated_features(ob_marks, ob_hi, ob_lo, lambda k: (bank[:, 7, k * META:(k + 1) * META], om_in), z_marks,
                           lambda k: next(mix) if k < 2 else None)

            stage(f"mixed_{L}")
            fence((AC, DV, PO, SP))
            dense = slots([0, 2, 4, 6], *dense.free_at[0], banks_read)
            drain(mix)
            add_residual((M_hi, M_lo, m_marks), KT, n_out)

        stage("out")
        fence()
        Y, c = place("gained", [P, KT, S], F32, R)
        rows_out, c = place("rows_out", [P, TT, D], F32, c)
        assert c <= mask_at
        gained_at = []
        for k in range(KT):
            gained_at.append(AC.did(nc.scalar.activation(Y[:, k, :].rearrange("p (r c) -> p c r", r=ROWS),
                                                         X[:, k, 0:S].rearrange("p (c r) -> p c r", r=ROWS), ACT.Copy,
                                                         scale=param("fin2", k))))
        sum_squares()
        PE.wait(state["acc"])
        for r in range(ROWS):
            part = r % 2 * GW
            ins = nc.tensor.matmul(bank[part:part + GW, 7, r // 2:r // 2 + 1], acc[:, r:S:ROWS], ones[:, 0:1],
                                   start=True, stop=True)
        m = PE.did(ins)
        DV.wait(m)
        m = DV.did(nc.vector.tensor_scalar(var[:, 0, 0:TT], bank[:, 7, 0:TT], 1.0 / D, EPS, ALU.mult, ALU.add))
        PO.wait(m)
        m_root = PO.did(nc.gpsimd.tensor_tensor(var[:, 1, 0:TT], var[:, 0, 0:TT], half[:, 0:TT], ALU.pow))
        AC.wait(m_root)
        DV.wait(m_root)
        out_sem = new_sem("out_written")
        turn = Slots([0, 1, 2, 3, 4, 5, 6])
        for t in range(TT):
            for f in range(2):
                b, i = turn.take(PE)
                for k in range(4):
                    PE.wait(gained_at[4 * f + k])
                    ins = nc.tensor.transpose(bank[:, b, k * P:(k + 1) * P], Y[:, 4 * f + k, t * P:(t + 1) * P], ident[:, :])
                m = PE.did(ins)
                e = evacuate(rows_out[:, t, 512 * f:512 * f + 512], bank[:, b, :], m, var[:, 1, t:t + 1], DV if f else AC)
                turn.free(i, e)
                SP.wait(e)
                nc.sync.dma_start(A["out"][t * P:(t + 1) * P, 512 * f:512 * f + 512],
                                  rows_out[:, t, 512 * f:512 * f + 512]).then_inc(out_sem, 16)
        nc.sync.wait_ge(out_sem, 2 * TT * 16)


def bass_windows(src):
    part = list(src.ap)[0]
    return bass.AP(tensor=src.tensor, offset=src.offset, ap=[part, [1, CB], [CS, NC]])


def kernel(**inputs):
    import numpy as _np
    import concourse.bacc as _bacc
    from concourse import mybir as _mybir
    from concourse.bass_utils import run_bass_kernel_spmd as _run

    f = {k: _np.asarray(v) for k, v in inputs.items()}

    def by_feature(v):
        return _np.reshape(v, (-1, 128)).T

    def twice(v):
        return _np.concatenate([v, v], axis=0)

    gate_b = _np.zeros((128, 2), _np.float32)
    gate_b[0:4, 0] = f["mlstm_gate_bias"][0, 0:4]
    gate_b[0:4, 1] = f["mlstm_gate_bias"][0, 4:8]
    cols = {
        "ln1": by_feature(f["ln1_g"]), "ln2": by_feature(f["ln2_g"]), "ple": by_feature(f["ple_norm_g"]),
        "fin1": by_feature(f["final_g"]), "conv_w": by_feature(f["conv_w"]), "conv_b": by_feature(f["conv_b"]),
        "mnorm": by_feature(f["mlstm_norm_g"]), "pe_k": twice(f["cmp_pos_k"][0].T), "pe_v": twice(f["cmp_pos_v"][0].T),
        "gate_b": gate_b, "norm_a": by_feature(f["norm_g_2"][0]), "norm_b": by_feature(f["norm_g_2"][1]),
        "fin2": by_feature(f["final_norm_g_2"]),
        "qg_a": twice(f["q_norm_g_2"][0][:, None]), "qg_b": twice(f["q_norm_g_2"][1][:, None]),
        "kg_a": twice(f["k_norm_g_2"][0][:, None]), "kg_b": twice(f["k_norm_g_2"][1][:, None]),
    }
    params = _np.ascontiguousarray(_np.concatenate([cols[n] for n, _ in PARAMS], axis=1))
    rpb = f["na_rpb_2"]
    rel = _np.zeros((2, 8, 8, DCP, 8), _np.float32)
    for r in range(8):
        rel[:, :, r, 8:8 + 31, :] = rpb[:, :, 7 - r:15 - r, :].transpose(0, 1, 3, 2)
    tables = constants()
    const_at, _ = offsets([(k, v.shape[1]) for k, v in tables.items()])
    consts = _np.ascontiguousarray(_np.concatenate(list(tables.values()), axis=1))
    arrays = {
        "x": f["x"][0], "p": f["p"][0, 0], "params": params, "consts": consts,
        "na_rel": rel.reshape(2, 8, 8, DCP * 8), "meta": f["meta_tokens_2"],
        "w_in": f["w_in"][0], "cmp_k_w1": f["cmp_k_w1"][0], "cmp_k_w2": f["cmp_k_w2"][0],
        "cmp_v_w1": f["cmp_v_w1"][0], "cmp_v_w2": f["cmp_v_w2"][0], "w_out": f["w_out"][0], "w_up": f["w_up"][0],
        "w_down": f["w_down"][0], "w_ple_gate": f["w_ple_gate"][0], "w_ple_proj": f["w_ple_proj"][0],
        "w_in_2": f["w_in_2"], "w_o_attn_2": f["w_o_attn_2"], "w_o_na_2": f["w_o_na_2"], "w_out_2": f["w_out_2"],
    }
    arrays = {k: _np.ascontiguousarray(v) for k, v in arrays.items()}
    nc = _bacc.Bacc("TRN2", target_bir_lowering=False, num_devices=1)
    A = {k: nc.dram_tensor(k, v.shape, _mybir.dt.float32, kind="ExternalInput").ap() for k, v in arrays.items()}
    A["const_at"] = const_at
    A["out"] = nc.dram_tensor("out", (S, D), _mybir.dt.float32, kind="ExternalOutput").ap()
    program(nc, A)
    r = _run(nc, [arrays], core_ids=[0])
    return r.results[0]["out"].reshape(1, S, D)
```
